# Optimizing a Trainium2 kernel written in Bass

```python
import jax
import jax.numpy as jnp
from jax import lax
import numpy as np
import jax, jax.numpy as jnp

D_MODEL = 1024
BATCH = 1
SEQ = 256
DEPTH = 2

GRID_W = 64
CTX_LEN = 256
EPS = 1e-6

NA_HEAD_DIM = 64
NA_HEADS = D_MODEL // (2 * NA_HEAD_DIM)
NA_WIN_ROWS = 8
NA_WIN_COLS = 16
NA_W = NA_HEADS * NA_HEAD_DIM

GDN_HEAD_DIM = 128
GDN_HEADS = D_MODEL // (2 * GDN_HEAD_DIM)
GDN_W = GDN_HEADS * GDN_HEAD_DIM
GDN_CONV = 5
GDN_CHUNK = 64

EVEN_IN = 3 * NA_W + 4 * GDN_W + 4 * GDN_HEADS
EVEN_MIX = NA_W + GDN_W

MLA_V = 128
MLA_HEADS = D_MODEL // MLA_V
MLA_NOPE = 128
MLA_ROPE = 64
MLA_Q_RANK = 384
MLA_KV_RANK = 256
MLA_IN = MLA_Q_RANK + MLA_KV_RANK + MLA_ROPE
MLA_QBLOCK = 128
ROPE_THETA = 10000.0

PEER_KEYS = 128
PEER_EXPERTS = PEER_KEYS * PEER_KEYS
PEER_HEADS = 8
PEER_TOPK = 16
PEER_DKEY = 256
PEER_BLOCK = 128

N_EVEN = (DEPTH + 1) // 2
N_ODD = DEPTH // 2


def rmsnorm(x, g):
    x32 = x.astype(jnp.float32)
    y = x32 * lax.rsqrt(jnp.mean(x32 * x32, axis=-1, keepdims=True) + EPS)
    return (y * g.astype(jnp.float32)).astype(x.dtype)

def l2norm(x):
    x32 = x.astype(jnp.float32)
    return x32 * lax.rsqrt(jnp.sum(x32 * x32, axis=-1, keepdims=True) + EPS)

def modulate(h, shift, scale):
    return h * (1.0 + scale[:, None, :]) + shift[:, None, :]

def split_heads(t, n_heads):
    b, l, w = t.shape
    return t.reshape(b, l, n_heads, w // n_heads).transpose(0, 2, 1, 3)

def merge_heads(t):
    b, h, l, d = t.shape
    return t.transpose(0, 2, 1, 3).reshape(b, l, h * d)

def axial_rope_tables(n_tokens, dim):
    half = dim // 2
    inv_freq = ROPE_THETA ** (-jnp.arange(0, half, 2, dtype=jnp.float32) / half)
    t = jnp.arange(n_tokens, dtype=jnp.int32)
    row = (t // GRID_W).astype(jnp.float32)
    col = (t % GRID_W).astype(jnp.float32)
    ang_r = row[:, None] * inv_freq[None, :]
    ang_c = col[:, None] * inv_freq[None, :]
    ang = jnp.concatenate([ang_r, ang_r, ang_c, ang_c], axis=-1)
    return jnp.cos(ang), jnp.sin(ang)

def apply_axial_rope(x, cos, sin):
    a, b, cq, d = jnp.split(x, 4, axis=-1)
    rot = jnp.concatenate([-b, a, -d, cq], axis=-1)
    return x * cos.astype(x.dtype) + rot * sin.astype(x.dtype)

def softmax_attend(q, k, v, scale):
    s = jnp.einsum('bhqd,bhkd->bhqk', q, k).astype(jnp.float32) * scale
    p = jax.nn.softmax(s, axis=-1).astype(v.dtype)
    return jnp.einsum('bhqk,bhkd->bhqd', p, v)

def blocked_attention(q, k, v, scale):
    b, h, l, dq = q.shape
    qb = jnp.moveaxis(q.reshape(b, h, l // MLA_QBLOCK, MLA_QBLOCK, dq), 2, 0)
    o = lax.map(lambda qi: softmax_attend(qi, k, v, scale), qb)
    return jnp.moveaxis(o, 0, 2).reshape(b, h, l, v.shape[-1])

def neighbourhood_attention(q, k, v, k_ctx, v_ctx, rpb):
    b, h, l, dh = q.shape
    rows = l // GRID_W
    wr = min(NA_WIN_ROWS, rows)
    wc = NA_WIN_COLS
    n_ctx = k_ctx.shape[2]
    scale = dh ** -0.5
    k_grid = k.reshape(b, h, rows, GRID_W, dh)
    v_grid = v.reshape(b, h, rows, GRID_W, dh)
    q_rows = jnp.moveaxis(q.reshape(b, h, rows, GRID_W, dh), 2, 0)
    q_col = jnp.arange(GRID_W)
    c_start = jnp.clip(q_col - wc // 2, 0, GRID_W - wc)
    k_col = jnp.tile(jnp.arange(GRID_W), wr)
    k_row_off = jnp.repeat(jnp.arange(wr), GRID_W)
    col_mask = (k_col[None, :] >= c_start[:, None]) & (k_col[None, :] < c_start[:, None] + wc)
    dc_idx = jnp.clip(k_col[None, :] - q_col[:, None], 1 - wc, wc - 1) + (NA_WIN_COLS - 1)

    def one_row(args):
        q_r, r = args
        r_start = jnp.clip(r - wr // 2, 0, rows - wr)
        k_r = lax.dynamic_slice_in_dim(k_grid, r_start, wr, axis=2).reshape(b, h, wr * GRID_W, dh)
        v_r = lax.dynamic_slice_in_dim(v_grid, r_start, wr, axis=2).reshape(b, h, wr * GRID_W, dh)
        dr_idx = r_start + k_row_off - r + (NA_WIN_ROWS - 1)
        bias = rpb[:, dr_idx[None, :], dc_idx].astype(jnp.float32)
        s_lat = jnp.einsum('bhqd,bhkd->bhqk', q_r, k_r).astype(jnp.float32) * scale + bias
        s_lat = jnp.where(col_mask, s_lat, -jnp.inf)
        s_ctx = jnp.einsum('bhqd,bhkd->bhqk', q_r, k_ctx).astype(jnp.float32) * scale
        p = jax.nn.softmax(jnp.concatenate([s_ctx, s_lat], axis=-1), axis=-1).astype(v.dtype)
        return (jnp.einsum('bhqk,bhkd->bhqd', p[..., :n_ctx], v_ctx)
                + jnp.einsum('bhqk,bhkd->bhqd', p[..., n_ctx:], v_r))

    out = lax.map(one_row, (q_rows, jnp.arange(rows)))
    return jnp.moveaxis(out, 0, 2).reshape(b, h, l, dh)

def short_conv(x, w):
    ch = x.shape[-1]
    return lax.conv_general_dilated(
        x, w.astype(x.dtype)[:, None, :], window_strides=(1,),
        padding=[(GDN_CONV // 2, GDN_CONV // 2)],
        dimension_numbers=('NWC', 'WIO', 'NWC'), feature_group_count=ch)

def gdn_chunk_scan(q, k, v, g, beta, s0, want_out):
    b, h, l, dk = q.shape
    dv = v.shape[-1]
    n = l // GDN_CHUNK
    f32 = jnp.float32
    q = q.astype(f32).reshape(b, h, n, GDN_CHUNK, dk)
    k = k.astype(f32).reshape(b, h, n, GDN_CHUNK, dk)
    v = v.astype(f32).reshape(b, h, n, GDN_CHUNK, dv)
    g = g.astype(f32).reshape(b, h, n, GDN_CHUNK)
    beta = beta.astype(f32).reshape(b, h, n, GDN_CHUNK)
    gc = jnp.cumsum(g, axis=-1)
    idx = jnp.arange(GDN_CHUNK)
    incl = idx[:, None] >= idx[None, :]
    strict = idx[:, None] > idx[None, :]
    dec = jnp.exp(jnp.where(incl, gc[..., :, None] - gc[..., None, :], -jnp.inf))
    a_mat = jnp.where(strict, beta[..., :, None] * jnp.einsum('bhncd,bhnkd->bhnck', k, k) * dec, 0.0)
    w_v = lax.linalg.triangular_solve(a_mat, beta[..., None] * v, left_side=True, lower=True,
                                      unit_diagonal=True)
    w_k = lax.linalg.triangular_solve(a_mat, (beta * jnp.exp(gc))[..., None] * k, left_side=True,
                                      lower=True, unit_diagonal=True)
    k_end = k * jnp.exp(gc[..., -1:] - gc)[..., None]
    b_end = jnp.exp(gc[..., -1])
    mv = lambda t: jnp.moveaxis(t, 2, 0)
    if want_out:
        p_in = jnp.einsum('bhncd,bhnkd->bhnck', q, k) * dec
        q_dec = q * jnp.exp(gc)[..., None]

        def step(s, xs):
            wv, wk, ke, be, qd, pp = xs
            u = wv - jnp.einsum('bhcd,bhde->bhce', wk, s)
            o = jnp.einsum('bhcd,bhde->bhce', qd, s) + jnp.einsum('bhck,bhke->bhce', pp, u)
            s = be[..., None, None] * s + jnp.einsum('bhcd,bhce->bhde', ke, u)
            return s, o

        s_fin, o = lax.scan(step, s0, (mv(w_v), mv(w_k), mv(k_end), mv(b_end), mv(q_dec), mv(p_in)))
        return s_fin, jnp.moveaxis(o, 0, 2).reshape(b, h, l, dv)

    def step_state(s, xs):
        wv, wk, ke, be = xs
        u = wv - jnp.einsum('bhcd,bhde->bhce', wk, s)
        return be[..., None, None] * s + jnp.einsum('bhcd,bhce->bhde', ke, u), None

    s_fin, _ = lax.scan(step_state, s0, (mv(w_v), mv(w_k), mv(k_end), mv(b_end)))
    return s_fin, None

def gdn_inputs(p, conv_w, a_log, dt_bias):
    b, l, _ = p.shape
    qkv = jax.nn.silu(short_conv(p[..., :3 * GDN_W], conv_w))
    q = l2norm(split_heads(qkv[..., :GDN_W], GDN_HEADS)) * (GDN_HEAD_DIM ** -0.5)
    k = l2norm(split_heads(qkv[..., GDN_W:2 * GDN_W], GDN_HEADS))
    v = split_heads(qkv[..., 2 * GDN_W:], GDN_HEADS)
    z = p[..., 3 * GDN_W:4 * GDN_W]
    gr = p[..., 4 * GDN_W:].astype(jnp.float32).reshape(b, l, 2, 2, GDN_HEADS).transpose(2, 3, 0, 4, 1)
    g = -jnp.exp(a_log.astype(jnp.float32))[:, None, :, None] * jax.nn.softplus(
        gr[:, 0] + dt_bias.astype(jnp.float32)[:, None, :, None])
    beta = jax.nn.sigmoid(gr[:, 1])
    return q, k, v, z, g, beta

def gdn_output(o, z, norm_g):
    b, h, l, dv = o.shape
    o = rmsnorm(o.transpose(0, 2, 1, 3), norm_g)
    gate = jax.nn.silu(z.astype(jnp.float32)).reshape(b, l, h, dv)
    return (o * gate).reshape(b, l, h * dv).astype(z.dtype)

def gated_deltanet(p, pc, conv_w, a_log, dt_bias, norm_g, want_ctx):
    q, k, v, z, g, beta = gdn_inputs(p, conv_w, a_log, dt_bias)
    qc, kc, vc, zc, gcx, betac = gdn_inputs(pc, conv_w, a_log, dt_bias)
    flip = lambda t: jnp.flip(t, axis=2)
    zero = jnp.zeros((q.shape[0], GDN_HEADS, GDN_HEAD_DIM, GDN_HEAD_DIM), jnp.float32)
    s_f, oc_f = gdn_chunk_scan(qc, kc, vc, gcx[0], betac[0], zero, want_ctx)
    s_b, oc_b = gdn_chunk_scan(flip(qc), flip(kc), flip(vc), flip(gcx[1]), flip(betac[1]), zero, want_ctx)
    _, o_f = gdn_chunk_scan(q, k, v, g[0], beta[0], s_f, True)
    _, o_b = gdn_chunk_scan(flip(q), flip(k), flip(v), flip(g[1]), flip(beta[1]), s_b, True)
    y = gdn_output(o_f + flip(o_b), z, norm_g)
    if not want_ctx:
        return y, None
    return y, gdn_output(oc_f + flip(oc_b), zc, norm_g)

def even_mixer(h, hc, w_in, conv_w, a_log, dt_bias, gdn_g, rpb, w_out, want_ctx):
    p = h @ w_in
    pc = hc @ w_in
    q = split_heads(p[..., :NA_W], NA_HEADS)
    k = split_heads(p[..., NA_W:2 * NA_W], NA_HEADS)
    v = split_heads(p[..., 2 * NA_W:3 * NA_W], NA_HEADS)
    kc = split_heads(pc[..., NA_W:2 * NA_W], NA_HEADS)
    vc = split_heads(pc[..., 2 * NA_W:3 * NA_W], NA_HEADS)
    y_a = merge_heads(neighbourhood_attention(q, k, v, kc, vc, rpb))
    y_b, yc_b = gated_deltanet(p[..., 3 * NA_W:], pc[..., 3 * NA_W:], conv_w, a_log, dt_bias, gdn_g, want_ctx)
    y = jnp.concatenate([y_a, y_b], axis=-1) @ w_out
    if not want_ctx:
        return y, None
    qc = split_heads(pc[..., :NA_W], NA_HEADS)
    yc_a = merge_heads(softmax_attend(qc, kc, vc, NA_HEAD_DIM ** -0.5))
    return y, jnp.concatenate([yc_a, yc_b], axis=-1) @ w_out

def mla_q(p, q_g, w_uq, rope):
    cq = rmsnorm(p[..., :MLA_Q_RANK], q_g)
    q = split_heads(cq @ w_uq, MLA_HEADS)
    q_nope, q_rope = q[..., :MLA_NOPE], q[..., MLA_NOPE:]
    if rope is not None:
        q_rope = apply_axial_rope(q_rope, rope[0], rope[1])
    return jnp.concatenate([q_nope, q_rope], axis=-1)

def mla_kv(p, kv_g, w_ukv, rope):
    b, l, _ = p.shape
    ckv = rmsnorm(p[..., MLA_Q_RANK:MLA_Q_RANK + MLA_KV_RANK], kv_g)
    kv = split_heads(ckv @ w_ukv, MLA_HEADS)
    k_nope, v = kv[..., :MLA_NOPE], kv[..., MLA_NOPE:]
    k_rope = p[..., MLA_Q_RANK + MLA_KV_RANK:][:, None]
    if rope is not None:
        k_rope = apply_axial_rope(k_rope, rope[0], rope[1])
    k = jnp.concatenate([k_nope, jnp.broadcast_to(k_rope, (b, MLA_HEADS, l, MLA_ROPE))], axis=-1)
    return k, v

def odd_mixer(h, hc, w_in, q_g, kv_g, w_uq, w_ukv, w_out, rope, want_ctx):
    p = h @ w_in
    pc = hc @ w_in
    scale = (MLA_NOPE + MLA_ROPE) ** -0.5
    q = mla_q(p, q_g, w_uq, rope)
    k, v = mla_kv(p, kv_g, w_ukv, rope)
    kc, vc = mla_kv(pc, kv_g, w_ukv, None)
    o = blocked_attention(q, jnp.concatenate([kc, k], axis=2), jnp.concatenate([vc, v], axis=2), scale)
    y = merge_heads(o) @ w_out
    if not want_ctx:
        return y, None
    qc = mla_q(pc, q_g, w_uq, None)
    return y, merge_heads(softmax_attend(qc, kc, vc, scale)) @ w_out

def peer_ffn(h, w_q, sub_keys, u_tab, v_tab):
    b, l, d = h.shape
    kk = PEER_TOPK
    blocks = h.reshape(b * l // PEER_BLOCK, PEER_BLOCK, d)

    def one_block(xb):
        t = xb.shape[0]
        qy = (xb @ w_q).reshape(t, PEER_HEADS, 2, PEER_DKEY // 2)
        s = jnp.einsum('thpd,hpnd->thpn', qy, sub_keys).astype(jnp.float32)
        s_top, i_top = lax.top_k(s, kk)
        comb = (s_top[:, :, 0, :, None] + s_top[:, :, 1, None, :]).reshape(t, PEER_HEADS, kk * kk)
        c_top, c_idx = lax.top_k(comb, kk)
        i1 = jnp.take_along_axis(i_top[:, :, 0], c_idx // kk, axis=-1)
        i2 = jnp.take_along_axis(i_top[:, :, 1], c_idx % kk, axis=-1)
        expert = i1 * PEER_KEYS + i2
        gate = jax.nn.softmax(c_top, axis=-1)
        u = u_tab[expert]
        vv = v_tab[expert]
        act = jax.nn.gelu(jnp.einsum('td,thkd->thk', xb, u).astype(jnp.float32), approximate=False)
        return jnp.einsum('thk,thkd->td', (gate * act).astype(xb.dtype), vv)

    return lax.map(one_block, blocks).reshape(b, l, d)

def first_inputs(seed: int = 0) -> dict:
    key = jax.random.key(seed)
    ks = iter(jax.random.split(key, 32))
    f32 = jnp.float32
    nrm = lambda shape, s: jax.random.normal(next(ks), shape, f32) * s
    gain = lambda shape: 1.0 + 0.02 * jax.random.normal(next(ks), shape, f32)
    dt = jnp.exp(jax.random.uniform(next(ks), (N_EVEN, 2, GDN_HEADS), f32, minval=-6.9, maxval=-2.3))
    return {
        'x': nrm((BATCH, SEQ, D_MODEL), 1.0),
        'c': nrm((BATCH, D_MODEL), 1.0),
        'ctx': nrm((BATCH, CTX_LEN, D_MODEL), 1.0),
        'c_ctx': nrm((D_MODEL,), 1.0),
        'ada_w': nrm((DEPTH, D_MODEL, 6 * D_MODEL), 0.5 * D_MODEL ** -0.5),
        'ada_b': nrm((DEPTH, 6 * D_MODEL), 0.01),
        'norm1_g': gain((DEPTH, D_MODEL)),
        'norm2_g': gain((DEPTH, D_MODEL)),
        'final_g': gain((D_MODEL,)),
        'even_w_in': nrm((N_EVEN, D_MODEL, EVEN_IN), D_MODEL ** -0.5),
        'even_conv_w': nrm((N_EVEN, GDN_CONV, 3 * GDN_W), GDN_CONV ** -0.5),
        'gdn_a_log': jnp.log(jax.random.uniform(next(ks), (N_EVEN, 2, GDN_HEADS), f32, minval=1.0, maxval=16.0)),
        'gdn_dt_bias': dt + jnp.log(-jnp.expm1(-dt)),
        'gdn_norm_g': gain((N_EVEN, GDN_HEAD_DIM)),
        'na_rpb': nrm((N_EVEN, NA_HEADS, 2 * NA_WIN_ROWS - 1, 2 * NA_WIN_COLS - 1), 0.1),
        'even_w_out': nrm((N_EVEN, EVEN_MIX, D_MODEL), EVEN_MIX ** -0.5),
        'mla_w_in': nrm((N_ODD, D_MODEL, MLA_IN), D_MODEL ** -0.5),
        'mla_q_g': gain((N_ODD, MLA_Q_RANK)),
        'mla_kv_g': gain((N_ODD, MLA_KV_RANK)),
        'mla_w_uq': nrm((N_ODD, MLA_Q_RANK, MLA_HEADS * (MLA_NOPE + MLA_ROPE)), MLA_Q_RANK ** -0.5),
        'mla_w_ukv': nrm((N_ODD, MLA_KV_RANK, MLA_HEADS * (MLA_NOPE + MLA_V)), MLA_KV_RANK ** -0.5),
        'mla_w_out': nrm((N_ODD, MLA_HEADS * MLA_V, D_MODEL), (MLA_HEADS * MLA_V) ** -0.5),
        'peer_w_q': nrm((DEPTH, D_MODEL, PEER_HEADS * PEER_DKEY), D_MODEL ** -0.5),
        'peer_sub_keys': nrm((DEPTH, PEER_HEADS, 2, PEER_KEYS, PEER_DKEY // 2), (PEER_DKEY // 2) ** -0.5),
        'peer_u': nrm((DEPTH, PEER_EXPERTS, D_MODEL), D_MODEL ** -0.5),
        'peer_v': nrm((DEPTH, PEER_EXPERTS, D_MODEL), PEER_HEADS ** -0.5),
    }

def first_block(x, c, ctx, c_ctx, ada_w, ada_b, norm1_g, norm2_g, final_g,
              even_w_in, even_conv_w, gdn_a_log, gdn_dt_bias, gdn_norm_g, na_rpb, even_w_out,
              mla_w_in, mla_q_g, mla_kv_g, mla_w_uq, mla_w_ukv, mla_w_out,
              peer_w_q, peer_sub_keys, peer_u, peer_v):
    rope = axial_rope_tables(x.shape[1], MLA_ROPE)
    cond = jax.nn.silu(c)
    cond_ctx = jax.nn.silu(c_ctx)[None, :]
    for layer in range(DEPTH):
        want_ctx = layer < DEPTH - 1
        i = layer // 2
        sh1, sc1, g1, sh2, sc2, g2 = jnp.split(cond @ ada_w[layer] + ada_b[layer], 6, axis=-1)
        csh1, csc1, cg1, csh2, csc2, cg2 = jnp.split(cond_ctx @ ada_w[layer] + ada_b[layer], 6, axis=-1)
        h = modulate(rmsnorm(x, norm1_g[layer]), sh1, sc1)
        hc = modulate(rmsnorm(ctx, norm1_g[layer]), csh1, csc1)
        if layer % 2 == 0:
            y, yc = even_mixer(h, hc, even_w_in[i], even_conv_w[i], gdn_a_log[i], gdn_dt_bias[i],
                               gdn_norm_g[i], na_rpb[i], even_w_out[i], want_ctx)
        else:
            y, yc = odd_mixer(h, hc, mla_w_in[i], mla_q_g[i], mla_kv_g[i], mla_w_uq[i], mla_w_ukv[i],
                              mla_w_out[i], rope, want_ctx)
        x = x + g1[:, None, :] * y
        x = x + g2[:, None, :] * peer_ffn(modulate(rmsnorm(x, norm2_g[layer]), sh2, sc2),
                                          peer_w_q[layer], peer_sub_keys[layer], peer_u[layer], peer_v[layer])
        if want_ctx:
            ctx = ctx + cg1[:, None, :] * yc
            ctx = ctx + cg2[:, None, :] * peer_ffn(modulate(rmsnorm(ctx, norm2_g[layer]), csh2, csc2),
                                                   peer_w_q[layer], peer_sub_keys[layer], peer_u[layer],
                                                   peer_v[layer])
    return rmsnorm(x, final_g)


CHUNK = 64
D_FF = 2816
CONV_W = D_MODEL
CONV_K = 3
CONV_GROUPS = 16
POOL_W = D_MODEL
POOL_WINDOWS = (2, 4, 8, 16)
POOL_GROUPS = len(POOL_WINDOWS)
POOL_GC = POOL_W // POOL_GROUPS
N_BRANCH = 2
IN_COLS = 3 * CONV_W + POOL_W + N_BRANCH * D_MODEL


def rms_norm(x, g):
    xf = x.astype(jnp.float32)
    y = xf * lax.rsqrt(jnp.mean(xf * xf, axis=-1, keepdims=True) + EPS)
    return (y * g.astype(jnp.float32)).astype(x.dtype)

def swiglu(h, w_gate_up, w_down):
    gu = h @ w_gate_up
    g, u = jnp.split(gu, 2, axis=-1)
    return (jax.nn.silu(g) * u) @ w_down

def causal_depthwise_conv(u, w):
    s = u.shape[1]
    u_pad = jnp.pad(u, ((0, 0), (CONV_K - 1, 0), (0, 0)))
    y = w[0] * u_pad[:, 0:s]
    for k in range(1, CONV_K):
        y = y + w[k] * u_pad[:, k:k + s]
    return y

def trailing_mean(u, win):
    s = u.shape[1]
    cs = jnp.cumsum(u, axis=1)
    cs_shift = jnp.pad(cs, ((0, 0), (win, 0), (0, 0)))[:, :s]
    count = jnp.minimum(jnp.arange(1, s + 1), win).astype(jnp.float32)
    return (cs - cs_shift) / count[None, :, None]

def pool_mixer(p, w_pg, b_pg, scale):
    b, s, _ = p.shape
    pf = p.astype(jnp.float32).reshape(b, s, POOL_GROUPS, POOL_GC)
    pooled = jnp.stack([trailing_mean(pf[:, :, gi], win) for gi, win in enumerate(POOL_WINDOWS)], axis=2)
    d = (pooled - pf).astype(p.dtype)
    y = jnp.einsum('bsgc,gcd->bsgd', d, w_pg) + b_pg
    return y.reshape(b, s, POOL_W) * scale

def hybrid_mixer(h, w_in, b_gate, conv_w, w_conv_out, w_pg, b_pg, pool_scale, w_pool_out, w_o):
    z = h @ w_in
    b_g, c_g, v, p, gates = jnp.split(
        z, [CONV_W, 2 * CONV_W, 3 * CONV_W, 3 * CONV_W + POOL_W], axis=-1)
    y_a = (b_g * causal_depthwise_conv(c_g * v, conv_w)) @ w_conv_out
    y_p = pool_mixer(p, w_pg, b_pg, pool_scale) @ w_pool_out
    g = jax.nn.sigmoid((gates + b_gate).astype(jnp.float32)).astype(h.dtype)
    g_a, g_p = jnp.split(g, N_BRANCH, axis=-1)
    return (g_a * y_a + g_p * y_p) @ w_o

def second_inputs(seed: int = 0) -> dict:
    key = jax.random.key(seed)
    ks = jax.random.split(key, 24)
    f32 = jnp.float32

    def nrm(k, shape, fan_in):
        return jax.random.normal(k, shape, f32) * (fan_in ** -0.5)

    def gain(k, shape):
        return 1.0 + 0.05 * jax.random.normal(k, shape, f32)

    L = DEPTH
    return {
        "x": jax.random.normal(ks[0], (BATCH, SEQ, D_MODEL), f32),
        "ffn1_pre": gain(ks[1], (L, D_MODEL)),
        "ffn1_post": gain(ks[2], (L, D_MODEL)),
        "ffn1_w_gate_up": nrm(ks[3], (L, D_MODEL, 2 * D_FF), D_MODEL),
        "ffn1_w_down": nrm(ks[4], (L, D_FF, D_MODEL), D_FF),
        "mix_pre": gain(ks[5], (L, D_MODEL)),
        "mix_post": gain(ks[6], (L, D_MODEL)),
        "w_in": nrm(ks[7], (L, D_MODEL, IN_COLS), D_MODEL),
        "b_gate": 0.01 * jax.random.normal(ks[8], (L, N_BRANCH * D_MODEL), f32),
        "conv_w": nrm(ks[9], (L, CONV_K, CONV_W), CONV_K),
        "w_conv_out": nrm(ks[10], (L, CONV_W, D_MODEL), CONV_W),
        "w_pool_group": nrm(ks[11], (L, POOL_GROUPS, POOL_GC, POOL_GC), POOL_GC),
        "b_pool_group": 0.01 * jax.random.normal(ks[12], (L, POOL_GROUPS, POOL_GC), f32),
        "pool_scale": gain(ks[13], (L, POOL_W)),
        "w_pool_out": nrm(ks[14], (L, POOL_W, D_MODEL), POOL_W),
        "w_o": nrm(ks[15], (L, D_MODEL, D_MODEL), D_MODEL),
        "ffn2_pre": gain(ks[16], (L, D_MODEL)),
        "ffn2_post": gain(ks[17], (L, D_MODEL)),
        "ffn2_w_gate_up": nrm(ks[18], (L, D_MODEL, 2 * D_FF), D_MODEL),
        "ffn2_w_down": nrm(ks[19], (L, D_FF, D_MODEL), D_FF),
    }

def second_block(x, ffn1_pre, ffn1_post, ffn1_w_gate_up, ffn1_w_down,
              mix_pre, mix_post, w_in, b_gate, conv_w, w_conv_out,
              w_pool_group, b_pool_group, pool_scale, w_pool_out, w_o,
              ffn2_pre, ffn2_post, ffn2_w_gate_up, ffn2_w_down):
    for l in range(DEPTH):
        h = swiglu(rms_norm(x, ffn1_pre[l]), ffn1_w_gate_up[l], ffn1_w_down[l])
        x = x + 0.5 * rms_norm(h, ffn1_post[l])
        h = hybrid_mixer(rms_norm(x, mix_pre[l]), w_in[l], b_gate[l], conv_w[l],
                         w_conv_out[l], w_pool_group[l], b_pool_group[l],
                         pool_scale[l], w_pool_out[l], w_o[l])
        x = x + rms_norm(h, mix_post[l])
        h = swiglu(rms_norm(x, ffn2_pre[l]), ffn2_w_gate_up[l], ffn2_w_down[l])
        x = x + 0.5 * rms_norm(h, ffn2_post[l])
    return x


def setup_inputs(seed=0):
    out = dict(first_inputs(seed))
    for name, value in second_inputs(seed + 1).items():
        if name != "x":
            out[name + "_2"] = value
    return out


def reference(
    x, c, ctx, c_ctx, ada_w, ada_b, norm1_g, norm2_g, final_g, even_w_in, even_conv_w,
    gdn_a_log, gdn_dt_bias, gdn_norm_g, na_rpb, even_w_out, mla_w_in, mla_q_g, mla_kv_g,
    mla_w_uq, mla_w_ukv, mla_w_out, peer_w_q, peer_sub_keys, peer_u, peer_v, ffn1_pre_2,
    ffn1_post_2, ffn1_w_gate_up_2, ffn1_w_down_2, mix_pre_2, mix_post_2, w_in_2, b_gate_2,
    conv_w_2, w_conv_out_2, w_pool_group_2, b_pool_group_2, pool_scale_2, w_pool_out_2, w_o_2,
    ffn2_pre_2, ffn2_post_2, ffn2_w_gate_up_2, ffn2_w_down_2,
):
    x = first_block(
        x, c, ctx, c_ctx, ada_w, ada_b, norm1_g, norm2_g, final_g, even_w_in, even_conv_w,
        gdn_a_log, gdn_dt_bias, gdn_norm_g, na_rpb, even_w_out, mla_w_in, mla_q_g, mla_kv_g,
        mla_w_uq, mla_w_ukv, mla_w_out, peer_w_q, peer_sub_keys, peer_u, peer_v,
    )
    return second_block(
        x, ffn1_pre_2, ffn1_post_2, ffn1_w_gate_up_2, ffn1_w_down_2, mix_pre_2, mix_post_2,
        w_in_2, b_gate_2, conv_w_2, w_conv_out_2, w_pool_group_2, b_pool_group_2, pool_scale_2,
        w_pool_out_2, w_o_2, ffn2_pre_2, ffn2_post_2, ffn2_w_gate_up_2, ffn2_w_down_2,
    )


_drawn_inputs = setup_inputs


def setup_inputs(seed=0):
    import zlib

    import numpy as np

    out = dict(_drawn_inputs(seed))
    spreads = {}
    factors = {'norm1_g': 4.111,
     'gdn_norm_g': 5.408,
     'na_rpb': 8.0,
     'mla_q_g': 8.0,
     'mla_kv_g': 8.0,
     'b_gate_2': 8.0,
     'b_pool_group_2': 6.739}
    for name, (base, spread) in spreads.items():
        noise = np.random.default_rng([zlib.crc32(name.encode()), seed]).standard_normal(out[name].shape)
        drawn = base * np.exp(spread * noise) if base else spread * noise
        out[name] = jnp.asarray(drawn.astype(out[name].dtype))
    for name, factor in factors.items():
        out[name] = (out[name] * factor).astype(out[name].dtype)
    return out
```

```python
from collections import namedtuple
from contextlib import contextmanager

import numpy as np

import concourse.bass as bass
from concourse import mybir

F32 = mybir.dt.float32
U32 = mybir.dt.uint32
ACT = mybir.ActivationFunctionType
ALU = mybir.AluOpType
AX = mybir.AxisListType

P = 128
L = 256
T2 = 2 * L
D = 1024
DT = D // P
EPS = 1e-6
GRID_W = 64
HEADS = 8
NA_DH = 64
GDN_H = 4
CHUNK = 128
NCHUNK = T2 // CHUNK
LEVELS = 7
KEYS = 128
TOPK = 16
D_FF = 2816
FF_T = D_FF // P
POOL_WINDOWS = (2, 4, 8, 16)
RING = 4
SLOT = 11 * P
BIG = 32768
AUX = 5120
CTX, TOK = 0, L

VECTORS = [
    ("c", 8), ("c_ctx", 8), ("ada_b", 96), ("norm1_g", 16), ("norm2_g", 16), ("final_g", 8),
    ("conv_w", 60), ("gdn_norm_g", 1), ("a_log", 8), ("dt_bias", 8), ("mla_q_g", 3), ("mla_kv_g", 2),
    ("ffn1_pre", 16), ("ffn1_post", 16), ("mix_pre", 16), ("mix_post", 16), ("ffn2_pre", 16),
    ("ffn2_post", 16), ("b_gate", 32), ("conv_w_2", 48), ("b_pool", 16), ("pool_scale", 16),
]
VEC_AT = {}
_n = 0
for _name, _w in VECTORS:
    VEC_AT[_name] = _n
    _n += _w
N_VEC = _n

def constants():
    i = np.arange(P)
    parts = {}
    parts["ident"] = np.eye(P)
    parts["ones"] = np.ones((P, P))
    parts["iota"] = np.broadcast_to(i, (P, P))
    parts["eps"] = np.broadcast_to(np.array([EPS, 4 * EPS, P * EPS, 1.0]), (P, 4))
    resident = sum(v.shape[1] for v in parts.values())
    parts["tri"] = np.concatenate([i[:, None] <= i[None, :], i[:, None] >= i[None, :]], 1)
    masks = []
    for d in range(2):
        for lev in range(LEVELS):
            b = 1 << lev
            m = (i[:, None] // (2 * b) == i[None, :] // (2 * b)) & (i[:, None] % (2 * b) >= b) & (i[None, :] % (2 * b) < b)
            masks.append(m if d == 0 else m.T)
    parts["levels"] = np.concatenate(masks, 1)
    start = np.clip(i % GRID_W - 8, 0, GRID_W - 16)[:, None]
    col = (np.arange(L) % GRID_W)[None, :]
    parts["window"] = np.where((col >= start) & (col < start + 16), 0.0, -1e30)
    inv = (10000.0 ** (-np.arange(0, 32, 2, dtype=np.float32) / 32)).astype(np.float32)
    t = np.arange(L)
    ar = (t // GRID_W).astype(np.float32)[:, None] * inv
    ac = (t % GRID_W).astype(np.float32)[:, None] * inv
    ang = np.concatenate([ar, ar, ac, ac], -1).T
    parts["cos"] = np.concatenate([np.cos(ang)] * 2, 0)
    parts["sin"] = np.concatenate([np.sin(ang)] * 2, 0)
    rot = np.zeros((P, P))
    for base in (0, 64):
        for blk in (0, 32):
            for j in range(16):
                rot[base + blk + 16 + j, base + blk + j] = -1.0
                rot[base + blk + j, base + blk + 16 + j] = 1.0
    parts["rot"] = rot
    parts["inv_count"] = np.concatenate(
        [np.broadcast_to(1.0 / np.minimum(t + 1, w), (P, L)) for w in POOL_WINDOWS], 1)
    at, n = {}, 0
    for name, v in parts.items():
        at[name] = (n, v.shape[1])
        n += v.shape[1]
    return np.ascontiguousarray(np.concatenate(list(parts.values()), 1).astype(np.float32)), at, resident


CONSTS, CONST_AT, N_RESIDENT = constants()


Unit = namedtuple("Unit", "q k keys v bias base dv out")
MixerWeights = namedtuple("MixerWeights", "w_in w_pg w_conv_out w_pool_out w_o")


class Core:
    pass


def at_least(eng, sem, value):
    if isinstance(value, int) and value <= 0:
        return
    eng.wait_ge(sem, value)


class Chain:

    def __init__(self, eng, sem):
        self.eng, self.sem, self.n = eng, sem, 0

    def add(self, ins):
        ins.then_inc(self.sem, 1)
        self.n += 1

    def settle(self):
        at_least(self.eng, self.sem, self.n)

    def link(self, ins):
        self.add(ins)
        self.settle()


@contextmanager
def stage(k, name, *signals):
    nc = k.nc
    k.stage_no += 1
    s = namedtuple("Signals", signals)(*(nc.alloc_semaphore(f"{name}_{k.stage_no}_{n}") for n in signals))
    with nc.Block() as block:
        yield block, s
    k.spent += list(s)
    if len(k.spent) > 130:
        nc.clear_and_free_semaphores(k.spent)
        nc.all_engine_barrier()
        k.spent = []


class Weights:

    def __init__(self, k, name, kc, chunks):
        self.k, self.dram, self.kc, self.chunks, self.name = k, k.io[name], kc, chunks, name
        self.loaded = None

    def load(self, sp, q, s):
        dst = self.k.ring[:, s, 0:self.kc * P]
        if isinstance(q, int):
            src = self.dram[self.first + q]
        else:
            src = self.dram[bass.ds(q + self.first, 1)].rearrange("o p n -> (o p) n")
        sp.dma_start(dst, src).then_inc(self.loaded[s], 16)

    def retire(self):
        self.k.spent += self.loaded

    def prime(self, sp, first=0):
        k = self.k
        self.first = first
        self.loaded = [k.nc.alloc_semaphore(f"{self.name}_loaded{s}_{k.stage_no}") for s in range(RING)]
        for q in range(min(RING, self.chunks)):
            self.load(sp, q, q)


def repeat(eng, rounds, body):
    if rounds > 0:
        body(0)
    if rounds > 1:
        with eng.Fori(1, rounds) as r:
            body(r)


def linear(k, name, w, kt, t, rhs, epilogue, engine="vector", then=None):
    nc = k.nc
    per_tile = kt // w.kc
    tiles = 1 if t == 2 else 512 // t
    c_unit = per_tile * tiles
    units = w.chunks // c_unit
    body = max(2, RING // c_unit)
    rounds, tail = divmod(units, body)
    assert units * c_unit == w.chunks and (body * c_unit) % RING == 0
    with stage(k, name, "chunk_used", "bank_free") as (block, s):

        @block.sync
        def _(sp):
            if w.loaded is None:
                w.prime(sp)

            def refill(r):
                for slot in range(RING):
                    sp.wait_ge(s.chunk_used, r * RING + (slot + 1))
                    w.load(sp, r * RING + (slot + RING), slot)

            full, rest = divmod(max(w.chunks - RING, 0), RING)
            repeat(sp, full, refill)
            for slot in range(rest):
                sp.wait_ge(s.chunk_used, full * RING + slot + 1)
                w.load(sp, full * RING + slot + RING, slot)
            if then is not None:
                sp.wait_ge(s.chunk_used, w.chunks)
                then(sp)

        @block.tensor
        def _(pe):
            def unit(r, b):
                at_least(pe, s.bank_free, (r - 1) * body + (b + 1))
                for c in range(c_unit):
                    at = b * c_unit + c
                    slot = at % RING
                    tile, part = divmod(c, per_tile)
                    pe.wait_ge(w.loaded[slot], r * (16 * body * c_unit // RING) + 16 * (at // RING + 1))
                    for j in range(w.kc):
                        kk = part * w.kc + j
                        last = nc.tensor.matmul(k.bank[b][:, tile * t:(tile + 1) * t],
                                                k.ring[:, slot, j * P:(j + 1) * P],
                                                rhs(kk, r * body + b),
                                                start=kk == 0, stop=kk == kt - 1)
                    last.then_inc(s.chunk_used, 1)

            repeat(pe, rounds, lambda r: [unit(r, b) for b in range(body)])
            for b in range(tail):
                unit(rounds, b)

        def empty(eng):
            def unit(r, b):
                eng.wait_ge(s.chunk_used, r * (body * c_unit) + (b + 1) * c_unit)
                epilogue(r * body + b, k.bank[b]).then_inc(s.bank_free, 1)

            repeat(eng, rounds, lambda r: [unit(r, b) for b in range(body)])
            for b in range(tail):
                unit(rounds, b)

        if engine == "vector":
            @block.vector
            def _(dve):
                empty(dve)
        else:
            @block.scalar
            def _(act):
                empty(act)
    w.retire()


def tile_of(buf, n, lo=0, hi=None):
    hi = buf.shape[2] if hi is None else hi
    if isinstance(n, int):
        return buf[:, n, lo:hi]
    return buf[:, bass.ds(n, 1), lo:hi].rearrange("p o t -> p (o t)")


def load(k, name, pairs, more=None):
    with stage(k, name, "arrived") as (block, s):

        @block.sync
        def _(sp):
            for dst, src in pairs:
                sp.dma_start(dst, src).then_inc(s.arrived, 16)
            sp.wait_ge(s.arrived, 16 * len(pairs))
            if more is not None:
                more(sp)


def condition(k, w):
    nc = k.nc
    c2 = k.aux[:, 0:16].rearrange("p (t j) -> p t j", j=2)
    with stage(k, "silu_c", "done") as (block, s):

        @block.scalar
        def _(act):
            nc.scalar.activation(c2[:, :, 0], k.v("c_ctx"), ACT.Silu)
            nc.scalar.activation(c2[:, :, 1], k.v("c"), ACT.Silu)

    linear(k, "ada", w, DT, 2, lambda kk, u: c2[:, kk, :],
           lambda u, bank: nc.vector.tensor_copy(tile_of(k.mod, u), bank[:, 0:2]))
    with stage(k, "ada_bias", "added") as (block, s):

        @block.vector
        def _(dve):
            chain = Chain(dve, s.added)
            chain.link(nc.vector.tensor_tensor(k.mod[:, :, :], k.mod[:, :, :],
                                               k.v("ada_b").unsqueeze(2).broadcast_to([P, 96, 2]), ALU.add))
            for layer in range(2):
                for part, gain in ((1, "norm1_g"), (4, "norm2_g")):
                    sc = k.mod[:, 48 * layer + 8 * part:48 * layer + 8 * part + 8, :]
                    g = k.v(gain, 8 * layer, 8).unsqueeze(2).broadcast_to([P, 8, 2])
                    chain.add(nc.vector.scalar_tensor_tensor(sc, sc, 1.0, g, ALU.add, ALU.mult))


def norm(k, name, src, dst, tiles, t, dim, gain, shift=None, residual=None, prime=None, squares=None):
    nc = k.nc
    squares = squares or dst
    factor = residual[1] if residual else 1.0
    std, rstd = k.aux[:, 0:t], k.aux[:, 512:512 + t]
    stat = k.bank[7][:, 0:t]
    eps = {1.0: 0, 0.5: 1}[factor]
    with stage(k, name, "sq_a", "sq_v", "summed", "rooted", "scaled", "done") as (block, s):

        @block.scalar
        def _(act):
            for i in range(0, tiles, 2):
                nc.scalar.activation(squares(i), src(i), ACT.Square).then_inc(s.sq_a, 1)
            act.wait_ge(s.summed, 1)
            nc.scalar.activation(std, stat, ACT.Sqrt, bias=k.eps[:, eps:eps + 1],
                                 scale=1.0 / (dim * factor * factor)).then_inc(s.rooted, 1)
            if shift is not None:
                for i in range(tiles):
                    act.wait_ge(s.scaled, i + 1)
                    for (lo, hi), sh in shift(i):
                        nc.scalar.activation(dst(i)[:, lo:hi], dst(i)[:, lo:hi], ACT.Identity, bias=sh)

        @block.vector
        def _(dve):
            for i in range(1, tiles, 2):
                nc.vector.tensor_tensor(squares(i), src(i), src(i), ALU.mult).then_inc(s.sq_v, 1)
            dve.wait_ge(s.rooted, 1)
            nc.vector.reciprocal(rstd, std).then_inc(s.done, 1)
            dve.wait_ge(s.done, 1)
            for i in range(tiles):
                parts = gain(i)
                for n, ((lo, hi), g) in enumerate(parts):
                    ins = nc.vector.scalar_tensor_tensor(dst(i)[:, lo:hi], src(i)[:, lo:hi], g,
                                                         rstd[:, lo:hi], ALU.mult, ALU.mult)
                    if n == len(parts) - 1:
                        ins.then_inc(s.scaled, 1)
            if residual is not None:
                for i in range(tiles):
                    dve.wait_ge(s.scaled, i + 1)
                    x = residual[0](i)
                    nc.vector.tensor_tensor(x, x, dst(i), ALU.add)

        @block.tensor
        def _(pe):
            for i in range(tiles):
                pe.wait_ge(s.sq_v if i % 2 else s.sq_a, i // 2 + 1)
                last = nc.tensor.matmul(stat, k.ones, squares(i), start=i == 0, stop=i == tiles - 1)
            last.then_inc(s.summed, 1)

        @block.sync
        def _(sp):
            if prime is not None:
                prime(sp)


def mod_norm(k, layer, second, halves, prime=None):
    part = 3 if second else 0
    lo, hi = halves
    base = 48 * layer + 8 * part

    def scalars(chunk):
        def at(i):
            out = []
            if lo < L:
                out.append(((0, L), k.mod[:, base + 8 * chunk + i, 0:1]))
            if hi > L:
                out.append(((L - lo, hi - lo), k.mod[:, base + 8 * chunk + i, 1:2]))
            return out
        return at

    norm(k, "mod_norm", lambda i: k.x[:, i, lo:hi], lambda i: k.h[:, i, lo:hi], DT, hi - lo, D,
         gain=scalars(1), shift=scalars(0), prime=prime)


def transposes(k, name, jobs):
    nc = k.nc
    with stage(k, name, "turned", "copied") as (block, s):

        @block.tensor
        def _(pe):
            for n, (src, _) in enumerate(jobs):
                at_least(pe, s.copied, n - 3)
                nc.tensor.transpose(k.bank[n % 4][:, 0:P], src, k.ident).then_inc(s.turned, 1)

        @block.vector
        def _(dve):
            for n, (_, dst) in enumerate(jobs):
                dve.wait_ge(s.turned, n + 1)
                nc.vector.tensor_copy(dst, k.bank[n % 4][:, 0:P]).then_inc(s.copied, 1)


def attention(k, name, units, scale, scratch, prime=None):
    nc = k.nc
    at = [scratch]

    def take(n):
        at[0] += n
        return k.big[:, at[0] - n:at[0]]

    score = [take(512) for _ in range(2)]
    prob = [take(512) for _ in range(2)]
    prob_t = [take(512) for _ in range(2)]
    bias = [take(L) for _ in range(2)]
    stat = [take(8) for _ in range(2)]
    n_units = len(units)
    biased = units[0].bias is not None
    exp_scale = 1.0 if biased else scale
    with stage(k, name, "scored", "maxed", "expd", "normed", "turned", "probs_t", "mixed", "stored",
               "chain", "bias_0", "bias_1", "bias_ready") as (block, s):
        bias_loaded = [s.bias_0, s.bias_1]

        @block.sync
        def _(sp):
            if biased:
                for u, un in enumerate(units):
                    at_least(sp, s.maxed, u - 1)
                    sp.dma_start(bias[u % 2], un.bias).then_inc(bias_loaded[u % 2], 16)
            if prime is not None:
                prime(sp)

        @block.gpsimd
        def _(pool):
            if biased:
                for u in range(n_units):
                    pool.wait_ge(bias_loaded[u % 2], 16 * (u // 2 + 1))
                    nc.gpsimd.tensor_tensor(bias[u % 2], bias[u % 2], k.window, ALU.add).then_inc(s.bias_ready, 1)

        @block.tensor
        def _(pe):
            def scores(u):
                un = units[u]
                at_least(pe, s.expd, u - 1)
                for j, (q, key) in enumerate(zip(un.q, un.k)):
                    last = nc.tensor.matmul(k.bank[u % 2][:, 0:un.keys], q, key,
                                            start=j == 0, stop=j == len(un.q) - 1)
                last.then_inc(s.scored, 1)

            def mix(u):
                un = units[u]
                pe.wait_ge(s.probs_t, u + 1)
                at_least(pe, s.stored, u - 1)
                n = un.keys // P
                for j in range(n):
                    last = nc.tensor.matmul(k.bank[4 + u % 2][un.base:un.base + un.dv, 0:P], un.v[j],
                                            prob_t[u % 2][:, j * P:(j + 1) * P], start=j == 0, stop=j == n - 1)
                last.then_inc(s.mixed, 1)

            scores(0)
            if n_units > 1:
                scores(1)
            for u in range(n_units):
                pe.wait_ge(s.normed, u + 1)
                at_least(pe, s.probs_t, u - 1)
                for j in range(units[u].keys // P):
                    last = nc.tensor.transpose(k.bank[2 + u % 2][:, j * P:(j + 1) * P],
                                               prob[u % 2][:, j * P:(j + 1) * P], k.ident)
                last.then_inc(s.turned, 1)
                if u >= 1:
                    mix(u - 1)
                if u + 2 < n_units:
                    scores(u + 2)
            mix(n_units - 1)

        @block.scalar
        def _(act):
            def expd(u):
                un = units[u]
                src = score[u % 2] if biased else k.bank[u % 2]
                act.wait_ge(s.maxed, u + 1)
                at_least(act, s.turned, u - 1)
                nc.scalar.activation(prob[u % 2][:, 0:un.keys], src[:, 0:un.keys], ACT.Exp, scale=exp_scale,
                                     bias=stat[u % 2][:, 1:2], accum_out=stat[u % 2][:, 2:3]).then_inc(s.expd, 1)

            def store(u):
                un = units[u]
                act.wait_ge(s.mixed, u + 1)
                nc.scalar.activation(un.out, k.bank[4 + u % 2][un.base:un.base + un.dv, 0:P],
                                     ACT.Copy).then_inc(s.stored, 1)

            expd(0)
            for u in range(n_units):
                if u + 1 < n_units:
                    expd(u + 1)
                n = units[u].keys
                act.wait_ge(s.turned, u + 1)
                at_least(act, s.mixed, u - 1)
                nc.scalar.activation(prob_t[u % 2][:, 0:n], k.bank[2 + u % 2][:, 0:n],
                                     ACT.Copy).then_inc(s.probs_t, 1)
                if u >= 1:
                    store(u - 1)
            store(n_units - 1)

        @block.vector
        def _(dve):
            chain = Chain(dve, s.chain)

            def maxima(u):
                un = units[u]
                bank, st = k.bank[u % 2], stat[u % 2]
                dve.wait_ge(s.scored, u + 1)
                at_least(dve, s.expd, u - 1)
                src = bank
                if biased:
                    dve.wait_ge(s.bias_ready, u + 1)
                    src = score[u % 2]
                    chain.add(nc.vector.tensor_scalar(src[:, 0:L], bank[:, 0:L], scale, None, ALU.mult))
                    chain.link(nc.vector.scalar_tensor_tensor(src[:, L:T2], bank[:, L:T2], scale, bias[u % 2],
                                                              ALU.mult, ALU.add))
                chain.link(nc.vector.reduce_max(st[:, 0:1], src[:, 0:un.keys], AX.X))
                nc.vector.tensor_scalar(st[:, 1:2], st[:, 0:1], -exp_scale, None, ALU.mult).then_inc(s.maxed, 1)

            maxima(0)
            for u in range(n_units):
                if u + 1 < n_units:
                    maxima(u + 1)
                st = stat[u % 2]
                dve.wait_ge(s.expd, u + 1)
                chain.link(nc.vector.reciprocal(st[:, 3:4], st[:, 2:3]))
                n = units[u].keys
                nc.vector.tensor_scalar(prob[u % 2][:, 0:n], prob[u % 2][:, 0:n], st[:, 3:4], None,
                                        ALU.mult).then_inc(s.normed, 1)


EVEN_P = 0
EVEN_Y = 29 * T2
EVEN_WORK = EVEN_Y + 8 * T2


def even_mixer(k, w_in, w_out, then):
    nc = k.nc
    p = k.view(EVEN_P, 29, T2)
    y = k.view(EVEN_Y, 8, T2)

    linear(k, "even_in", w_in, DT, T2, lambda kk, u: k.h[:, kk, :],
           lambda u, bank: nc.scalar.activation(tile_of(p, u), bank[:, 0:T2], ACT.Copy), engine="scalar",
           then=lambda sp: w_out.prime(sp))

    v_tok = k.view(EVEN_WORK, NCHUNK, 512)
    transposes(k, "na_v", [(p[:, 8 + f, c * P:(c + 1) * P], v_tok[:, c, f * P:(f + 1) * P])
                           for c in range(NCHUNK) for f in range(4)])
    load(k, "window", [(k.aux[:, 0:L], k.const("window"))])
    k.window = k.aux[:, 0:L]
    for first in (TOK, CTX):
        units = []
        for head in range(HEADS):
            base, tile = NA_DH * (head % 2), head // 2
            rows = slice(base, base + NA_DH)
            for qt in range(2):
                cols = slice(first + qt * P, first + (qt + 1) * P)
                keys = T2 if first == TOK else L
                units.append(Unit(
                    q=[p[rows, tile, cols]], k=[p[rows, 4 + tile, 0:keys]], keys=keys,
                    v=[v_tok[:, c, head * NA_DH:(head + 1) * NA_DH] for c in range(keys // P)],
                    bias=k.io["na_bias"][head, qt] if first == TOK else None,
                    base=base, dv=NA_DH, out=y[rows, tile, cols]))
        attention(k, "na", units, NA_DH ** -0.5, EVEN_WORK + NCHUNK * 512)

    gated_delta(k, p, y)

    def add_residual(u, bank):
        for half, lo in ((0, CTX), (1, TOK)):
            x = tile_of(k.x, u, lo, lo + L)
            ins = nc.vector.scalar_tensor_tensor(x, bank[:, lo:lo + L], k.mod_at(0, 2, u, half), x,
                                                 ALU.mult, ALU.add)
        return ins

    linear(k, "even_out", w_out, DT, T2, lambda kk, u: y[:, kk, :], add_residual, then=then)


def gated_delta(k, p, y):
    nc = k.nc
    conv_w = k.v("conv_w").rearrange("p (t j) -> p t j", j=5)
    with stage(k, "conv", "chain", "conved") as (block, s):

        @block.vector
        def _(dve):
            chain = Chain(dve, s.chain)
            for pair in range(6):
                for j in (2, 0, 1, 3, 4):
                    for t in (2 * pair, 2 * pair + 1):
                        src = p[:, 12 + t, :].rearrange("p (h n) -> p h n", h=2)
                        dst = p[:, t, :].rearrange("p (h n) -> p h n", h=2)
                        tap = conv_w[:, t, j:j + 1]
                        if j == 2:
                            ins = nc.vector.tensor_scalar(dst, src, tap, None, ALU.mult)
                        else:
                            o = j - 2
                            a, b = max(0, -o), L - max(0, o)
                            ins = nc.vector.scalar_tensor_tensor(dst[:, :, a:b], src[:, :, a + o:b + o], tap,
                                                                 dst[:, :, a:b], ALU.mult, ALU.add)
                        if j == 4:
                            ins.then_inc(s.conved, 1)
                        else:
                            chain.add(ins)
                    if j != 4:
                        chain.settle()

        @block.scalar
        def _(act):
            for t in range(12):
                act.wait_ge(s.conved, t + 1)
                nc.scalar.activation(p[:, t, :], p[:, t, :], ACT.Silu)

    sq = k.view(EVEN_WORK, 8, T2)
    root = k.view(EVEN_WORK + 8 * T2, 8, T2)
    with stage(k, "l2norm", "squared", "summed", "rooted", "inverted") as (block, s):

        @block.vector
        def _(dve):
            for t in range(8):
                nc.vector.tensor_tensor(sq[:, t, :], p[:, t, :], p[:, t, :], ALU.mult).then_inc(s.squared, 1)
            for t in range(8):
                dve.wait_ge(s.rooted, t + 1)
                nc.vector.reciprocal(root[:, t, :], root[:, t, :]).then_inc(s.inverted, 1)
            for t in range(8):
                dve.wait_ge(s.inverted, t + 1)
                nc.vector.tensor_tensor(p[:, t, :], p[:, t, :], root[:, t, :], ALU.mult)

        @block.tensor
        def _(pe):
            for t in range(8):
                pe.wait_ge(s.squared, t + 1)
                nc.tensor.matmul(k.bank[t][:, :], k.ones, sq[:, t, :], start=True, stop=True).then_inc(s.summed, 1)

        @block.scalar
        def _(act):
            for t in range(8):
                act.wait_ge(s.summed, t + 1)
                nc.scalar.activation(root[:, t, :], k.bank[t][:, :], ACT.Sqrt,
                                     bias=k.eps[:, 2:3] if t < 4 else k.eps[:, 0:1],
                                     scale=float(P) if t < 4 else 1.0).then_inc(s.rooted, 1)

    k_tok = k.view(12 * T2, NCHUNK, 512)
    v_tok = k.view(16 * T2, NCHUNK, 512)
    out = k.view(20 * T2, GDN_H, T2)
    gate_t = k.view(EVEN_WORK, NCHUNK, P)
    transposes(k, "gdn_turn",
               [(p[:, 28, c * P:(c + 1) * P], gate_t[:, c, :]) for c in range(NCHUNK)]
               + [(p[:, 4 + h, c * P:(c + 1) * P], k_tok[:, c, h * P:(h + 1) * P])
                  for c in range(NCHUNK) for h in range(GDN_H)]
               + [(p[:, 8 + h, c * P:(c + 1) * P], v_tok[:, c, h * P:(h + 1) * P])
                  for c in range(NCHUNK) for h in range(GDN_H)])

    names = ["a", "beta", "abs", "e", "g", "gc", "eg", "total", "k_end", "s_end", "nbeg"]
    tok = {n: k.aux[:, 32 * i:32 * (i + 1)].rearrange("p (c d) -> p c d", d=8) for i, n in enumerate(names)}
    levels = k.aux[:, 512:512 + 2 * LEVELS * P].rearrange("p (l n) -> p l n", n=P)
    tri = k.aux[:, 2304:2304 + 2 * P]
    state = [k.aux[:, 2560 + 512 * d:3072 + 512 * d].rearrange("p (h n) -> p h n", h=GDN_H) for d in range(2)]
    with stage(k, "gates", "tables", "a_ready", "act", "chain", "cumsum") as (block, s):

        @block.sync
        def _(sp):
            sp.dma_start(tri, k.const("tri")).then_inc(s.tables, 16)
            sp.dma_start(levels[:, :, :], k.const("levels").rearrange("p (l n) -> p l n", n=P)).then_inc(s.tables, 16)
            sp.wait_ge(s.tables, 32)

        @block.vector
        def _(dve):
            chain = Chain(dve, s.chain)
            for d in range(2):
                chain.add(nc.vector.tensor_copy(tok["a"][:, :, 4 * d:4 * d + 4], gate_t[:, :, 8 * d:8 * d + 4]))
            chain.settle()
            dt = k.v("dt_bias").unsqueeze(1).broadcast_to([P, NCHUNK, 8])
            nc.vector.tensor_tensor(tok["a"], tok["a"], dt, ALU.add).then_inc(s.a_ready, 1)
            dve.wait_ge(s.act, 6)
            dve.wait_ge(s.a_ready, 1)
            chain.link(nc.vector.scalar_tensor_tensor(tok["e"], tok["a"], 0.0, tok["e"], ALU.max, ALU.add))
            ea = k.aux[:, 384:392].unsqueeze(1).broadcast_to([P, NCHUNK, 8])
            chain.link(nc.vector.scalar_tensor_tensor(tok["g"], tok["e"], -1.0, ea, ALU.mult, ALU.mult))
            dve.wait_ge(s.cumsum, 1)
            sums = k.bank[0][:, 0:64]
            for d in range(2):
                src = sums[:, 16 * d:16 * d + 16].rearrange("p (c h) -> p c h", h=4)
                chain.add(nc.vector.tensor_copy(tok["gc"][:, :, 4 * d:4 * d + 4], src))
            chain.link(nc.vector.tensor_copy(tok["total"], sums[:, 32:64].rearrange("p (c d) -> p c d", d=8)))
            chain.link(nc.vector.tensor_tensor(tok["k_end"], tok["total"], tok["gc"], ALU.subtract))
            dve.wait_ge(s.act, 9)
            nc.vector.scalar_tensor_tensor(tok["nbeg"], tok["beta"], -1.0, tok["eg"], ALU.mult, ALU.mult)
            for d in range(2):
                nc.vector.memset(state[d], 0.0)
            nc.vector.memset(out[:, :, :], 0.0)

        @block.scalar
        def _(act):
            for d in range(2):
                nc.scalar.activation(tok["beta"][:, :, 4 * d:4 * d + 4], gate_t[:, :, 8 * d + 4:8 * d + 8],
                                     ACT.Sigmoid).then_inc(s.act, 1)
            act.wait_ge(s.a_ready, 1)
            nc.scalar.activation(tok["abs"], tok["a"], ACT.Abs).then_inc(s.act, 1)
            act.wait_ge(s.act, 3)
            nc.scalar.activation(tok["e"], tok["abs"], ACT.Exp, scale=-1.0).then_inc(s.act, 1)
            nc.scalar.activation(k.aux[:, 384:392], k.v("a_log"), ACT.Exp).then_inc(s.act, 1)
            act.wait_ge(s.act, 4)
            nc.scalar.activation(tok["e"], tok["e"], ACT.Ln, bias=k.eps[:, 3:4]).then_inc(s.act, 1)
            act.wait_ge(s.chain, 8)
            nc.scalar.activation(tok["eg"], tok["gc"], ACT.Exp).then_inc(s.act, 1)
            nc.scalar.activation(tok["s_end"], tok["total"], ACT.Exp).then_inc(s.act, 1)
            nc.scalar.activation(tok["k_end"], tok["k_end"], ACT.Exp).then_inc(s.act, 1)

        @block.tensor
        def _(pe):
            pe.wait_ge(s.tables, 32)
            pe.wait_ge(s.chain, 4)
            for d in range(2):
                nc.tensor.matmul(k.bank[0][:, 16 * d:16 * d + 16], tri[:, d * P:(d + 1) * P],
                                 tok["g"][:, :, 4 * d:4 * d + 4], start=True, stop=True)
            nc.tensor.matmul(k.bank[0][:, 32:64], k.ones, tok["g"], start=True, stop=True).then_inc(s.cumsum, 1)

    delta_rule(k, p, k_tok, v_tok, out, tok, levels, tri, state)

    z = p[:, 24:28, :]
    sq = k.view(EVEN_WORK, GDN_H, T2)
    root = k.view(EVEN_WORK + 4 * T2, GDN_H, T2)
    with stage(k, "gdn_out", "squared", "summed", "gated", "rooted", "chain") as (block, s):

        @block.vector
        def _(dve):
            chain = Chain(dve, s.chain)
            for h in range(GDN_H):
                nc.vector.tensor_tensor(sq[:, h, :], out[:, h, :], out[:, h, :], ALU.mult).then_inc(s.squared, 1)
            dve.wait_ge(s.rooted, GDN_H)
            chain.link(nc.vector.reciprocal(root[:, :, :], root[:, :, :]))
            chain.link(nc.vector.scalar_tensor_tensor(out[:, :, :], out[:, :, :], k.v("gdn_norm_g"), root[:, :, :],
                                                      ALU.mult, ALU.mult))
            nc.vector.tensor_tensor(y[:, 4:8, :], out[:, :, :], z, ALU.mult)

        @block.tensor
        def _(pe):
            for h in range(GDN_H):
                pe.wait_ge(s.squared, h + 1)
                nc.tensor.matmul(k.bank[h][:, :], k.ones, sq[:, h, :], start=True, stop=True).then_inc(s.summed, 1)

        @block.scalar
        def _(act):
            nc.scalar.activation(z, z, ACT.Silu)
            for h in range(GDN_H):
                act.wait_ge(s.summed, h + 1)
                nc.scalar.activation(root[:, h, :], k.bank[h][:, :], ACT.Sqrt, bias=k.eps[:, 0:1],
                                     scale=1.0 / P).then_inc(s.rooted, 1)


def delta_rule(k, p, k_tok, v_tok, out, tok, levels, tri, state):
    nc = k.nc
    H4 = range(GDN_H)
    bufs = ["x", "xt", "z", "am", "a", "pt", "exp_r", "dec_t", "kend", "bv", "qdec", "r", "u"]
    w = [{n: k.big[:, EVEN_WORK + 512 * (13 * d + i):EVEN_WORK + 512 * (13 * d + i + 1)]
          .rearrange("p (h n) -> p h n", h=GDN_H) for i, n in enumerate(bufs)} for d in range(2)]
    bank = [[k.bank[4 * d + n][:, :].rearrange("p (h n) -> p h n", h=GDN_H) for n in range(4)] for d in range(2)]
    order = [[0, 1, 2, 3], [1, 0, 3, 2]]
    steps = [(i, d, order[d][i]) for i in range(NCHUNK) for d in range(2)]
    with stage(k, "delta", "mats", "exp_r", "clamped", "decays", "qk_ready", "pool", "masked", "z_made", "z_copied",
               "deltas", "grown", "ks", "rhs", "u_made", "u_copied", "out_made", "s_made", "out_added",
               "s_done", "chain") as (block, s):

        def cols(c):
            return slice(c * P, (c + 1) * P)

        @block.tensor
        def _(pe):
            for i in range(NCHUNK):
                for d in range(2):
                    n, c, b = 2 * i + d, order[d][i], bank[d]
                    at_least(pe, s.out_added, n - 1)
                    for h in H4:
                        nc.tensor.matmul(b[0][:, h, :], tok["g"][:, c, 4 * d + h:4 * d + h + 1].broadcast_to([P, P]),
                                         tri[:, d * P:(d + 1) * P], start=True, stop=True)
                    for h in H4:
                        nc.tensor.matmul(b[1][:, h, :], p[:, 4 + h, cols(c)], p[:, 4 + h, cols(c)],
                                         start=True, stop=True)
                    for h in H4:
                        last = nc.tensor.matmul(b[2][:, h, :], p[:, 4 + h, cols(c)], p[:, h, cols(c)],
                                                start=True, stop=True)
                    last.then_inc(s.mats, 1)
                for lev in range(LEVELS):
                    for d in range(2):
                        m = (2 * i + d) * LEVELS + lev
                        pe.wait_ge(s.masked, (i * LEVELS + lev) * 2 + d + 1)
                        pe.wait_ge(s.grown, (i * (LEVELS + 1) + lev) * 2 + d + 1)
                        for h in H4:
                            last = nc.tensor.matmul(bank[d][0][:, h, :], w[d]["am"][:, h, :], w[d]["xt"][:, h, :],
                                                    start=True, stop=True)
                        last.then_inc(s.z_made, 1)
                    for d in range(2):
                        pe.wait_ge(s.z_copied, (i * LEVELS + lev) * 2 + d + 1)
                        for h in H4:
                            last = nc.tensor.matmul(bank[d][1][:, h, :], w[d]["x"][:, h, :], w[d]["z"][:, h, :],
                                                    start=True, stop=True)
                        if lev < LEVELS - 1:
                            for h in H4:
                                last = nc.tensor.matmul(bank[d][2][:, h, :], w[d]["z"][:, h, :], w[d]["x"][:, h, :],
                                                        start=True, stop=True)
                        last.then_inc(s.deltas, 1)
                for d in range(2):
                    n, c = 2 * i + d, order[d][i]
                    at_least(pe, s.s_done, n - 1)
                    for h in H4:
                        last = nc.tensor.matmul(bank[d][0][:, h, :], p[:, 4 + h, cols(c)], state[d][:, h, :],
                                                start=True, stop=True)
                    last.then_inc(s.ks, 1)
                for d in range(2):
                    n, c = 2 * i + d, order[d][i]
                    pe.wait_ge(s.rhs, n + 1)
                    pe.wait_ge(s.grown, (i * (LEVELS + 1) + LEVELS) * 2 + d + 1)
                    for h in H4:
                        last = nc.tensor.matmul(bank[d][1][:, h, :], w[d]["xt"][:, h, :], w[d]["r"][:, h, :],
                                                start=True, stop=True)
                    last.then_inc(s.u_made, 1)
                for d in range(2):
                    n, c = 2 * i + d, order[d][i]
                    pe.wait_ge(s.u_copied, n + 1)
                    pe.wait_ge(s.pool, n + 1)
                    pe.wait_ge(s.qk_ready, n + 1)
                    for h in H4:
                        nc.tensor.matmul(bank[d][2][:, h, :], state[d][:, h, :], w[d]["qdec"][:, h, :],
                                         start=True, stop=False)
                        last = nc.tensor.matmul(bank[d][2][:, h, :], w[d]["u"][:, h, :], w[d]["pt"][:, h, :],
                                                start=False, stop=True)
                    last.then_inc(s.out_made, 1)
                    for h in H4:
                        last = nc.tensor.matmul(bank[d][3][:, h, :], w[d]["kend"][:, h, :], w[d]["u"][:, h, :],
                                                start=True, stop=True)
                    last.then_inc(s.s_made, 1)

        @block.scalar
        def _(act):
            for i in range(NCHUNK):
                for d in range(2):
                    n = 2 * i + d
                    act.wait_ge(s.clamped, n + 1)
                    at_least(act, s.pool, n - 1)
                    nc.scalar.activation(w[d]["exp_r"], bank[d][0], ACT.Exp).then_inc(s.exp_r, 1)
                for d in range(2):
                    nc.scalar.activation(w[d]["a"], w[d]["a"], ACT.Exp, scale=-1.0)
                    nc.scalar.activation(w[d]["dec_t"], w[d]["dec_t"], ACT.Exp).then_inc(s.decays, 1)
                for lev in range(LEVELS):
                    for d in range(2):
                        m = (i * LEVELS + lev) * 2 + d
                        act.wait_ge(s.z_made, m + 1)
                        at_least(act, s.deltas, m - 1)
                        nc.scalar.activation(w[d]["z"], bank[d][0], ACT.Copy).then_inc(s.z_copied, 1)
                for d in range(2):
                    n = 2 * i + d
                    act.wait_ge(s.u_made, n + 1)
                    at_least(act, s.s_made, n - 1)
                    nc.scalar.activation(w[d]["u"], bank[d][1], ACT.Copy).then_inc(s.u_copied, 1)

        @block.gpsimd
        def _(pool):
            for i, d, c in steps:
                n = 2 * i + d
                at_least(pool, s.s_made, n - 1)
                at_least(pool, s.rhs, n - 1)
                for h in H4:
                    nc.gpsimd.tensor_scalar(w[d]["kend"][:, h, :], k_tok[:, c, h * P:(h + 1) * P],
                                            tok["k_end"][:, c, 4 * d + h:4 * d + h + 1], None, ALU.mult)
                    nc.gpsimd.tensor_scalar(w[d]["bv"][:, h, :], v_tok[:, c, h * P:(h + 1) * P],
                                            tok["beta"][:, c, 4 * d + h:4 * d + h + 1], None, ALU.mult)
                pool.wait_ge(s.exp_r, n + 1)
                nc.gpsimd.tensor_tensor(w[d]["qdec"], p[:, 0:GDN_H, cols(c)], w[d]["exp_r"],
                                        ALU.mult).then_inc(s.pool, 1)

        @block.vector
        def _(dve):
            chain = Chain(dve, s.chain)
            for i in range(NCHUNK):
                for d in range(2):
                    n, c, b, q = 2 * i + d, order[d][i], bank[d], w[d]
                    dve.wait_ge(s.mats, n + 1)
                    at_least(dve, s.out_made, n - 1)
                    chain.add(nc.vector.tensor_copy(q["x"], k.ident.unsqueeze(1).broadcast_to([P, GDN_H, P])))
                    nc.vector.tensor_copy(q["xt"], k.ident.unsqueeze(1).broadcast_to([P, GDN_H, P])).then_inc(s.grown, 1)
                    for h in H4:
                        gc = tok["gc"][:, c, 4 * d + h:4 * d + h + 1]
                        nc.vector.tensor_scalar(q["a"][:, h, :], b[0][:, h, :], gc, 0.0, ALU.subtract, ALU.max)
                        ins = nc.vector.tensor_scalar(q["dec_t"][:, h, :], b[0][:, h, :], gc, 0.0,
                                                      ALU.subtract, ALU.min)
                    ins.then_inc(s.clamped, 1)
                for d in range(2):
                    n, c, b, q = 2 * i + d, order[d][i], bank[d], w[d]
                    dve.wait_ge(s.decays, n + 1)
                    for h in H4:
                        chain.add(nc.vector.scalar_tensor_tensor(
                            q["a"][:, h, :], b[1][:, h, :], tok["beta"][:, c, 4 * d + h:4 * d + h + 1],
                            q["a"][:, h, :], ALU.mult, ALU.mult))
                    chain.link(nc.vector.tensor_tensor(q["pt"], b[2], q["dec_t"], ALU.mult))
                    nc.vector.tensor_tensor(q["pt"], q["pt"],
                                            tri[:, d * P:(d + 1) * P].unsqueeze(1).broadcast_to([P, GDN_H, P]),
                                            ALU.mult).then_inc(s.qk_ready, 1)
                for lev in range(LEVELS):
                    for d in range(2):
                        m, q = (i * LEVELS + lev) * 2 + d, w[d]
                        at_least(dve, s.z_made, m - 1)
                        mask = levels[:, d * LEVELS + lev, :].unsqueeze(1).broadcast_to([P, GDN_H, P])
                        nc.vector.tensor_tensor(q["am"], q["a"], mask, ALU.mult).then_inc(s.masked, 1)
                    for d in range(2):
                        m, q = (i * LEVELS + lev) * 2 + d, w[d]
                        dve.wait_ge(s.deltas, m + 1)
                        dve.wait_ge(s.grown, (i * (LEVELS + 1) + lev) * 2 + d + 1)
                        if lev < LEVELS - 1:
                            nc.vector.tensor_tensor(q["x"], q["x"], bank[d][2], ALU.subtract)
                        nc.vector.tensor_tensor(q["xt"], q["xt"], bank[d][1], ALU.subtract).then_inc(s.grown, 1)
                for d in range(2):
                    n, c, q = 2 * i + d, order[d][i], w[d]
                    dve.wait_ge(s.ks, n + 1)
                    dve.wait_ge(s.pool, n + 1)
                    for h in H4:
                        ins = nc.vector.scalar_tensor_tensor(
                            q["r"][:, h, :], bank[d][0][:, h, :], tok["nbeg"][:, c, 4 * d + h:4 * d + h + 1],
                            q["bv"][:, h, :], ALU.mult, ALU.add)
                    ins.then_inc(s.rhs, 1)
                for d in range(2):
                    n, c = 2 * i + d, order[d][i]
                    dve.wait_ge(s.out_made, n + 1)
                    dve.wait_ge(s.out_added, n) if n else None
                    o = out[:, :, cols(c)]
                    nc.vector.tensor_tensor(o, o, bank[d][2], ALU.add).then_inc(s.out_added, 1)
                    dve.wait_ge(s.s_made, n + 1)
                    at_least(dve, s.s_done, n - 1)
                    for h in H4:
                        ins = nc.vector.scalar_tensor_tensor(
                            state[d][:, h, :], state[d][:, h, :], tok["s_end"][:, c, 4 * d + h:4 * d + h + 1],
                            bank[d][3][:, h, :], ALU.mult, ALU.add)
                    ins.then_inc(s.s_done, 1)


def odd_mixer(k, w_in, w_uq, w_ukv, w_out, then):
    nc = k.nc
    at = [0]

    def take(tiles, t):
        v = k.view(at[0], tiles, t)
        at[0] += tiles * t
        return v

    p, cq, ckv = take(6, T2), take(3, L), take(2, T2)
    q, kv, v_tok, y = take(12, L), take(16, T2), take(NCHUNK, 1024), take(8, L)
    linear(k, "mla_in", w_in, DT, T2, lambda kk, u: k.h[:, kk, :],
           lambda u, bank: nc.scalar.activation(tile_of(p, u), bank[:, 0:T2], ACT.Copy), engine="scalar",
           then=lambda sp: w_uq.prime(sp))
    norm(k, "q_norm", lambda i: p[:, i, TOK:T2], lambda i: cq[:, i, :], 3, L, 384,
         gain=lambda i: [((0, L), k.v("mla_q_g", i, 1))])
    norm(k, "kv_norm", lambda i: p[:, 3 + i, :], lambda i: ckv[:, i, :], 2, T2, 256,
         gain=lambda i: [((0, T2), k.v("mla_kv_g", i, 1))])
    q2 = q.rearrange("p (u s) t -> p u (s t)", s=2)
    linear(k, "mla_q", w_uq, 3, L, lambda kk, u: cq[:, kk, :],
           lambda u, bank: nc.scalar.activation(tile_of(q2, u), bank[:, 0:T2], ACT.Copy), engine="scalar",
           then=lambda sp: w_ukv.prime(sp))
    linear(k, "mla_kv", w_ukv, 2, T2, lambda kk, u: ckv[:, kk, :],
           lambda u, bank: nc.scalar.activation(tile_of(kv, u), bank[:, 0:T2], ACT.Copy), engine="scalar",
           then=lambda sp: w_out.prime(sp))

    rot, cos, sin = k.aux[:, 0:P], k.aux[:, 512:512 + L], k.aux[:, 768:768 + L]
    tmp = k.aux[:, 1024:1024 + 5 * L].rearrange("p (n t) -> p n t", t=L)
    roped = [q[:, 8 + j, :] for j in range(4)] + [p[:, 5, TOK:T2]]
    with stage(k, "rope", "tables", "turned", "chain") as (block, s):

        @block.sync
        def _(sp):
            for dst, name in ((rot, "rot"), (cos, "cos"), (sin, "sin")):
                sp.dma_start(dst, k.const(name)).then_inc(s.tables, 16)

        @block.tensor
        def _(pe):
            pe.wait_ge(s.tables, 48)
            for j, x in enumerate(roped):
                nc.tensor.matmul(k.bank[j][:, 0:L], rot, x, start=True, stop=True).then_inc(s.turned, 1)

        @block.vector
        def _(dve):
            chain = Chain(dve, s.chain)
            dve.wait_ge(s.tables, 48)
            for j, x in enumerate(roped):
                dve.wait_ge(s.turned, j + 1)
                chain.add(nc.vector.tensor_tensor(tmp[:, j, :], k.bank[j][:, 0:L], sin, ALU.mult))
                chain.link(nc.vector.tensor_tensor(x, x, cos, ALU.mult))
                nc.vector.tensor_tensor(x, x, tmp[:, j, :], ALU.add)

    transposes(k, "mla_v", [(kv[:, 8 + h, c * P:(c + 1) * P], v_tok[:, c, h * P:(h + 1) * P])
                            for c in range(NCHUNK) for h in range(HEADS)])
    units = []
    for h in range(HEADS):
        rows = slice(64 * (h % 2), 64 * (h % 2) + 64)
        for qt in range(2):
            cols = slice(qt * P, (qt + 1) * P)
            units.append(Unit(
                q=[q[:, h, cols], q[rows, 8 + h // 2, cols]], k=[kv[:, h, :], p[rows, 5, :]], keys=T2,
                v=[v_tok[:, c, h * P:(h + 1) * P] for c in range(NCHUNK)], bias=None, base=0, dv=P,
                out=y[:, h, cols]))
    attention(k, "mla", units, (128 + 64) ** -0.5, at[0])
    chain_residual(k, "mla_out", w_out, lambda kk, u: y[:, kk, :], lambda u: k.mod_at(1, 2, u, 1), then)


def chain_residual(k, name, w, rhs, gate, then):
    nc = k.nc

    def add(u, bank):
        for j in range(2):
            x = tile_of(k.x, u * 2 + j, TOK, T2)
            ins = nc.vector.scalar_tensor_tensor(x, bank[:, j * L:(j + 1) * L], gate(u * 2 + j), x,
                                                 ALU.mult, ALU.add)
        return ins

    linear(k, name, w, DT, L, rhs, add, then=then)


def experts(k, layer, first, w_q, then):
    nc = k.nc
    h = k.h[:, :, first:first + L]
    half = first // L
    qy = k.view(0, 16, L)
    keys = k.view(4096, 16, KEYS)
    score = [k.view(6144 + 2048 * i, 16, KEYS) for i in range(2)]
    q2 = k.big[:, 0:4096].rearrange("p (u n) -> p u n", n=512)
    linear(k, "peer_q", w_q, DT, L, lambda kk, u: h[:, kk, :],
           lambda u, bank: nc.scalar.activation(tile_of(q2, u), bank[:, 0:T2], ACT.Copy), engine="scalar")

    with stage(k, "peer_scores", "keys", "scored", "copied") as (block, s):

        @block.sync
        def _(sp):
            sp.dma_start(keys[:, :, :], k.io["sub_keys"][layer].rearrange("p (n m) -> p n m", n=16)).then_inc(s.keys, 16)

        @block.tensor
        def _(pe):
            pe.wait_ge(s.keys, 16)
            for tt in range(2):
                for g in range(4):
                    for j in range(4):
                        last = nc.tensor.matmul(k.bank[4 * tt + g][:, j * P:(j + 1) * P],
                                                qy[:, 4 * g + j, tt * P:(tt + 1) * P], keys[:, 4 * g + j, :],
                                                start=True, stop=True)
                    last.then_inc(s.scored, 1)

        @block.scalar
        def _(act):
            for tt in range(2):
                for g in range(4):
                    act.wait_ge(s.scored, 4 * tt + g + 1)
                    nc.scalar.activation(score[tt][:, 4 * g:4 * g + 4, :],
                                         k.bank[4 * tt + g][:, :].rearrange("p (n m) -> p n m", n=4), ACT.Copy)

    i1_t, i2_t, gate_t = (k.aux[:, L * j:L * (j + 1)] for j in range(3))
    routing(k, score, (i1_t, i2_t, gate_t))

    table = k.big[:, :].rearrange("p (i t) -> p i t", t=L)
    row_hot = [k.aux[:, 768 + 1024 * b:1280 + 1024 * b].rearrange("p (q n) -> p q n", n=KEYS) for b in range(2)]
    col_hot = [k.aux[:, 1280 + 1024 * b:1792 + 1024 * b].rearrange("p (q n) -> p q n", n=KEYS) for b in range(2)]
    u_loaded = [nc.alloc_semaphore(f"u_loaded{b}_{k.stage_no}") for b in range(2)]
    v_loaded = [nc.alloc_semaphore(f"v_loaded{b}_{k.stage_no}") for b in range(2)]
    u_dram, v_dram = k.io["experts_u"], k.io["experts_v"]
    e0 = layer * KEYS

    def expert_row(dram, i):
        if isinstance(i, int):
            return dram[e0 + i]
        return dram[bass.ds(i + e0, 1)].rearrange("o p n -> (o p) n")

    def load_u(sp, i, b):
        sp.dma_start(k.ring[:, 2 * b, 0:D], expert_row(u_dram, i)).then_inc(u_loaded[b], 16)

    def load_v(sp, i, b):
        sp.dma_start(k.ring[:, 2 * b + 1, 0:D], expert_row(v_dram, i)).then_inc(v_loaded[b], 16)

    with stage(k, "table", "rows", "columns", "spread", "stored") as (block, s):

        @block.sync
        def _(sp):
            for b in range(2):
                load_u(sp, b, b)
                load_v(sp, b, b)

        @block.vector
        def _(dve):
            iota = k.iota.unsqueeze(1).broadcast_to([P, 4, KEYS])

            def group(r, b):
                g = r * 2 + b
                at_least(dve, s.spread, (r - 1) * 2 + (b + 1))
                tok = bass.ds(g * 4, 4)

                def spread(t):
                    return t[:, tok].unsqueeze(2).broadcast_to([P, 4, KEYS])

                nc.vector.tensor_tensor(col_hot[b], iota, spread(i2_t), ALU.is_equal).then_inc(s.columns, 1)
                nc.vector.tensor_tensor(row_hot[b], iota, spread(i1_t), ALU.is_equal).then_inc(s.rows, 1)
                dve.wait_ge(s.columns, g * 2 + 1)
                nc.vector.tensor_tensor(col_hot[b], col_hot[b], spread(gate_t), ALU.mult).then_inc(s.columns, 1)

            repeat(dve, L // 8, lambda r: [group(r, b) for b in range(2)])

        @block.tensor
        def _(pe):
            def group(r, b):
                g = r * 2 + b
                pe.wait_ge(s.columns, g * 2 + 2)
                pe.wait_ge(s.rows, g + 1)
                at_least(pe, s.stored, (r - 1) * 2 + (b + 1))
                for j in range(4):
                    last = nc.tensor.matmul(k.bank[b][:, j * P:(j + 1) * P], col_hot[b][:, j, :],
                                            row_hot[b][:, j, :], start=True, stop=True)
                last.then_inc(s.spread, 1)

            repeat(pe, L // 8, lambda r: [group(r, b) for b in range(2)])

        @block.scalar
        def _(act):
            def group(r, b):
                g = r * 2 + b
                act.wait_ge(s.spread, g + 1)
                nc.scalar.activation(table[:, :, bass.ds(g * 4, 4)],
                                     k.bank[b][:, :].rearrange("p (q n) -> p n q", n=KEYS),
                                     ACT.Copy).then_inc(s.stored, 1)

            repeat(act, L // 8, lambda r: [group(r, b) for b in range(2)])

    act_buf = [k.aux[:, 768 + L * b:768 + L * (b + 1)] for b in range(2)]
    gated = [k.aux[:, 1280 + L * b:1280 + L * (b + 1)] for b in range(2)]
    with stage(k, "experts", "hidden", "activated", "gated", "mixed", "added") as (block, s):

        @block.sync
        def _(sp):
            def refill(r):
                for b in range(2):
                    i = r * 2 + b
                    sp.wait_ge(s.hidden, i + 1)
                    load_u(sp, i + 2, b)
                    sp.wait_ge(s.mixed, i + 1)
                    load_v(sp, i + 2, b)

            repeat(sp, KEYS // 2 - 1, refill)
            if then is not None:
                sp.wait_ge(s.mixed, KEYS)
                then(sp)

        @block.tensor
        def _(pe):
            def hidden(r, b):
                pe.wait_ge(u_loaded[b], r * 16 + 16)
                at_least(pe, s.activated, (r - 1) * 2 + (b + 1))
                for kk in range(DT):
                    last = nc.tensor.matmul(k.bank[4 + b][:, 0:L], k.ring[:, 2 * b, kk * P:(kk + 1) * P],
                                            h[:, kk, :], start=kk == 0, stop=kk == DT - 1)
                last.then_inc(s.hidden, 1)

            def mix(r, b, first=False, last_group=False):
                pe.wait_ge(v_loaded[b], r * 16 + 16)
                pe.wait_ge(s.gated, r * 2 + b + 1)
                for dt in range(DT):
                    ins = nc.tensor.matmul(k.bank[dt // 2][:, (dt % 2) * L:(dt % 2 + 1) * L],
                                           k.ring[:, 2 * b + 1, dt * P:(dt + 1) * P], gated[b],
                                           start=first and dt % 2 == 0, stop=last_group, skip_group_check=True)
                ins.then_inc(s.mixed, 1)

            hidden(0, 0)
            hidden(0, 1)
            mix(0, 0, first=True)
            hidden(1, 0)
            mix(0, 1)

            with pe.Fori(1, KEYS // 2 - 1) as r:
                hidden(r, 1)
                mix(r, 0)
                hidden(r + 1, 0)
                mix(r, 1)
            end = KEYS // 2 - 1
            hidden(end, 1)
            mix(end, 0)
            mix(end, 1, last_group=True)

        @block.scalar
        def _(act):
            def group(r, b):
                i = r * 2 + b
                act.wait_ge(s.hidden, i + 1)
                at_least(act, s.gated, (r - 1) * 2 + (b + 1))
                nc.scalar.activation(act_buf[b], k.bank[4 + b][:, 0:L], ACT.Gelu).then_inc(s.activated, 1)

            repeat(act, KEYS // 2, lambda r: [group(r, b) for b in range(2)])

        @block.vector
        def _(dve):
            def group(r, b):
                i = r * 2 + b
                dve.wait_ge(s.activated, i + 1)
                at_least(dve, s.mixed, (r - 1) * 2 + (b + 1))
                nc.vector.tensor_tensor(gated[b], act_buf[b], tile_of(table, i), ALU.mult).then_inc(s.gated, 1)

            repeat(dve, KEYS // 2, lambda r: [group(r, b) for b in range(2)])
            dve.wait_ge(s.mixed, KEYS)
            for dt in range(DT):
                x = k.x[:, dt, first:first + L]
                nc.vector.scalar_tensor_tensor(x, k.bank[dt // 2][:, (dt % 2) * L:(dt % 2 + 1) * L],
                                               k.mod_at(layer, 5, dt, half), x, ALU.mult, ALU.add)
    k.spent += u_loaded + v_loaded


def routing(k, score, results):
    nc = k.nc
    at = [10240]

    def take(n, dt=F32):
        at[0] += n
        v = k.big[:, at[0] - n:at[0]]
        return v if dt == F32 else v.bitcast(dt)

    top, top_i = take(512), take(512, U32)
    top_f = take(512)
    best, best_i = take(256), take(256, U32)
    hi_i, lo_i = take(256, U32), take(256, U32)
    hi_f, lo_f = take(256), take(256)
    comb = take(2 * 2048)
    hot = take(2048)
    row, col, gate = take(256), take(256), take(256)
    small = take(64)
    three = lambda v, n, m: v.rearrange("p (n m) -> p n m", m=m)
    with stage(k, "routing", "chain", "tops", "exps", "ready", "turned") as (block, s):

        @block.vector
        def _(dve):
            chain = Chain(dve, s.chain)

            def best16(values, out, out_i, jobs):
                for half in range(2):
                    sl = slice(8 * half, 8 * half + 8)
                    for j in jobs:
                        chain.add(nc.vector.max(out=out(j)[:, sl], in_=values(j)))
                    chain.settle()
                    for j in jobs:
                        chain.add(nc.vector.max_index(out=out_i(j)[:, sl], in_max=out(j)[:, sl], in_values=values(j)))
                    if half == 0:
                        chain.settle()
                        for j in jobs:
                            chain.add(nc.vector.match_replace(out=values(j), in_to_replace=out(j)[:, sl],
                                                              in_values=values(j), imm_value=-3e38))
                        chain.settle()

            jobs = [(tt, n) for tt in range(2) for n in range(16)]
            sub = lambda v: lambda j: v[:, 256 * j[0] + 16 * j[1]:256 * j[0] + 16 * j[1] + 16]
            best16(lambda j: score[j[0]][:, j[1], :], sub(top), sub(top_i), jobs)
            chain.settle()
            chain.link(nc.vector.tensor_copy(top_f, top_i))
            heads = [(tt, n) for tt in range(2) for n in range(HEADS)]
            pair = three(comb, 16, 256)
            for tt, n in heads:
                a = top[:, 256 * tt + 32 * n:256 * tt + 32 * n + 16]
                b = top[:, 256 * tt + 32 * n + 16:256 * tt + 32 * n + 32]
                chain.add(nc.vector.tensor_tensor(
                    pair[:, 8 * tt + n, :].rearrange("p (i j) -> p i j", j=16),
                    a.unsqueeze(2).broadcast_to([P, 16, 16]), b.unsqueeze(1).broadcast_to([P, 16, 16]), ALU.add))
            chain.settle()
            sub8 = lambda v: lambda j: v[:, 128 * j[0] + 16 * j[1]:128 * j[0] + 16 * j[1] + 16]
            best16(lambda j: pair[:, 8 * j[0] + j[1], :], sub8(best), sub8(best_i), heads)
            chain.settle()
            b3, g3 = three(best, 16, 16), three(gate, 16, 16)
            nc.vector.tensor_tensor(g3, b3, b3[:, :, 0:1].broadcast_to([P, 16, 16]), ALU.subtract).then_inc(s.tops, 1)
            chain.add(nc.vector.tensor_single_scalar(hi_i, best_i, 4, ALU.logical_shift_right))
            chain.add(nc.vector.tensor_single_scalar(lo_i, best_i, 15, ALU.bitwise_and))
            chain.settle()
            chain.add(nc.vector.tensor_copy(hi_f, hi_i))
            chain.add(nc.vector.tensor_copy(lo_f, lo_i))
            chain.settle()
            iota16 = k.iota[:, 0:16].unsqueeze(1).broadcast_to([P, P, 16])
            h3 = three(hot, 128, 16)
            h4 = hot.rearrange("p (h r j) -> p h r j", r=16, j=16)
            for tt in range(2):
                for rank, first, dst in ((hi_f, 0, row), (lo_f, 16, col)):
                    chain.link(nc.vector.tensor_tensor(
                        h3, rank[:, 128 * tt:128 * tt + 128].unsqueeze(2).broadcast_to([P, P, 16]), iota16, ALU.is_equal))
                    ids = top_f[:, 256 * tt:256 * tt + 256].rearrange("p (h n) -> p h n", n=32)[:, :, first:first + 16]
                    chain.link(nc.vector.tensor_tensor(h4, h4, ids.unsqueeze(2).broadcast_to([P, HEADS, 16, 16]), ALU.mult))
                    chain.link(nc.vector.tensor_reduce(dst[:, 128 * tt:128 * tt + 128], h3, AX.X, ALU.add))
            dve.wait_ge(s.exps, 1)
            chain.link(nc.vector.tensor_reduce(small[:, 0:16], g3, AX.X, ALU.add))
            chain.link(nc.vector.reciprocal(small[:, 16:32], small[:, 0:16]))
            nc.vector.tensor_tensor(g3, g3, small[:, 16:32].unsqueeze(2).broadcast_to([P, 16, 16]),
                                    ALU.mult).then_inc(s.ready, 1)
            dve.wait_ge(s.turned, 1)
            for n, dst in enumerate(results):
                nc.vector.tensor_copy(dst, k.bank[n][:, 0:L])

        @block.scalar
        def _(act):
            act.wait_ge(s.tops, 1)
            nc.scalar.activation(gate, gate, ACT.Exp).then_inc(s.exps, 1)

        @block.tensor
        def _(pe):
            pe.wait_ge(s.ready, 1)
            for n, src in enumerate((row, col, gate)):
                for tt in range(2):
                    last = nc.tensor.transpose(k.bank[n][:, tt * P:(tt + 1) * P], src[:, tt * P:(tt + 1) * P], k.ident)
            last.then_inc(s.turned, 1)


def swiglu(k, layer, which, w_up, w_down, then):
    nc = k.nc
    a = k.view(0, FF_T, L)
    y = k.view(FF_T * L, DT, L)
    gate = [k.aux[:, 1024 + L * b:1024 + L * (b + 1)] for b in range(2)]
    pre, post = f"ffn{which}_pre", f"ffn{which}_post"
    norm(k, "ffn_norm", lambda i: k.x[:, i, TOK:T2], lambda i: k.h[:, i, 0:L], DT, L, D,
         gain=lambda i: [((0, L), k.v(pre, 8 * layer + i, 1))])
    per, body = 2, 2
    rounds = FF_T // body
    w = w_up
    with stage(k, "ffn_up", "chunk_used", "silu", "product") as (block, s):

        @block.sync
        def _(sp):
            if w.loaded is None:
                w.prime(sp)

            def refill(r):
                for slot in range(RING):
                    sp.wait_ge(s.chunk_used, r * RING + (slot + 1))
                    w.load(sp, r * RING + (slot + RING), slot)

            repeat(sp, w.chunks // RING - 1, refill)
            sp.wait_ge(s.chunk_used, w.chunks)
            w_down.prime(sp)

        @block.tensor
        def _(pe):
            def unit(r, b):
                at_least(pe, s.product, (r - 1) * body + (b + 1))
                for c in range(per):
                    slot = b * per + c
                    pe.wait_ge(w.loaded[slot], r * 16 + 16)
                    for kk in range(DT):
                        last = nc.tensor.matmul(k.bank[b][:, c * L:(c + 1) * L], k.ring[:, slot, kk * P:(kk + 1) * P],
                                                k.h[:, kk, 0:L], start=kk == 0, stop=kk == DT - 1)
                    last.then_inc(s.chunk_used, 1)

            repeat(pe, rounds, lambda r: [unit(r, b) for b in range(body)])

        @block.scalar
        def _(act):
            def unit(r, b):
                act.wait_ge(s.chunk_used, r * RING + (2 * b + 2))
                at_least(act, s.product, (r - 1) * body + (b + 1))
                nc.scalar.activation(gate[b], k.bank[b][:, 0:L], ACT.Silu).then_inc(s.silu, 1)

            repeat(act, rounds, lambda r: [unit(r, b) for b in range(body)])

        @block.vector
        def _(dve):
            def unit(r, b):
                dve.wait_ge(s.silu, r * body + (b + 1))
                nc.vector.tensor_tensor(tile_of(a, r * body + b), gate[b], k.bank[b][:, L:T2],
                                        ALU.mult).then_inc(s.product, 1)

            repeat(dve, rounds, lambda r: [unit(r, b) for b in range(body)])

    w_up.retire()
    y2 = k.big[:, FF_T * L:(FF_T + DT) * L].rearrange("p (u n) -> p u n", n=T2)
    linear(k, "ffn_down", w_down, FF_T, L, lambda kk, u: a[:, kk, :],
           lambda u, bank: nc.scalar.activation(tile_of(y2, u), bank[:, 0:T2], ACT.Copy), engine="scalar", then=then)
    norm(k, "ffn_post", lambda i: y[:, i, :], lambda i: k.h[:, i, 0:L], DT, L, D,
         gain=lambda i: [((0, L), k.v(post, 8 * layer + i, 1))],
         residual=(lambda i: k.x[:, i, TOK:T2], 0.5))


def conv_pool_mixer(k, layer, w, then):
    nc = k.nc
    z = k.view(0, 48, L)
    z2 = k.big[:, 0:48 * L].rearrange("p (u n) -> p u n", n=T2)
    base = 48 * L
    ya, pool, m1, m2 = (k.view(base + 8 * L * i, DT, L) for i in range(4))
    spare = k.view(base + 32 * L, DT, L)
    counts = k.view(base + 40 * L, 4, L)
    norm(k, "mix_norm", lambda i: k.x[:, i, TOK:T2], lambda i: k.h[:, i, 0:L], DT, L, D,
         gain=lambda i: [((0, L), k.v("mix_pre", 8 * layer + i, 1))])
    linear(k, "mix_in", w.w_in, DT, L, lambda kk, u: k.h[:, kk, 0:L],
           lambda u, bank: nc.scalar.activation(tile_of(z2, u), bank[:, 0:T2], ACT.Copy), engine="scalar",
           then=lambda sp: w.w_pg.prime(sp))
    taps = k.v("conv_w_2", 24 * layer, 24).rearrange("p (t j) -> p t j", j=3)
    with stage(k, "conv_pool", "counts", "chain", "gates") as (block, s):

        @block.sync
        def _(sp):
            sp.dma_start(counts[:, :, :], k.const("inv_count").rearrange("p (n t) -> p n t", t=L)).then_inc(s.counts, 16)

        @block.scalar
        def _(act):
            for i in range(16):
                nc.scalar.activation(z[:, 32 + i, :], z[:, 32 + i, :], ACT.Sigmoid,
                                     bias=k.v("b_gate", 16 * layer + i, 1)).then_inc(s.gates, 1)

        @block.vector
        def _(dve):
            chain = Chain(dve, s.chain)
            u = m1
            chain.link(nc.vector.tensor_tensor(u[:, :, :], z[:, 8:16, :], z[:, 16:24, :], ALU.mult))
            for i in range(DT):
                chain.add(nc.vector.tensor_scalar(ya[:, i, :], u[:, i, :], taps[:, i, 2:3], None, ALU.mult))
            chain.settle()
            for j in (1, 0):
                o = 2 - j
                for i in range(DT):
                    chain.add(nc.vector.scalar_tensor_tensor(ya[:, i, o:L], u[:, i, 0:L - o], taps[:, i, j:j + 1],
                                                             ya[:, i, o:L], ALU.mult, ALU.add))
                chain.settle()
            chain.add(nc.vector.tensor_tensor(ya[:, :, :], ya[:, :, :], z[:, 0:8, :], ALU.mult))
            src = z[:, 24:32, :]
            dst = m2
            for g in range(4):
                lo = 2 * g
                o = 1 << g
                chain.add(nc.vector.tensor_tensor(dst[:, lo:8, o:L], src[:, lo:8, o:L], src[:, lo:8, 0:L - o], ALU.add))
                chain.link(nc.vector.tensor_copy(dst[:, lo:8, 0:o], src[:, lo:8, 0:o]))
                if g == 0:
                    dve.wait_ge(s.counts, 16)
                part = pool[:, lo:lo + 2, :]
                chain.link(nc.vector.tensor_tensor(part, dst[:, lo:lo + 2, :],
                                                   counts[:, g:g + 1, :].broadcast_to([P, 2, L]), ALU.mult))
                chain.link(nc.vector.tensor_tensor(part, part, z[:, 24 + lo:26 + lo, :], ALU.subtract))
                src, dst = dst, (spare if dst is m2 else m2)

    pooled = m1
    def pool_bias(u, bank):
        for j in range(2):
            n = 2 * u + j
            ins = nc.vector.tensor_scalar(pooled[:, n, :], bank[:, j * L:(j + 1) * L],
                                          k.v("b_pool", 8 * layer + n, 1), k.v("pool_scale", 8 * layer + n, 1),
                                          ALU.add, ALU.mult)
        return ins

    with stage(k, "pool_group", "made", "stored") as (block, s):

        @block.tensor
        def _(pe):
            for g in range(4):
                for j in range(2):
                    for kk in range(2):
                        if kk == 0 and j == 0:
                            pe.wait_ge(w.w_pg.loaded[g], 16)
                        last = nc.tensor.matmul(k.bank[g][:, j * L:(j + 1) * L],
                                                k.ring[:, g, (2 * j + kk) * P:(2 * j + kk + 1) * P],
                                                pool[:, 2 * g + kk, :], start=kk == 0, stop=kk == 1)
                last.then_inc(s.made, 1)

        @block.vector
        def _(dve):
            for g in range(4):
                dve.wait_ge(s.made, g + 1)
                pool_bias(g, k.bank[g])

        @block.sync
        def _(sp):
            sp.wait_ge(s.made, 4)
            w.w_conv_out.prime(sp)

    w.w_pg.retire()

    def branch(dst, gate):
        def run(u, bank):
            for j in range(2):
                ins = nc.vector.tensor_tensor(tile_of(dst, u * 2 + j), bank[:, j * L:(j + 1) * L],
                                              tile_of(z, u * 2 + j + gate), ALU.mult)
            return ins
        return run

    linear(k, "conv_out", w.w_conv_out, DT, L, lambda kk, u: ya[:, kk, :], branch(m2, 32),
           then=lambda sp: w.w_pool_out.prime(sp))
    linear(k, "pool_out", w.w_pool_out, DT, L, lambda kk, u: pooled[:, kk, :], branch(spare, 40),
           then=lambda sp: w.w_o.prime(sp))
    with stage(k, "mix_add") as (block, s):

        @block.vector
        def _(dve):
            nc.vector.tensor_tensor(m2[:, :, :], m2[:, :, :], spare[:, :, :], ALU.add)

    y2 = k.big[:, base:base + 8 * L].rearrange("p (u n) -> p u n", n=T2)
    linear(k, "mix_o", w.w_o, DT, L, lambda kk, u: m2[:, kk, :],
           lambda u, bank: nc.scalar.activation(tile_of(y2, u), bank[:, 0:T2], ACT.Copy), engine="scalar", then=then)
    norm(k, "mix_post", lambda i: ya[:, i, :], lambda i: k.h[:, i, 0:L], DT, L, D,
         gain=lambda i: [((0, L), k.v("mix_post", 8 * layer + i, 1))],
         residual=(lambda i: k.x[:, i, TOK:T2], 1.0))


def build_program(nc, io, out, stop=None):
    k = Core()
    k.nc, k.io, k.stage_no, k.spent = nc, io, 0, []
    k.big = nc.alloc_sbuf_tensor("big", [P, BIG], F32)
    k.x = nc.alloc_sbuf_tensor("x_all", [P, DT, T2], F32)
    k.h = nc.alloc_sbuf_tensor("h_all", [P, DT, T2], F32)
    k.ring = nc.alloc_sbuf_tensor("weight_ring", [P, RING, SLOT], F32)
    k.mod = nc.alloc_sbuf_tensor("modulation", [P, 96, 2], F32)
    vec = nc.alloc_sbuf_tensor("vectors", [P, N_VEC], F32)
    res = nc.alloc_sbuf_tensor("resident_consts", [P, N_RESIDENT], F32)
    k.aux = nc.alloc_sbuf_tensor("aux", [P, AUX], F32)
    k.bank = [nc.alloc_psum_tensor(f"bank{i}", [P, 512], F32) for i in range(8)]

    def resident(name):
        a, n = CONST_AT[name]
        return res[:, a:a + n]

    k.ident, k.ones, k.iota, k.eps = (resident(n) for n in ("ident", "ones", "iota", "eps"))
    k.v = lambda name, off=0, n=None: vec[:, VEC_AT[name] + off:VEC_AT[name] + off + (n or dict(VECTORS)[name])]
    k.const = lambda name: io["consts"][:, CONST_AT[name][0]:CONST_AT[name][0] + CONST_AT[name][1]]
    k.view = lambda at, tiles, t: k.big[:, at:at + tiles * t].rearrange("p (n t) -> p n t", t=t)

    def mod_at(layer, part, tile, half):
        n = tile + (48 * layer + 8 * part)
        if isinstance(n, int):
            return k.mod[:, n, half:half + 1]
        return k.mod[:, bass.ds(n, 1), half:half + 1].rearrange("p o t -> p (o t)")

    k.mod_at = mod_at

    def weights(name, kc, chunks, first=0):
        w = Weights(k, name, kc, chunks)
        prime = w.prime
        w.prime = lambda sp: prime(sp, first)
        return w

    w_ada = weights("w_ada", 8, 96)
    w_even_in = weights("w_even_in", 8, 29)
    w_even_out = weights("w_even_out", 8, 8)
    load(k, "inputs", [(k.x[:, :, CTX:L], io["ctx"]), (k.x[:, :, TOK:T2], io["x"]), (vec[:, :], io["vectors"]),
                       (res[:, :], io["consts"][:, 0:N_RESIDENT])], more=w_ada.prime)
    condition(k, w_ada)

    def finish(src):
        with stage(k, "store", "stored") as (block, s):
            @block.sync
            def _(sp):
                sp.dma_start(out, src).then_inc(s.stored, 16)
                sp.wait_ge(s.stored, 16)

    mod_norm(k, 0, False, (0, T2), prime=w_even_in.prime)
    if stop == "norm1":
        return finish(k.h[:, :, :])
    even_mixer(k, w_even_in, w_even_out, None)
    if stop == "even":
        return finish(k.x[:, :, :])
    mod_norm(k, 0, True, (0, T2))
    for first in (CTX, TOK):
        experts(k, 0, first, weights("w_peer_q", 8, 16, 0), None)
    if stop == "peer0":
        return finish(k.x[:, :, :])
    mod_norm(k, 1, False, (0, T2))
    odd_mixer(k, weights("w_mla_in", 8, 6), weights("w_mla_uq", 3, 12), weights("w_mla_ukv", 2, 16),
              weights("w_mla_out", 8, 8), None)
    if stop == "mla":
        return finish(k.x[:, :, :])
    mod_norm(k, 1, True, (L, T2))
    experts(k, 1, TOK, weights("w_peer_q", 8, 16, 16), None)
    norm(k, "final", lambda i: k.x[:, i, TOK:T2], lambda i: k.x[:, i, TOK:T2], DT, L, D,
         gain=lambda i: [((0, L), k.v("final_g", i, 1))], squares=lambda i: k.h[:, i, 0:L])
    if stop == "first":
        return finish(k.x[:, :, :])
    for layer in range(2):
        swiglu(k, layer, 1, weights("w_up1", 8, 44, 44 * layer), weights("w_down1", 11, 16, 16 * layer), None)
        if stop == "ffn1" and layer == 0:
            return finish(k.x[:, :, :])
        conv_pool_mixer(k, layer, MixerWeights(
            w_in=weights("w_in2", 8, 48, 48 * layer), w_pg=weights("w_pg", 4, 4, 4 * layer),
            w_conv_out=weights("w_conv_out", 8, 8, 8 * layer), w_pool_out=weights("w_pool_out", 8, 8, 8 * layer),
            w_o=weights("w_o", 8, 8, 8 * layer)), None)
        if stop == "mix" and layer == 0:
            return finish(k.x[:, :, :])
        swiglu(k, layer, 2, weights("w_up2", 8, 44, 44 * layer), weights("w_down2", 11, 16, 16 * layer), None)
    finish(k.x[:, :, TOK:T2])


def tiled(w, kc):
    kdim, n = w.shape
    if n % P:
        w = np.concatenate([w, np.zeros((kdim, P - n % P), w.dtype)], 1)
    kt, nt = kdim // P, w.shape[1] // P
    return np.ascontiguousarray(w.reshape(kt // kc, kc, P, nt, P).transpose(3, 0, 2, 1, 4)).reshape(
        nt * (kt // kc), P, kc * P)


def columns(v):
    return np.ascontiguousarray(v.reshape(-1, P).T)


def lay_out(a):
    a = {n: np.asarray(v) for n, v in a.items()}
    io = {}
    feature_major = lambda t: np.ascontiguousarray(t.reshape(L, DT, P).transpose(2, 1, 0))
    io["x"], io["ctx"] = feature_major(a["x"][0]), feature_major(a["ctx"][0])
    per_partition = lambda v: np.broadcast_to(v.reshape(1, -1), (P, v.size))
    taps = lambda w: np.ascontiguousarray(w.reshape(w.shape[0], -1, P).transpose(2, 1, 0)).reshape(P, -1)
    vectors = {
        "c": columns(a["c"]), "c_ctx": columns(a["c_ctx"]), "ada_b": columns(a["ada_b"]),
        "norm1_g": columns(a["norm1_g"]), "norm2_g": columns(a["norm2_g"]), "final_g": columns(a["final_g"]),
        "conv_w": taps(a["even_conv_w"][0]), "gdn_norm_g": columns(a["gdn_norm_g"]),
        "a_log": per_partition(a["gdn_a_log"]), "dt_bias": per_partition(a["gdn_dt_bias"]),
        "mla_q_g": columns(a["mla_q_g"]), "mla_kv_g": columns(a["mla_kv_g"]),
        "ffn1_pre": columns(a["ffn1_pre_2"]), "ffn1_post": columns(a["ffn1_post_2"]),
        "mix_pre": columns(a["mix_pre_2"]), "mix_post": columns(a["mix_post_2"]),
        "ffn2_pre": columns(a["ffn2_pre_2"]), "ffn2_post": columns(a["ffn2_post_2"]),
        "b_gate": columns(a["b_gate_2"]),
        "conv_w_2": np.concatenate([taps(a["conv_w_2"][i]) for i in range(2)], 1),
        "b_pool": columns(a["b_pool_group_2"]), "pool_scale": columns(a["pool_scale_2"]),
    }
    io["vectors"] = np.ascontiguousarray(np.concatenate([vectors[n] for n, _ in VECTORS], 1))
    io["consts"] = CONSTS
    io["w_ada"] = np.concatenate([tiled(a["ada_w"][i], 8) for i in range(2)])
    io["w_even_in"] = tiled(a["even_w_in"][0], 8)
    io["w_even_out"] = tiled(a["even_w_out"][0], 8)
    rpb = a["na_rpb"][0]
    wide = np.pad(rpb, ((0, 0), (0, 0), (GRID_W - 16, GRID_W - 16)))
    by_col = np.stack([wide[:, :, GRID_W - 1 - c:2 * GRID_W - 1 - c] for c in range(GRID_W)], 2)
    rows = L // GRID_W
    bias = np.stack([by_col[:, 7 - r:7 - r + rows] for r in range(rows)], 1)
    io["na_bias"] = np.ascontiguousarray(bias.transpose(0, 1, 3, 2, 4)).reshape(HEADS, 2, P, L)
    w = a["mla_w_in"][0]
    io["w_mla_in"] = tiled(np.concatenate([w, w[:, 640:704]], 1), 8)
    w = a["mla_w_uq"][0].reshape(384, HEADS, 192)
    io["w_mla_uq"] = tiled(np.concatenate([w[:, :, :128].reshape(384, -1), w[:, :, 128:].reshape(384, -1)], 1), 3)
    w = a["mla_w_ukv"][0].reshape(256, HEADS, 256)
    io["w_mla_ukv"] = tiled(np.concatenate([w[:, :, :128].reshape(256, -1), w[:, :, 128:].reshape(256, -1)], 1), 2)
    io["w_mla_out"] = tiled(a["mla_w_out"][0], 8)
    both = lambda name, kc: np.concatenate([tiled(a[name][i], kc) for i in range(2)])
    io["w_peer_q"] = both("peer_w_q", 8)
    io["sub_keys"] = np.ascontiguousarray(a["peer_sub_keys"].reshape(2, 16, KEYS, P).transpose(0, 3, 1, 2)).reshape(2, P, -1)
    io["experts_u"] = np.ascontiguousarray(
        a["peer_u"].reshape(2, KEYS, KEYS, DT, P).transpose(0, 1, 4, 3, 2)).reshape(2 * KEYS, P, D)
    io["experts_v"] = np.ascontiguousarray(a["peer_v"].reshape(2 * KEYS, KEYS, D))
    for which in (1, 2):
        w = a[f"ffn{which}_w_gate_up_2"].reshape(2, D, 2, FF_T, P).transpose(0, 1, 3, 2, 4).reshape(2, D, 2 * D_FF)
        io[f"w_up{which}"] = np.concatenate([tiled(w[i], 8) for i in range(2)])
        io[f"w_down{which}"] = both(f"ffn{which}_w_down_2", 11)
    io["w_in2"] = both("w_in_2", 8)
    w = a["w_pool_group_2"].reshape(2, 4, 2, P, 2, P)
    io["w_pg"] = np.ascontiguousarray(w.transpose(0, 1, 3, 4, 2, 5)).reshape(8, P, 4 * P)
    io["w_conv_out"], io["w_pool_out"], io["w_o"] = both("w_conv_out_2", 8), both("w_pool_out_2", 8), both("w_o_2", 8)
    return io


def kernel(**inputs):
    import concourse.bacc as bacc
    from concourse.bass_utils import run_bass_kernel_spmd

    io = lay_out(inputs)
    nc = bacc.Bacc("TRN2", target_bir_lowering=False, num_devices=1)
    arrays = {f"in_{n}": v for n, v in io.items()}
    aps = {n: nc.dram_tensor(f"in_{n}", v.shape, mybir.dt.from_np(v.dtype), kind="ExternalInput").ap()
           for n, v in io.items()}
    out = nc.dram_tensor("out_features", (P, DT, L), F32, kind="ExternalOutput").ap()
    build_program(nc, aps, out)
    r = run_bass_kernel_spmd(nc, [arrays], core_ids=[0])
    y = np.asarray(r.results[0]["out_features"])
    return np.ascontiguousarray(y.transpose(2, 1, 0)).reshape(1, L, D)
```

```python
from collections import namedtuple
from contextlib import contextmanager

import numpy as np

import concourse.bass as bass
from concourse import mybir

F32 = mybir.dt.float32
BF16 = mybir.dt.bfloat16
U32 = mybir.dt.uint32
ACT = mybir.ActivationFunctionType
ALU = mybir.AluOpType
AX = mybir.AxisListType

P = 128
L = 256
T2 = 2 * L
D = 1024
DT = D // P
EPS = 1e-6
GRID_W = 64
HEADS = 8
NA_DH = 64
GDN_H = 4
CHUNK = 128
NCHUNK = T2 // CHUNK
LEVELS = 7
KEYS = 128
TOPK = 16
D_FF = 2816
FF_T = D_FF // P
POOL_WINDOWS = (2, 4, 8, 16)
RING = 4
SLOT = 11 * P
BIG = 32768
AUX = 5120
CTX, TOK = 0, L
PARTS = 24576
SCRATCH = 28672

VECTORS = [
    ("c", 8), ("c_ctx", 8), ("ada_b", 96), ("norm1_g", 16), ("norm2_g", 16), ("final_g", 8),
    ("conv_w", 60), ("gdn_norm_g", 1), ("a_log", 8), ("dt_bias", 8), ("mla_q_g", 3), ("mla_kv_g", 2),
    ("ffn1_pre", 16), ("ffn1_post", 16), ("mix_pre", 16), ("mix_post", 16), ("ffn2_pre", 16),
    ("ffn2_post", 16), ("b_gate", 32), ("conv_w_2", 48), ("b_pool", 16), ("pool_scale", 16),
]
VEC_AT = {}
_n = 0
for _name, _w in VECTORS:
    VEC_AT[_name] = _n
    _n += _w
N_VEC = _n

def constants():
    i = np.arange(P)
    parts = {}
    parts["ident"] = np.eye(P)
    parts["ones"] = np.ones((P, P))
    parts["iota"] = np.broadcast_to(i, (P, P))
    parts["eps"] = np.broadcast_to(np.array([EPS, 4 * EPS, P * EPS, 1.0]), (P, 4))
    resident = sum(v.shape[1] for v in parts.values())
    parts["tri"] = np.concatenate([i[:, None] <= i[None, :], i[:, None] >= i[None, :]], 1)
    masks = []
    for d in range(2):
        for lev in range(LEVELS):
            b = 1 << lev
            m = (i[:, None] // (2 * b) == i[None, :] // (2 * b)) & (i[:, None] % (2 * b) >= b) & (i[None, :] % (2 * b) < b)
            masks.append(m if d == 0 else m.T)
    parts["levels"] = np.concatenate(masks, 1)
    start = np.clip(i % GRID_W - 8, 0, GRID_W - 16)[:, None]
    col = (np.arange(L) % GRID_W)[None, :]
    parts["window"] = np.where((col >= start) & (col < start + 16), 0.0, -1e30)
    inv = (10000.0 ** (-np.arange(0, 32, 2, dtype=np.float32) / 32)).astype(np.float32)
    t = np.arange(L)
    ar = (t // GRID_W).astype(np.float32)[:, None] * inv
    ac = (t % GRID_W).astype(np.float32)[:, None] * inv
    ang = np.concatenate([ar, ar, ac, ac], -1).T
    parts["cos"] = np.concatenate([np.cos(ang)] * 2, 0)
    parts["sin"] = np.concatenate([np.sin(ang)] * 2, 0)
    rot = np.zeros((P, P))
    for base in (0, 64):
        for blk in (0, 32):
            for j in range(16):
                rot[base + blk + 16 + j, base + blk + j] = -1.0
                rot[base + blk + j, base + blk + 16 + j] = 1.0
    parts["rot"] = rot
    parts["inv_count"] = np.concatenate(
        [np.broadcast_to(1.0 / np.minimum(t + 1, w), (P, L)) for w in POOL_WINDOWS], 1)
    at, n = {}, 0
    for name, v in parts.items():
        at[name] = (n, v.shape[1])
        n += v.shape[1]
    return np.ascontiguousarray(np.concatenate(list(parts.values()), 1).astype(np.float32)), at, resident


CONSTS, CONST_AT, N_RESIDENT = constants()


Unit = namedtuple("Unit", "q k keys v bias base dv out")
MixerWeights = namedtuple("MixerWeights", "w_in w_pg w_conv_out w_pool_out w_o")


class Core:
    pass


def at_least(eng, sem, value):
    if isinstance(value, int) and value <= 0:
        return
    eng.wait_ge(sem, value)


class Chain:

    def __init__(self, eng, sem):
        self.eng, self.sem, self.n = eng, sem, 0

    def add(self, ins):
        ins.then_inc(self.sem, 1)
        self.n += 1

    def settle(self):
        at_least(self.eng, self.sem, self.n)

    def link(self, ins):
        self.add(ins)
        self.settle()


@contextmanager
def stage(k, name, *signals):
    nc = k.nc
    k.stage_no += 1
    s = namedtuple("Signals", signals)(*(nc.alloc_semaphore(f"{name}_{k.stage_no}_{n}") for n in signals))
    with nc.Block() as block:
        yield block, s
    k.spent += list(s)
    if len(k.spent) > 130:
        nc.clear_and_free_semaphores(k.spent)
        nc.all_engine_barrier()
        k.spent = []


class Weights:

    def __init__(self, k, name, kc, chunks):
        self.k, self.dram, self.kc, self.chunks, self.name = k, k.io[name], kc, chunks, name
        self.loaded = None

    def load(self, sp, q, s):
        dst = self.k.ring[:, s, 0:self.kc * P]
        if isinstance(q, int):
            src = self.dram[self.first + q]
        else:
            src = self.dram[bass.ds(q + self.first, 1)].rearrange("o p n -> (o p) n")
        sp.dma_start(dst, src).then_inc(self.loaded[s], 16)

    def retire(self):
        self.k.spent += self.loaded

    def prime(self, sp, first=0):
        k = self.k
        self.first = first
        self.loaded = [k.nc.alloc_semaphore(f"{self.name}_loaded{s}_{k.stage_no}") for s in range(RING)]
        for q in range(min(RING, self.chunks)):
            self.load(sp, q, q)


def repeat(eng, rounds, body):
    if rounds > 0:
        body(0)
    if rounds > 1:
        with eng.Fori(1, rounds) as r:
            body(r)


def linear(k, name, w, kt, t, rhs, epilogue, engine="vector", then=None):
    nc = k.nc
    per_tile = kt // w.kc
    tiles = 1 if t == 2 else 512 // t
    c_unit = per_tile * tiles
    units = w.chunks // c_unit
    body = max(2, RING // c_unit)
    rounds, tail = divmod(units, body)
    assert units * c_unit == w.chunks and (body * c_unit) % RING == 0
    with stage(k, name, "chunk_used", "bank_free") as (block, s):

        @block.sync
        def _(sp):
            if w.loaded is None:
                w.prime(sp)

            def refill(r):
                for slot in range(RING):
                    sp.wait_ge(s.chunk_used, r * RING + (slot + 1))
                    w.load(sp, r * RING + (slot + RING), slot)

            full, rest = divmod(max(w.chunks - RING, 0), RING)
            repeat(sp, full, refill)
            for slot in range(rest):
                sp.wait_ge(s.chunk_used, full * RING + slot + 1)
                w.load(sp, full * RING + slot + RING, slot)
            if then is not None:
                sp.wait_ge(s.chunk_used, w.chunks)
                then(sp)

        @block.tensor
        def _(pe):
            def unit(r, b):
                at_least(pe, s.bank_free, (r - 1) * body + (b + 1))
                for c in range(c_unit):
                    at = b * c_unit + c
                    slot = at % RING
                    tile, part = divmod(c, per_tile)
                    pe.wait_ge(w.loaded[slot], r * (16 * body * c_unit // RING) + 16 * (at // RING + 1))
                    for j in range(w.kc):
                        kk = part * w.kc + j
                        last = nc.tensor.matmul(k.bank[b][:, tile * t:(tile + 1) * t],
                                                k.ring[:, slot, j * P:(j + 1) * P],
                                                rhs(kk, r * body + b),
                                                start=kk == 0, stop=kk == kt - 1)
                    last.then_inc(s.chunk_used, 1)

            repeat(pe, rounds, lambda r: [unit(r, b) for b in range(body)])
            for b in range(tail):
                unit(rounds, b)

        def empty(eng):
            def unit(r, b):
                eng.wait_ge(s.chunk_used, r * (body * c_unit) + (b + 1) * c_unit)
                epilogue(r * body + b, k.bank[b]).then_inc(s.bank_free, 1)

            repeat(eng, rounds, lambda r: [unit(r, b) for b in range(body)])
            for b in range(tail):
                unit(rounds, b)

        if engine == "vector":
            @block.vector
            def _(dve):
                empty(dve)
        else:
            @block.scalar
            def _(act):
                empty(act)
    w.retire()


def linear3(k, name, w, kt, t, rhs, epilogue, engine="vector", then=None, body=None, lag=1):
    nc = k.nc
    per_tile = kt // w.kc
    c_unit = per_tile * (512 // t)
    units = w.chunks // c_unit
    body = body or min(4, max(2, units))
    rounds, tail = divmod(units, body)
    size = w.kc * P
    assert units * c_unit == w.chunks and (body * c_unit) % RING == 0
    hi, lo = k.parts(SLOT)
    with stage(k, name, "high", "low", "chunk_used", "bank_free") as (block, s):

        @block.sync
        def _(sp):
            if w.loaded is None:
                w.prime(sp)

            def refill(r):
                for slot in range(RING):
                    sp.wait_ge(s.low, r * RING + (slot + 1))
                    w.load(sp, r * RING + (slot + RING), slot)

            full, rest = divmod(max(w.chunks - RING, 0), RING)
            repeat(sp, full, refill)
            for slot in range(rest):
                sp.wait_ge(s.low, full * RING + slot + 1)
                w.load(sp, full * RING + slot + RING, slot)
            if then is not None:
                sp.wait_ge(s.low, w.chunks)
                then(sp)

        @block.tensor
        def _(pe):
            def unit(r, b):
                at_least(pe, s.bank_free, (r - 1) * body + (b + 1))
                for c in range(c_unit):
                    at = b * c_unit + c
                    slot = at % RING
                    tile, part = divmod(c, per_tile)
                    pe.wait_ge(s.low, r * (body * c_unit) + (at + 1))
                    for j in range(w.kc):
                        kk = part * w.kc + j
                        xh, xl = rhs(kk)
                        dst = k.bank[b][:, tile * t:(tile + 1) * t]
                        cols = slice(j * P, (j + 1) * P)
                        nc.tensor.matmul(dst, hi[slot][:, cols], xh, start=kk == 0, stop=False)
                        nc.tensor.matmul(dst, hi[slot][:, cols], xl, start=False, stop=False)
                        last = nc.tensor.matmul(dst, lo[slot][:, cols], xh, start=False, stop=kk == kt - 1)
                    last.then_inc(s.chunk_used, 1)

            repeat(pe, rounds, lambda r: [unit(r, b) for b in range(body)])
            for b in range(tail):
                unit(rounds, b)

        def split(eng, r, b):
            for c in range(c_unit):
                at = b * c_unit + c
                slot = at % RING
                if eng is nc.scalar:
                    eng.wait_ge(w.loaded[slot], r * (16 * body * c_unit // RING) + 16 * (at // RING + 1))
                    at_least(eng, s.chunk_used, r * (body * c_unit) + (at + 1 - RING))
                    nc.scalar.activation(hi[slot][:, 0:size], k.ring[:, slot, 0:size], ACT.Copy).then_inc(s.high, 1)
                else:
                    eng.wait_ge(s.high, r * (body * c_unit) + (at + 1))
                    nc.vector.tensor_tensor(lo[slot][:, 0:size], k.ring[:, slot, 0:size], hi[slot][:, 0:size],
                                            ALU.subtract).then_inc(s.low, 1)

        def empty(eng, r, b):
            eng.wait_ge(s.chunk_used, r * (body * c_unit) + (b + 1) * c_unit)
            epilogue(r * body + b, k.bank[b]).then_inc(s.bank_free, 1)

        def program(eng, empties):
            def round_(r):
                for b in range(body):
                    split(eng, r, b)
                    if empties and not (isinstance(r, int) and r == 0 and b == 0):
                        empty(eng, r if b else r - 1, b - 1 if b else body - 1)

            repeat(eng, rounds, round_)
            for b in range(tail):
                split(eng, rounds, b)
                if empties:
                    empty(eng, rounds if b else rounds - 1, b - 1 if b else body - 1)
            if empties:
                empty(eng, rounds if tail else rounds - 1, tail - 1 if tail else body - 1)

        @block.vector
        def _(dve):
            program(nc.vector, engine == "vector")

        @block.scalar
        def _(act):
            program(nc.scalar, engine == "scalar")
    w.retire()


def split(k, name, src, tiles, t, hi=None, lo=None, then=None):
    nc = k.nc
    hi = k.hh if hi is None else hi
    lo = k.hl if lo is None else lo
    with stage(k, name, "high") as (block, s):

        @block.scalar
        def _(act):
            for i in range(tiles):
                nc.scalar.activation(hi[:, i, 0:t], src[:, i, :], ACT.Copy).then_inc(s.high, 1)

        @block.vector
        def _(dve):
            for i in range(tiles):
                dve.wait_ge(s.high, i + 1)
                nc.vector.tensor_tensor(lo[:, i, 0:t], src[:, i, :], hi[:, i, 0:t], ALU.subtract)


def tile_of(buf, n, lo=0, hi=None):
    hi = buf.shape[2] if hi is None else hi
    if isinstance(n, int):
        return buf[:, n, lo:hi]
    return buf[:, bass.ds(n, 1), lo:hi].rearrange("p o t -> p (o t)")


def load(k, name, pairs, more=None):
    with stage(k, name, "arrived") as (block, s):

        @block.sync
        def _(sp):
            for dst, src in pairs:
                sp.dma_start(dst, src).then_inc(s.arrived, 16)
            sp.wait_ge(s.arrived, 16 * len(pairs))
            if more is not None:
                more(sp)


def condition(k, w):
    nc = k.nc
    c2 = k.aux[:, 0:16].rearrange("p (t j) -> p t j", j=2)
    rows = k.big[0:2, 0:96 * P]
    units = 96 * P // 512
    n_sq = 4
    with stage(k, "ada", "silu", "chunk_used", "row_out", "turned") as (block, s):

        @block.sync
        def _(sp):
            def refill(r):
                for slot in range(RING):
                    sp.wait_ge(s.chunk_used, r * RING + (slot + 1))
                    w.load(sp, r * RING + (slot + RING), slot)

            repeat(sp, w.chunks // RING - 1, refill)

        @block.scalar
        def _(act):
            nc.scalar.activation(c2[:, :, 0], k.v("c_ctx"), ACT.Silu)
            nc.scalar.activation(c2[:, :, 1], k.v("c"), ACT.Silu).then_inc(s.silu, 1)

        @block.tensor
        def _(pe):
            pe.wait_ge(s.silu, 1)

            def round_(r):
                for b in range(2):
                    at_least(pe, s.row_out, (r - 1) * 2 + (b + 1))
                    for c in range(n_sq):
                        pe.wait_ge(w.loaded[c], r * 32 + 16 * (b + 1))
                        for j in range(2):
                            kk = 2 * c + j
                            last = nc.tensor.matmul(k.bank[b][0:2, :], c2[:, kk, :],
                                                    k.ring[:, c, 512 * j:512 * (j + 1)],
                                                    start=kk == 0, stop=kk == DT - 1)
                        last.then_inc(s.chunk_used, 1)

            repeat(pe, units // 2, round_)
            pe.wait_ge(s.row_out, units)
            for n in range(96):
                last = nc.tensor.matmul(k.bank[2][:, 2 * n:2 * n + 2], rows[:, n * P:(n + 1) * P],
                                        k.ident[0:2, 0:2], start=True, stop=True)
            last.then_inc(s.turned, 1)

        @block.vector
        def _(dve):
            def round_(r):
                for b in range(2):
                    u = r * 2 + b
                    dve.wait_ge(s.chunk_used, r * 8 + 4 * (b + 1))
                    nc.vector.tensor_copy(rows[:, bass.ds(u * 512, 512)], k.bank[b][0:2, :]).then_inc(s.row_out, 1)

            repeat(dve, units // 2, round_)
    w.retire()
    with stage(k, "ada_bias", "added") as (block, s):

        @block.vector
        def _(dve):
            chain = Chain(dve, s.added)
            turned = k.bank[2][:, 0:192].rearrange("p (n j) -> p n j", j=2)
            chain.link(nc.vector.tensor_tensor(k.mod[:, :, :], turned,
                                               k.v("ada_b").unsqueeze(2).broadcast_to([P, 96, 2]), ALU.add))
            for layer in range(2):
                for part, gain in ((1, "norm1_g"), (4, "norm2_g")):
                    sc = k.mod[:, 48 * layer + 8 * part:48 * layer + 8 * part + 8, :]
                    g = k.v(gain, 8 * layer, 8).unsqueeze(2).broadcast_to([P, 8, 2])
                    chain.add(nc.vector.scalar_tensor_tensor(sc, sc, 1.0, g, ALU.add, ALU.mult))


def norm(k, name, src, dst, tiles, t, dim, gain, shift=None, residual=None, prime=None, squares=None,
         halves=None):
    nc = k.nc
    squares = squares or dst
    factor = residual[1] if residual else 1.0
    std, rstd = k.aux[:, 0:t], k.aux[:, 512:512 + t]
    stat = k.bank[7][:, 0:t]
    eps = {1.0: 0, 0.5: 1}[factor]
    with stage(k, name, "sq_a", "sq_v", "summed", "rooted", "scaled", "done", "shifted", "high") as (block, s):

        @block.scalar
        def _(act):
            for i in range(0, tiles, 2):
                nc.scalar.activation(squares(i), src(i), ACT.Square).then_inc(s.sq_a, 1)
            act.wait_ge(s.summed, 1)
            nc.scalar.activation(std, stat, ACT.Sqrt, bias=k.eps[:, eps:eps + 1],
                                 scale=1.0 / (dim * factor * factor)).then_inc(s.rooted, 1)
            if shift is not None:
                for i in range(tiles):
                    act.wait_ge(s.scaled, i + 1)
                    for (lo, hi), sh in shift(i):
                        nc.scalar.activation(dst(i)[:, lo:hi], dst(i)[:, lo:hi], ACT.Identity,
                                             bias=sh).then_inc(s.shifted, 1)
                    if halves is not None:
                        act.wait_ge(s.shifted, (i + 1) * len(shift(0)))
                        nc.scalar.activation(halves(i)[0], dst(i), ACT.Copy).then_inc(s.high, 1)
            elif halves is not None:
                for i in range(tiles):
                    act.wait_ge(s.scaled, i + 1)
                    nc.scalar.activation(halves(i)[0], dst(i), ACT.Copy).then_inc(s.high, 1)

        @block.vector
        def _(dve):
            for i in range(1, tiles, 2):
                nc.vector.tensor_tensor(squares(i), src(i), src(i), ALU.mult).then_inc(s.sq_v, 1)
            dve.wait_ge(s.rooted, 1)
            nc.vector.reciprocal(rstd, std).then_inc(s.done, 1)
            dve.wait_ge(s.done, 1)
            for i in range(tiles):
                parts = gain(i)
                for n, ((lo, hi), g) in enumerate(parts):
                    ins = nc.vector.scalar_tensor_tensor(dst(i)[:, lo:hi], src(i)[:, lo:hi], g,
                                                         rstd[:, lo:hi], ALU.mult, ALU.mult)
                    if n == len(parts) - 1:
                        ins.then_inc(s.scaled, 1)
            if halves is not None:
                for i in range(tiles):
                    dve.wait_ge(s.high, i + 1)
                    nc.vector.tensor_tensor(halves(i)[1], dst(i), halves(i)[0], ALU.subtract)
            if residual is not None:
                for i in range(tiles):
                    dve.wait_ge(s.scaled, i + 1)
                    x = residual[0](i)
                    nc.vector.tensor_tensor(x, x, dst(i), ALU.add)

        @block.tensor
        def _(pe):
            for i in range(tiles):
                pe.wait_ge(s.sq_v if i % 2 else s.sq_a, i // 2 + 1)
                last = nc.tensor.matmul(stat, k.ones, squares(i), start=i == 0, stop=i == tiles - 1)
            last.then_inc(s.summed, 1)

        @block.sync
        def _(sp):
            if prime is not None:
                prime(sp)


def halves_of_h(k, t):
    return lambda i: (k.hh[:, i, 0:t], k.hl[:, i, 0:t])


def mod_norm(k, layer, second, halves, prime=None, whole=False):
    part = 3 if second else 0
    lo, hi = halves
    base = 48 * layer + 8 * part

    def scalars(chunk):
        def at(i):
            out = []
            if lo < L:
                out.append(((0, L), k.mod[:, base + 8 * chunk + i, 0:1]))
            if hi > L:
                out.append(((L - lo, hi - lo), k.mod[:, base + 8 * chunk + i, 1:2]))
            return out
        return at

    if whole:
        norm(k, "mod_norm", lambda i: k.x[:, i, lo:hi], lambda i: k.h[:, i, lo:hi], DT, hi - lo, D,
             gain=scalars(1), shift=scalars(0), prime=prime)
    else:
        wide = k.view(SCRATCH, DT, hi - lo)
        norm(k, "mod_norm", lambda i: k.x[:, i, lo:hi], lambda i: wide[:, i, :], DT, hi - lo, D,
             gain=scalars(1), shift=scalars(0), prime=prime, halves=halves_of_h(k, hi - lo))


def transposes(k, name, jobs):
    nc = k.nc
    with stage(k, name, "turned", "copied") as (block, s):

        @block.tensor
        def _(pe):
            for n, (src, _) in enumerate(jobs):
                at_least(pe, s.copied, n - 3)
                nc.tensor.transpose(k.bank[n % 4][:, 0:P], src, k.ident).then_inc(s.turned, 1)

        @block.vector
        def _(dve):
            for n, (_, dst) in enumerate(jobs):
                dve.wait_ge(s.turned, n + 1)
                nc.vector.tensor_copy(dst, k.bank[n % 4][:, 0:P]).then_inc(s.copied, 1)


def attention(k, name, units, scale, scratch, prime=None):
    nc = k.nc
    at = [scratch]

    def take(n):
        at[0] += n
        return k.big[:, at[0] - n:at[0]]

    score = [take(512) for _ in range(2)]
    prob = [take(512) for _ in range(2)]
    prob_t = [take(512) for _ in range(2)]
    bias = [take(L) for _ in range(2)]
    stat = [take(8) for _ in range(2)]
    n_units = len(units)
    biased = units[0].bias is not None
    exp_scale = 1.0 if biased else scale
    with stage(k, name, "scored", "maxed", "expd", "normed", "turned", "probs_t", "mixed", "stored",
               "chain", "bias_0", "bias_1", "bias_ready") as (block, s):
        bias_loaded = [s.bias_0, s.bias_1]

        @block.sync
        def _(sp):
            if biased:
                for u, un in enumerate(units):
                    at_least(sp, s.maxed, u - 1)
                    sp.dma_start(bias[u % 2], un.bias).then_inc(bias_loaded[u % 2], 16)
            if prime is not None:
                prime(sp)

        @block.gpsimd
        def _(pool):
            if biased:
                for u in range(n_units):
                    pool.wait_ge(bias_loaded[u % 2], 16 * (u // 2 + 1))
                    nc.gpsimd.tensor_tensor(bias[u % 2], bias[u % 2], k.window, ALU.add).then_inc(s.bias_ready, 1)

        @block.tensor
        def _(pe):
            def scores(u):
                un = units[u]
                at_least(pe, s.expd, u - 1)
                for j, (q, key) in enumerate(zip(un.q, un.k)):
                    last = nc.tensor.matmul(k.bank[u % 2][:, 0:un.keys], q, key,
                                            start=j == 0, stop=j == len(un.q) - 1)
                last.then_inc(s.scored, 1)

            def mix(u):
                un = units[u]
                pe.wait_ge(s.probs_t, u + 1)
                at_least(pe, s.stored, u - 1)
                n = un.keys // P
                for j in range(n):
                    last = nc.tensor.matmul(k.bank[4 + u % 2][un.base:un.base + un.dv, 0:P], un.v[j],
                                            prob_t[u % 2][:, j * P:(j + 1) * P], start=j == 0, stop=j == n - 1)
                last.then_inc(s.mixed, 1)

            scores(0)
            if n_units > 1:
                scores(1)
            for u in range(n_units):
                pe.wait_ge(s.normed, u + 1)
                at_least(pe, s.probs_t, u - 1)
                for j in range(units[u].keys // P):
                    last = nc.tensor.transpose(k.bank[2 + u % 2][:, j * P:(j + 1) * P],
                                               prob[u % 2][:, j * P:(j + 1) * P], k.ident)
                last.then_inc(s.turned, 1)
                if u >= 1:
                    mix(u - 1)
                if u + 2 < n_units:
                    scores(u + 2)
            mix(n_units - 1)

        @block.scalar
        def _(act):
            def expd(u):
                un = units[u]
                src = score[u % 2] if biased else k.bank[u % 2]
                act.wait_ge(s.maxed, u + 1)
                at_least(act, s.turned, u - 1)
                nc.scalar.activation(prob[u % 2][:, 0:un.keys], src[:, 0:un.keys], ACT.Exp, scale=exp_scale,
                                     bias=stat[u % 2][:, 1:2], accum_out=stat[u % 2][:, 2:3]).then_inc(s.expd, 1)

            def store(u):
                un = units[u]
                act.wait_ge(s.mixed, u + 1)
                nc.scalar.activation(un.out, k.bank[4 + u % 2][un.base:un.base + un.dv, 0:P],
                                     ACT.Copy).then_inc(s.stored, 1)

            expd(0)
            for u in range(n_units):
                if u + 1 < n_units:
                    expd(u + 1)
                n = units[u].keys
                act.wait_ge(s.turned, u + 1)
                at_least(act, s.mixed, u - 1)
                nc.scalar.activation(prob_t[u % 2][:, 0:n], k.bank[2 + u % 2][:, 0:n],
                                     ACT.Copy).then_inc(s.probs_t, 1)
                if u >= 1:
                    store(u - 1)
            store(n_units - 1)

        @block.vector
        def _(dve):
            chain = Chain(dve, s.chain)

            def maxima(u):
                un = units[u]
                bank, st = k.bank[u % 2], stat[u % 2]
                dve.wait_ge(s.scored, u + 1)
                at_least(dve, s.expd, u - 1)
                src = bank
                if biased:
                    dve.wait_ge(s.bias_ready, u + 1)
                    src = score[u % 2]
                    chain.add(nc.vector.tensor_scalar(src[:, 0:L], bank[:, 0:L], scale, None, ALU.mult))
                    chain.link(nc.vector.scalar_tensor_tensor(src[:, L:T2], bank[:, L:T2], scale, bias[u % 2],
                                                              ALU.mult, ALU.add))
                chain.link(nc.vector.reduce_max(st[:, 0:1], src[:, 0:un.keys], AX.X))
                nc.vector.tensor_scalar(st[:, 1:2], st[:, 0:1], -exp_scale, None, ALU.mult).then_inc(s.maxed, 1)

            maxima(0)
            for u in range(n_units):
                if u + 1 < n_units:
                    maxima(u + 1)
                st = stat[u % 2]
                dve.wait_ge(s.expd, u + 1)
                chain.link(nc.vector.reciprocal(st[:, 3:4], st[:, 2:3]))
                n = units[u].keys
                nc.vector.tensor_scalar(prob[u % 2][:, 0:n], prob[u % 2][:, 0:n], st[:, 3:4], None,
                                        ALU.mult).then_inc(s.normed, 1)


EVEN_P = 0
EVEN_Y = 29 * T2
EVEN_WORK = EVEN_Y + 8 * T2


def even_mixer(k, w_in, w_out, then):
    nc = k.nc
    p = k.view(EVEN_P, 29, T2)
    y = k.view(EVEN_Y, 8, T2)

    linear(k, "even_in", w_in, DT, T2, lambda kk, u: k.h[:, kk, :],
           lambda u, bank: nc.scalar.activation(tile_of(p, u), bank[:, 0:T2], ACT.Copy), engine="scalar",
           then=lambda sp: w_out.prime(sp))

    v_tok = k.view(EVEN_WORK, NCHUNK, 512)
    transposes(k, "na_v", [(p[:, 8 + f, c * P:(c + 1) * P], v_tok[:, c, f * P:(f + 1) * P])
                           for c in range(NCHUNK) for f in range(4)])
    load(k, "window", [(k.aux[:, 0:L], k.const("window"))])
    k.window = k.aux[:, 0:L]
    for first in (TOK, CTX):
        units = []
        for head in range(HEADS):
            base, tile = NA_DH * (head % 2), head // 2
            rows = slice(base, base + NA_DH)
            for qt in range(2):
                cols = slice(first + qt * P, first + (qt + 1) * P)
                keys = T2 if first == TOK else L
                units.append(Unit(
                    q=[p[rows, tile, cols]], k=[p[rows, 4 + tile, 0:keys]], keys=keys,
                    v=[v_tok[:, c, head * NA_DH:(head + 1) * NA_DH] for c in range(keys // P)],
                    bias=k.io["na_bias"][head, qt] if first == TOK else None,
                    base=base, dv=NA_DH, out=y[rows, tile, cols]))
        attention(k, "na", units, NA_DH ** -0.5, EVEN_WORK + NCHUNK * 512)

    gated_delta(k, p, y)

    def add_residual(u, bank):
        for half, lo in ((0, CTX), (1, TOK)):
            x = tile_of(k.x, u, lo, lo + L)
            ins = nc.vector.scalar_tensor_tensor(x, bank[:, lo:lo + L], k.mod_at(0, 2, u, half), x,
                                                 ALU.mult, ALU.add)
        return ins

    linear(k, "even_out", w_out, DT, T2, lambda kk, u: y[:, kk, :], add_residual, then=then)


def gated_delta(k, p, y):
    nc = k.nc
    conv_w = k.v("conv_w").rearrange("p (t j) -> p t j", j=5)
    with stage(k, "conv", "chain", "conved") as (block, s):

        @block.vector
        def _(dve):
            chain = Chain(dve, s.chain)
            for pair in range(6):
                for j in (2, 0, 1, 3, 4):
                    for t in (2 * pair, 2 * pair + 1):
                        src = p[:, 12 + t, :].rearrange("p (h n) -> p h n", h=2)
                        dst = p[:, t, :].rearrange("p (h n) -> p h n", h=2)
                        tap = conv_w[:, t, j:j + 1]
                        if j == 2:
                            ins = nc.vector.tensor_scalar(dst, src, tap, None, ALU.mult)
                        else:
                            o = j - 2
                            a, b = max(0, -o), L - max(0, o)
                            ins = nc.vector.scalar_tensor_tensor(dst[:, :, a:b], src[:, :, a + o:b + o], tap,
                                                                 dst[:, :, a:b], ALU.mult, ALU.add)
                        if j == 4:
                            ins.then_inc(s.conved, 1)
                        else:
                            chain.add(ins)
                    if j != 4:
                        chain.settle()

        @block.scalar
        def _(act):
            for t in range(12):
                act.wait_ge(s.conved, t + 1)
                nc.scalar.activation(p[:, t, :], p[:, t, :], ACT.Silu)

    sq = k.view(EVEN_WORK, 8, T2)
    root = k.view(EVEN_WORK + 8 * T2, 8, T2)
    with stage(k, "l2norm", "squared", "summed", "rooted", "inverted") as (block, s):

        @block.vector
        def _(dve):
            for t in range(8):
                nc.vector.tensor_tensor(sq[:, t, :], p[:, t, :], p[:, t, :], ALU.mult).then_inc(s.squared, 1)
            for t in range(8):
                dve.wait_ge(s.rooted, t + 1)
                nc.vector.reciprocal(root[:, t, :], root[:, t, :]).then_inc(s.inverted, 1)
            for t in range(8):
                dve.wait_ge(s.inverted, t + 1)
                nc.vector.tensor_tensor(p[:, t, :], p[:, t, :], root[:, t, :], ALU.mult)

        @block.tensor
        def _(pe):
            for t in range(8):
                pe.wait_ge(s.squared, t + 1)
                nc.tensor.matmul(k.bank[t][:, :], k.ones, sq[:, t, :], start=True, stop=True).then_inc(s.summed, 1)

        @block.scalar
        def _(act):
            for t in range(8):
                act.wait_ge(s.summed, t + 1)
                nc.scalar.activation(root[:, t, :], k.bank[t][:, :], ACT.Sqrt,
                                     bias=k.eps[:, 2:3] if t < 4 else k.eps[:, 0:1],
                                     scale=float(P) if t < 4 else 1.0).then_inc(s.rooted, 1)

    k_tok = k.view(12 * T2, NCHUNK, 512)
    v_tok = k.view(16 * T2, NCHUNK, 512)
    out = k.view(20 * T2, GDN_H, T2)
    gate_t = k.view(EVEN_WORK, NCHUNK, P)
    transposes(k, "gdn_turn",
               [(p[:, 28, c * P:(c + 1) * P], gate_t[:, c, :]) for c in range(NCHUNK)]
               + [(p[:, 4 + h, c * P:(c + 1) * P], k_tok[:, c, h * P:(h + 1) * P])
                  for c in range(NCHUNK) for h in range(GDN_H)]
               + [(p[:, 8 + h, c * P:(c + 1) * P], v_tok[:, c, h * P:(h + 1) * P])
                  for c in range(NCHUNK) for h in range(GDN_H)])

    names = ["a", "beta", "abs", "e", "g", "gc", "eg", "total", "k_end", "s_end", "nbeg"]
    tok = {n: k.aux[:, 32 * i:32 * (i + 1)].rearrange("p (c d) -> p c d", d=8) for i, n in enumerate(names)}
    levels = k.aux[:, 512:512 + 2 * LEVELS * P].rearrange("p (l n) -> p l n", n=P)
    tri = k.aux[:, 2304:2304 + 2 * P]
    state = [k.aux[:, 2560 + 512 * d:3072 + 512 * d].rearrange("p (h n) -> p h n", h=GDN_H) for d in range(2)]
    with stage(k, "gates", "tables", "a_ready", "act", "chain", "cumsum") as (block, s):

        @block.sync
        def _(sp):
            sp.dma_start(tri, k.const("tri")).then_inc(s.tables, 16)
            sp.dma_start(levels[:, :, :], k.const("levels").rearrange("p (l n) -> p l n", n=P)).then_inc(s.tables, 16)
            sp.wait_ge(s.tables, 32)

        @block.vector
        def _(dve):
            chain = Chain(dve, s.chain)
            for d in range(2):
                chain.add(nc.vector.tensor_copy(tok["a"][:, :, 4 * d:4 * d + 4], gate_t[:, :, 8 * d:8 * d + 4]))
            chain.settle()
            dt = k.v("dt_bias").unsqueeze(1).broadcast_to([P, NCHUNK, 8])
            nc.vector.tensor_tensor(tok["a"], tok["a"], dt, ALU.add).then_inc(s.a_ready, 1)
            dve.wait_ge(s.act, 6)
            dve.wait_ge(s.a_ready, 1)
            chain.link(nc.vector.scalar_tensor_tensor(tok["e"], tok["a"], 0.0, tok["e"], ALU.max, ALU.add))
            ea = k.aux[:, 384:392].unsqueeze(1).broadcast_to([P, NCHUNK, 8])
            chain.link(nc.vector.scalar_tensor_tensor(tok["g"], tok["e"], -1.0, ea, ALU.mult, ALU.mult))
            dve.wait_ge(s.cumsum, 1)
            sums = k.bank[0][:, 0:64]
            for d in range(2):
                src = sums[:, 16 * d:16 * d + 16].rearrange("p (c h) -> p c h", h=4)
                chain.add(nc.vector.tensor_copy(tok["gc"][:, :, 4 * d:4 * d + 4], src))
            chain.link(nc.vector.tensor_copy(tok["total"], sums[:, 32:64].rearrange("p (c d) -> p c d", d=8)))
            chain.link(nc.vector.tensor_tensor(tok["k_end"], tok["total"], tok["gc"], ALU.subtract))
            dve.wait_ge(s.act, 9)
            nc.vector.scalar_tensor_tensor(tok["nbeg"], tok["beta"], -1.0, tok["eg"], ALU.mult, ALU.mult)
            for d in range(2):
                nc.vector.memset(state[d], 0.0)
            nc.vector.memset(out[:, :, :], 0.0)

        @block.scalar
        def _(act):
            for d in range(2):
                nc.scalar.activation(tok["beta"][:, :, 4 * d:4 * d + 4], gate_t[:, :, 8 * d + 4:8 * d + 8],
                                     ACT.Sigmoid).then_inc(s.act, 1)
            act.wait_ge(s.a_ready, 1)
            nc.scalar.activation(tok["abs"], tok["a"], ACT.Abs).then_inc(s.act, 1)
            act.wait_ge(s.act, 3)
            nc.scalar.activation(tok["e"], tok["abs"], ACT.Exp, scale=-1.0).then_inc(s.act, 1)
            nc.scalar.activation(k.aux[:, 384:392], k.v("a_log"), ACT.Exp).then_inc(s.act, 1)
            act.wait_ge(s.act, 4)
            nc.scalar.activation(tok["e"], tok["e"], ACT.Ln, bias=k.eps[:, 3:4]).then_inc(s.act, 1)
            act.wait_ge(s.chain, 8)
            nc.scalar.activation(tok["eg"], tok["gc"], ACT.Exp).then_inc(s.act, 1)
            nc.scalar.activation(tok["s_end"], tok["total"], ACT.Exp).then_inc(s.act, 1)
            nc.scalar.activation(tok["k_end"], tok["k_end"], ACT.Exp).then_inc(s.act, 1)

        @block.tensor
        def _(pe):
            pe.wait_ge(s.tables, 32)
            pe.wait_ge(s.chain, 4)
            for d in range(2):
                nc.tensor.matmul(k.bank[0][:, 16 * d:16 * d + 16], tri[:, d * P:(d + 1) * P],
                                 tok["g"][:, :, 4 * d:4 * d + 4], start=True, stop=True)
            nc.tensor.matmul(k.bank[0][:, 32:64], k.ones, tok["g"], start=True, stop=True).then_inc(s.cumsum, 1)

    delta_rule(k, p, k_tok, v_tok, out, tok, levels, tri, state)

    z = p[:, 24:28, :]
    sq = k.view(EVEN_WORK, GDN_H, T2)
    root = k.view(EVEN_WORK + 4 * T2, GDN_H, T2)
    with stage(k, "gdn_out", "squared", "summed", "gated", "rooted", "chain") as (block, s):

        @block.vector
        def _(dve):
            chain = Chain(dve, s.chain)
            for h in range(GDN_H):
                nc.vector.tensor_tensor(sq[:, h, :], out[:, h, :], out[:, h, :], ALU.mult).then_inc(s.squared, 1)
            dve.wait_ge(s.rooted, GDN_H)
            chain.link(nc.vector.reciprocal(root[:, :, :], root[:, :, :]))
            chain.link(nc.vector.scalar_tensor_tensor(out[:, :, :], out[:, :, :], k.v("gdn_norm_g"), root[:, :, :],
                                                      ALU.mult, ALU.mult))
            nc.vector.tensor_tensor(y[:, 4:8, :], out[:, :, :], z, ALU.mult)

        @block.tensor
        def _(pe):
            for h in range(GDN_H):
                pe.wait_ge(s.squared, h + 1)
                nc.tensor.matmul(k.bank[h][:, :], k.ones, sq[:, h, :], start=True, stop=True).then_inc(s.summed, 1)

        @block.scalar
        def _(act):
            nc.scalar.activation(z, z, ACT.Silu)
            for h in range(GDN_H):
                act.wait_ge(s.summed, h + 1)
                nc.scalar.activation(root[:, h, :], k.bank[h][:, :], ACT.Sqrt, bias=k.eps[:, 0:1],
                                     scale=1.0 / P).then_inc(s.rooted, 1)


def delta_rule(k, p, k_tok, v_tok, out, tok, levels, tri, state):
    nc = k.nc
    H4 = range(GDN_H)
    bufs = ["x", "xt", "z", "am", "a", "pt", "exp_r", "dec_t", "kend", "bv", "qdec", "r", "u"]
    w = [{n: k.big[:, EVEN_WORK + 512 * (13 * d + i):EVEN_WORK + 512 * (13 * d + i + 1)]
          .rearrange("p (h n) -> p h n", h=GDN_H) for i, n in enumerate(bufs)} for d in range(2)]
    bank = [[k.bank[4 * d + n][:, :].rearrange("p (h n) -> p h n", h=GDN_H) for n in range(4)] for d in range(2)]
    order = [[0, 1, 2, 3], [1, 0, 3, 2]]
    steps = [(i, d, order[d][i]) for i in range(NCHUNK) for d in range(2)]
    with stage(k, "delta", "mats", "exp_r", "clamped", "decays", "qk_ready", "pool", "masked", "z_made", "z_copied",
               "deltas", "grown", "ks", "rhs", "u_made", "u_copied", "out_made", "s_made", "out_added",
               "s_done", "chain") as (block, s):

        def cols(c):
            return slice(c * P, (c + 1) * P)

        @block.tensor
        def _(pe):
            for i in range(NCHUNK):
                for d in range(2):
                    n, c, b = 2 * i + d, order[d][i], bank[d]
                    at_least(pe, s.out_added, n - 1)
                    for h in H4:
                        nc.tensor.matmul(b[0][:, h, :], tok["g"][:, c, 4 * d + h:4 * d + h + 1].broadcast_to([P, P]),
                                         tri[:, d * P:(d + 1) * P], start=True, stop=True)
                    for h in H4:
                        nc.tensor.matmul(b[1][:, h, :], p[:, 4 + h, cols(c)], p[:, 4 + h, cols(c)],
                                         start=True, stop=True)
                    for h in H4:
                        last = nc.tensor.matmul(b[2][:, h, :], p[:, 4 + h, cols(c)], p[:, h, cols(c)],
                                                start=True, stop=True)
                    last.then_inc(s.mats, 1)
                for lev in range(LEVELS):
                    for d in range(2):
                        m = (2 * i + d) * LEVELS + lev
                        pe.wait_ge(s.masked, (i * LEVELS + lev) * 2 + d + 1)
                        pe.wait_ge(s.grown, (i * (LEVELS + 1) + lev) * 2 + d + 1)
                        for h in H4:
                            last = nc.tensor.matmul(bank[d][0][:, h, :], w[d]["am"][:, h, :], w[d]["xt"][:, h, :],
                                                    start=True, stop=True)
                        last.then_inc(s.z_made, 1)
                    for d in range(2):
                        pe.wait_ge(s.z_copied, (i * LEVELS + lev) * 2 + d + 1)
                        for h in H4:
                            last = nc.tensor.matmul(bank[d][1][:, h, :], w[d]["x"][:, h, :], w[d]["z"][:, h, :],
                                                    start=True, stop=True)
                        if lev < LEVELS - 1:
                            for h in H4:
                                last = nc.tensor.matmul(bank[d][2][:, h, :], w[d]["z"][:, h, :], w[d]["x"][:, h, :],
                                                        start=True, stop=True)
                        last.then_inc(s.deltas, 1)
                for d in range(2):
                    n, c = 2 * i + d, order[d][i]
                    at_least(pe, s.s_done, n - 1)
                    for h in H4:
                        last = nc.tensor.matmul(bank[d][0][:, h, :], p[:, 4 + h, cols(c)], state[d][:, h, :],
                                                start=True, stop=True)
                    last.then_inc(s.ks, 1)
                for d in range(2):
                    n, c = 2 * i + d, order[d][i]
                    pe.wait_ge(s.rhs, n + 1)
                    pe.wait_ge(s.grown, (i * (LEVELS + 1) + LEVELS) * 2 + d + 1)
                    for h in H4:
                        last = nc.tensor.matmul(bank[d][1][:, h, :], w[d]["xt"][:, h, :], w[d]["r"][:, h, :],
                                                start=True, stop=True)
                    last.then_inc(s.u_made, 1)
                for d in range(2):
                    n, c = 2 * i + d, order[d][i]
                    pe.wait_ge(s.u_copied, n + 1)
                    pe.wait_ge(s.pool, n + 1)
                    pe.wait_ge(s.qk_ready, n + 1)
                    for h in H4:
                        nc.tensor.matmul(bank[d][2][:, h, :], state[d][:, h, :], w[d]["qdec"][:, h, :],
                                         start=True, stop=False)
                        last = nc.tensor.matmul(bank[d][2][:, h, :], w[d]["u"][:, h, :], w[d]["pt"][:, h, :],
                                                start=False, stop=True)
                    last.then_inc(s.out_made, 1)
                    for h in H4:
                        last = nc.tensor.matmul(bank[d][3][:, h, :], w[d]["kend"][:, h, :], w[d]["u"][:, h, :],
                                                start=True, stop=True)
                    last.then_inc(s.s_made, 1)

        @block.scalar
        def _(act):
            for i in range(NCHUNK):
                for d in range(2):
                    n = 2 * i + d
                    act.wait_ge(s.clamped, n + 1)
                    at_least(act, s.pool, n - 1)
                    nc.scalar.activation(w[d]["exp_r"], bank[d][0], ACT.Exp).then_inc(s.exp_r, 1)
                for d in range(2):
                    nc.scalar.activation(w[d]["a"], w[d]["a"], ACT.Exp, scale=-1.0)
                    nc.scalar.activation(w[d]["dec_t"], w[d]["dec_t"], ACT.Exp).then_inc(s.decays, 1)
                for lev in range(LEVELS):
                    for d in range(2):
                        m = (i * LEVELS + lev) * 2 + d
                        act.wait_ge(s.z_made, m + 1)
                        at_least(act, s.deltas, m - 1)
                        nc.scalar.activation(w[d]["z"], bank[d][0], ACT.Copy).then_inc(s.z_copied, 1)
                for d in range(2):
                    n = 2 * i + d
                    act.wait_ge(s.u_made, n + 1)
                    at_least(act, s.s_made, n - 1)
                    nc.scalar.activation(w[d]["u"], bank[d][1], ACT.Copy).then_inc(s.u_copied, 1)

        @block.gpsimd
        def _(pool):
            for i, d, c in steps:
                n = 2 * i + d
                at_least(pool, s.s_made, n - 1)
                at_least(pool, s.rhs, n - 1)
                for h in H4:
                    nc.gpsimd.tensor_scalar(w[d]["kend"][:, h, :], k_tok[:, c, h * P:(h + 1) * P],
                                            tok["k_end"][:, c, 4 * d + h:4 * d + h + 1], None, ALU.mult)
                    nc.gpsimd.tensor_scalar(w[d]["bv"][:, h, :], v_tok[:, c, h * P:(h + 1) * P],
                                            tok["beta"][:, c, 4 * d + h:4 * d + h + 1], None, ALU.mult)
                pool.wait_ge(s.exp_r, n + 1)
                nc.gpsimd.tensor_tensor(w[d]["qdec"], p[:, 0:GDN_H, cols(c)], w[d]["exp_r"],
                                        ALU.mult).then_inc(s.pool, 1)

        @block.vector
        def _(dve):
            chain = Chain(dve, s.chain)
            for i in range(NCHUNK):
                for d in range(2):
                    n, c, b, q = 2 * i + d, order[d][i], bank[d], w[d]
                    dve.wait_ge(s.mats, n + 1)
                    at_least(dve, s.out_made, n - 1)
                    chain.add(nc.vector.tensor_copy(q["x"], k.ident.unsqueeze(1).broadcast_to([P, GDN_H, P])))
                    nc.vector.tensor_copy(q["xt"], k.ident.unsqueeze(1).broadcast_to([P, GDN_H, P])).then_inc(s.grown, 1)
                    for h in H4:
                        gc = tok["gc"][:, c, 4 * d + h:4 * d + h + 1]
                        nc.vector.tensor_scalar(q["a"][:, h, :], b[0][:, h, :], gc, 0.0, ALU.subtract, ALU.max)
                        ins = nc.vector.tensor_scalar(q["dec_t"][:, h, :], b[0][:, h, :], gc, 0.0,
                                                      ALU.subtract, ALU.min)
                    ins.then_inc(s.clamped, 1)
                for d in range(2):
                    n, c, b, q = 2 * i + d, order[d][i], bank[d], w[d]
                    dve.wait_ge(s.decays, n + 1)
                    for h in H4:
                        chain.add(nc.vector.scalar_tensor_tensor(
                            q["a"][:, h, :], b[1][:, h, :], tok["beta"][:, c, 4 * d + h:4 * d + h + 1],
                            q["a"][:, h, :], ALU.mult, ALU.mult))
                    chain.link(nc.vector.tensor_tensor(q["pt"], b[2], q["dec_t"], ALU.mult))
                    nc.vector.tensor_tensor(q["pt"], q["pt"],
                                            tri[:, d * P:(d + 1) * P].unsqueeze(1).broadcast_to([P, GDN_H, P]),
                                            ALU.mult).then_inc(s.qk_ready, 1)
                for lev in range(LEVELS):
                    for d in range(2):
                        m, q = (i * LEVELS + lev) * 2 + d, w[d]
                        at_least(dve, s.z_made, m - 1)
                        mask = levels[:, d * LEVELS + lev, :].unsqueeze(1).broadcast_to([P, GDN_H, P])
                        nc.vector.tensor_tensor(q["am"], q["a"], mask, ALU.mult).then_inc(s.masked, 1)
                    for d in range(2):
                        m, q = (i * LEVELS + lev) * 2 + d, w[d]
                        dve.wait_ge(s.deltas, m + 1)
                        dve.wait_ge(s.grown, (i * (LEVELS + 1) + lev) * 2 + d + 1)
                        if lev < LEVELS - 1:
                            nc.vector.tensor_tensor(q["x"], q["x"], bank[d][2], ALU.subtract)
                        nc.vector.tensor_tensor(q["xt"], q["xt"], bank[d][1], ALU.subtract).then_inc(s.grown, 1)
                for d in range(2):
                    n, c, q = 2 * i + d, order[d][i], w[d]
                    dve.wait_ge(s.ks, n + 1)
                    dve.wait_ge(s.pool, n + 1)
                    for h in H4:
                        ins = nc.vector.scalar_tensor_tensor(
                            q["r"][:, h, :], bank[d][0][:, h, :], tok["nbeg"][:, c, 4 * d + h:4 * d + h + 1],
                            q["bv"][:, h, :], ALU.mult, ALU.add)
                    ins.then_inc(s.rhs, 1)
                for d in range(2):
                    n, c = 2 * i + d, order[d][i]
                    dve.wait_ge(s.out_made, n + 1)
                    dve.wait_ge(s.out_added, n) if n else None
                    o = out[:, :, cols(c)]
                    nc.vector.tensor_tensor(o, o, bank[d][2], ALU.add).then_inc(s.out_added, 1)
                    dve.wait_ge(s.s_made, n + 1)
                    at_least(dve, s.s_done, n - 1)
                    for h in H4:
                        ins = nc.vector.scalar_tensor_tensor(
                            state[d][:, h, :], state[d][:, h, :], tok["s_end"][:, c, 4 * d + h:4 * d + h + 1],
                            bank[d][3][:, h, :], ALU.mult, ALU.add)
                    ins.then_inc(s.s_done, 1)


def odd_mixer(k, w_in, w_uq, w_ukv, w_out, then):
    nc = k.nc
    at = [0]

    def take(tiles, t):
        v = k.view(at[0], tiles, t)
        at[0] += tiles * t
        return v

    p, cq, ckv = take(6, T2), take(3, L), take(2, T2)
    q, kv, v_tok, y = take(12, L), take(16, T2), take(NCHUNK, 1024), take(8, L)
    linear(k, "mla_in", w_in, DT, T2, lambda kk, u: k.h[:, kk, :],
           lambda u, bank: nc.scalar.activation(tile_of(p, u), bank[:, 0:T2], ACT.Copy), engine="scalar",
           then=lambda sp: w_uq.prime(sp))
    norm(k, "q_norm", lambda i: p[:, i, TOK:T2], lambda i: cq[:, i, :], 3, L, 384,
         gain=lambda i: [((0, L), k.v("mla_q_g", i, 1))])
    norm(k, "kv_norm", lambda i: p[:, 3 + i, :], lambda i: ckv[:, i, :], 2, T2, 256,
         gain=lambda i: [((0, T2), k.v("mla_kv_g", i, 1))])
    q2 = q.rearrange("p (u s) t -> p u (s t)", s=2)
    linear(k, "mla_q", w_uq, 3, L, lambda kk, u: cq[:, kk, :],
           lambda u, bank: nc.scalar.activation(tile_of(q2, u), bank[:, 0:T2], ACT.Copy), engine="scalar",
           then=lambda sp: w_ukv.prime(sp))
    linear(k, "mla_kv", w_ukv, 2, T2, lambda kk, u: ckv[:, kk, :],
           lambda u, bank: nc.scalar.activation(tile_of(kv, u), bank[:, 0:T2], ACT.Copy), engine="scalar",
           then=lambda sp: w_out.prime(sp))

    rot, cos, sin = k.aux[:, 0:P], k.aux[:, 512:512 + L], k.aux[:, 768:768 + L]
    tmp = k.aux[:, 1024:1024 + 5 * L].rearrange("p (n t) -> p n t", t=L)
    roped = [q[:, 8 + j, :] for j in range(4)] + [p[:, 5, TOK:T2]]
    with stage(k, "rope", "tables", "turned", "chain") as (block, s):

        @block.sync
        def _(sp):
            for dst, name in ((rot, "rot"), (cos, "cos"), (sin, "sin")):
                sp.dma_start(dst, k.const(name)).then_inc(s.tables, 16)

        @block.tensor
        def _(pe):
            pe.wait_ge(s.tables, 48)
            for j, x in enumerate(roped):
                nc.tensor.matmul(k.bank[j][:, 0:L], rot, x, start=True, stop=True).then_inc(s.turned, 1)

        @block.vector
        def _(dve):
            chain = Chain(dve, s.chain)
            dve.wait_ge(s.tables, 48)
            for j, x in enumerate(roped):
                dve.wait_ge(s.turned, j + 1)
                chain.add(nc.vector.tensor_tensor(tmp[:, j, :], k.bank[j][:, 0:L], sin, ALU.mult))
                chain.link(nc.vector.tensor_tensor(x, x, cos, ALU.mult))
                nc.vector.tensor_tensor(x, x, tmp[:, j, :], ALU.add)

    transposes(k, "mla_v", [(kv[:, 8 + h, c * P:(c + 1) * P], v_tok[:, c, h * P:(h + 1) * P])
                            for c in range(NCHUNK) for h in range(HEADS)])
    units = []
    for h in range(HEADS):
        rows = slice(64 * (h % 2), 64 * (h % 2) + 64)
        for qt in range(2):
            cols = slice(qt * P, (qt + 1) * P)
            units.append(Unit(
                q=[q[:, h, cols], q[rows, 8 + h // 2, cols]], k=[kv[:, h, :], p[rows, 5, :]], keys=T2,
                v=[v_tok[:, c, h * P:(h + 1) * P] for c in range(NCHUNK)], bias=None, base=0, dv=P,
                out=y[:, h, cols]))
    attention(k, "mla", units, (128 + 64) ** -0.5, at[0])
    chain_residual(k, "mla_out", w_out, lambda kk, u: y[:, kk, :], lambda u: k.mod_at(1, 2, u, 1), then)


def chain_residual(k, name, w, rhs, gate, then):
    nc = k.nc

    def add(u, bank):
        for j in range(2):
            x = tile_of(k.x, u * 2 + j, TOK, T2)
            ins = nc.vector.scalar_tensor_tensor(x, bank[:, j * L:(j + 1) * L], gate(u * 2 + j), x,
                                                 ALU.mult, ALU.add)
        return ins

    linear(k, name, w, DT, L, rhs, add, then=then)


def experts(k, layer, first, w_q, then):
    nc = k.nc
    half = first // L
    xs = lambda kk: (k.hh[:, kk, 0:L], k.hl[:, kk, 0:L])
    mod_norm(k, layer, True, (first, first + L), prime=w_q.prime)
    qy = k.view(0, 16, L)
    keys = k.view(4096, 16, KEYS)
    score = [k.view(6144 + 2048 * i, 16, KEYS) for i in range(2)]
    q2 = k.big[:, 0:4096].rearrange("p (u n) -> p u n", n=512)
    linear3(k, "peer_q", w_q, DT, L, xs,
           lambda u, bank: nc.scalar.activation(tile_of(q2, u), bank[:, 0:T2], ACT.Copy), engine="scalar")

    with stage(k, "peer_scores", "keys", "scored", "copied") as (block, s):

        @block.sync
        def _(sp):
            sp.dma_start(keys[:, :, :], k.io["sub_keys"][layer].rearrange("p (n m) -> p n m", n=16)).then_inc(s.keys, 16)

        @block.tensor
        def _(pe):
            pe.wait_ge(s.keys, 16)
            for tt in range(2):
                for g in range(4):
                    for j in range(4):
                        last = nc.tensor.matmul(k.bank[4 * tt + g][:, j * P:(j + 1) * P],
                                                qy[:, 4 * g + j, tt * P:(tt + 1) * P], keys[:, 4 * g + j, :],
                                                start=True, stop=True)
                    last.then_inc(s.scored, 1)

        @block.scalar
        def _(act):
            for tt in range(2):
                for g in range(4):
                    act.wait_ge(s.scored, 4 * tt + g + 1)
                    nc.scalar.activation(score[tt][:, 4 * g:4 * g + 4, :],
                                         k.bank[4 * tt + g][:, :].rearrange("p (n m) -> p n m", n=4), ACT.Copy)

    i1_t, i2_t, gate_t = (k.aux[:, L * j:L * (j + 1)] for j in range(3))
    routing(k, score, (i1_t, i2_t, gate_t))

    table = k.big[:, :].rearrange("p (i t) -> p i t", t=L)
    row_hot = [k.aux[:, 768 + 1024 * b:1280 + 1024 * b].rearrange("p (q n) -> p q n", n=KEYS) for b in range(2)]
    col_hot = [k.aux[:, 1280 + 1024 * b:1792 + 1024 * b].rearrange("p (q n) -> p q n", n=KEYS) for b in range(2)]
    u_loaded = [nc.alloc_semaphore(f"u_loaded{b}_{k.stage_no}") for b in range(2)]
    v_loaded = [nc.alloc_semaphore(f"v_loaded{b}_{k.stage_no}") for b in range(2)]
    u_dram, v_dram = k.io["experts_u"], k.io["experts_v"]
    e0 = layer * KEYS

    def expert_row(dram, i):
        if isinstance(i, int):
            return dram[e0 + i]
        return dram[bass.ds(i + e0, 1)].rearrange("o p n -> (o p) n")

    def load_u(sp, i, b):
        sp.dma_start(k.ring[:, 2 * b, 0:D], expert_row(u_dram, i)).then_inc(u_loaded[b], 16)

    def load_v(sp, i, b):
        sp.dma_start(k.ring[:, 2 * b + 1, 0:D], expert_row(v_dram, i)).then_inc(v_loaded[b], 16)

    with stage(k, "table", "rows", "columns", "spread", "stored") as (block, s):

        @block.sync
        def _(sp):
            for b in range(2):
                load_u(sp, b, b)
                load_v(sp, b, b)

        @block.vector
        def _(dve):
            iota = k.iota.unsqueeze(1).broadcast_to([P, 4, KEYS])

            def group(r, b):
                g = r * 2 + b
                at_least(dve, s.spread, (r - 1) * 2 + (b + 1))
                tok = bass.ds(g * 4, 4)

                def spread(t):
                    return t[:, tok].unsqueeze(2).broadcast_to([P, 4, KEYS])

                nc.vector.tensor_tensor(col_hot[b], iota, spread(i2_t), ALU.is_equal).then_inc(s.columns, 1)
                nc.vector.tensor_tensor(row_hot[b], iota, spread(i1_t), ALU.is_equal).then_inc(s.rows, 1)
                dve.wait_ge(s.columns, g * 2 + 1)
                nc.vector.tensor_tensor(col_hot[b], col_hot[b], spread(gate_t), ALU.mult).then_inc(s.columns, 1)

            repeat(dve, L // 8, lambda r: [group(r, b) for b in range(2)])

        @block.tensor
        def _(pe):
            def group(r, b):
                g = r * 2 + b
                pe.wait_ge(s.columns, g * 2 + 2)
                pe.wait_ge(s.rows, g + 1)
                at_least(pe, s.stored, (r - 1) * 2 + (b + 1))
                for j in range(4):
                    last = nc.tensor.matmul(k.bank[b][:, j * P:(j + 1) * P], col_hot[b][:, j, :],
                                            row_hot[b][:, j, :], start=True, stop=True)
                last.then_inc(s.spread, 1)

            repeat(pe, L // 8, lambda r: [group(r, b) for b in range(2)])

        @block.scalar
        def _(act):
            def group(r, b):
                g = r * 2 + b
                act.wait_ge(s.spread, g + 1)
                nc.scalar.activation(table[:, :, bass.ds(g * 4, 4)],
                                     k.bank[b][:, :].rearrange("p (q n) -> p n q", n=KEYS),
                                     ACT.Copy).then_inc(s.stored, 1)

            repeat(act, L // 8, lambda r: [group(r, b) for b in range(2)])

    hi, lo = k.parts(D, at=0, buf=k.aux)
    act_buf = [k.aux[:, 4096 + L * b:4096 + L * (b + 1)] for b in range(2)]
    product = [k.aux[:, 4608 + L * b:4608 + L * (b + 1)] for b in range(2)]
    ends = [k.ring[:, b, D:D + L].bitcast(BF16) for b in range(2)]
    gated = [(ends[b][:, 0:L], ends[b][:, L:2 * L]) for b in range(2)]
    with stage(k, "experts", "u_high", "v_high", "u_low", "v_low", "hidden", "activated", "product", "gated_high",
               "gated", "mixed") as (block, s):
        u_slot = [k.ring[:, 2 * b, 0:D] for b in range(2)]
        v_slot = [k.ring[:, 2 * b + 1, 0:D] for b in range(2)]

        @block.sync
        def _(sp):
            def refill(r):
                for b in range(2):
                    i = r * 2 + b
                    sp.wait_ge(s.u_low, i + 1)
                    load_u(sp, i + 2, b)
                    sp.wait_ge(s.v_low, i + 1)
                    load_v(sp, i + 2, b)

            repeat(sp, KEYS // 2 - 1, refill)
            if then is not None:
                then(sp)

        @block.tensor
        def _(pe):
            def hidden(r, b):
                pe.wait_ge(s.u_low, r * 2 + b + 1)
                at_least(pe, s.activated, (r - 1) * 2 + (b + 1))
                dst = k.bank[4 + b][:, 0:L]
                for kk in range(DT):
                    cols = slice(kk * P, (kk + 1) * P)
                    xh, xl = xs(kk)
                    nc.tensor.matmul(dst, hi[2 * b][:, cols], xh, start=kk == 0, stop=False)
                    nc.tensor.matmul(dst, hi[2 * b][:, cols], xl, start=False, stop=False)
                    last = nc.tensor.matmul(dst, lo[2 * b][:, cols], xh, start=False, stop=kk == DT - 1)
                last.then_inc(s.hidden, 1)

            def mix(r, b, first=False, last_group=False):
                pe.wait_ge(s.v_low, r * 2 + b + 1)
                pe.wait_ge(s.gated, r * 2 + b + 1)
                gh, gl = gated[b]
                for dt in range(DT):
                    cols = slice(dt * P, (dt + 1) * P)
                    dst = k.bank[dt // 2][:, (dt % 2) * L:(dt % 2 + 1) * L]
                    nc.tensor.matmul(dst, hi[2 * b + 1][:, cols], gh, start=first and dt % 2 == 0, stop=False,
                                     skip_group_check=True)
                    nc.tensor.matmul(dst, hi[2 * b + 1][:, cols], gl, start=False, stop=False, skip_group_check=True)
                    ins = nc.tensor.matmul(dst, lo[2 * b + 1][:, cols], gh, start=False, stop=last_group,
                                           skip_group_check=True)
                ins.then_inc(s.mixed, 1)

            hidden(0, 0)
            hidden(0, 1)
            mix(0, 0, first=True)
            hidden(1, 0)
            mix(0, 1)

            with pe.Fori(1, KEYS // 2 - 1) as r:
                hidden(r, 1)
                mix(r, 0)
                hidden(r + 1, 0)
                mix(r, 1)
            end = KEYS // 2 - 1
            hidden(end, 1)
            mix(end, 0)
            mix(end, 1, last_group=True)

        @block.scalar
        def _(act):
            def u_high(r, b):
                act.wait_ge(u_loaded[b], r * 16 + 16)
                at_least(act, s.hidden, (r - 1) * 2 + (b + 1))
                nc.scalar.activation(hi[2 * b], u_slot[b], ACT.Copy).then_inc(s.u_high, 1)

            def group(r, b, more=True):
                i = r * 2 + b
                if more:
                    u_high(r if b == 0 else r + 1, 1 - b)
                act.wait_ge(v_loaded[b], r * 16 + 16)
                at_least(act, s.mixed, (r - 1) * 2 + (b + 1))
                nc.scalar.activation(hi[2 * b + 1], v_slot[b], ACT.Copy).then_inc(s.v_high, 1)
                act.wait_ge(s.hidden, i + 1)
                at_least(act, s.product, (r - 1) * 2 + (b + 1))
                nc.scalar.activation(act_buf[b], k.bank[4 + b][:, 0:L], ACT.Gelu).then_inc(s.activated, 1)

            u_high(0, 0)
            repeat(act, KEYS // 2 - 1, lambda r: [group(r, b) for b in range(2)])
            group(KEYS // 2 - 1, 0)
            group(KEYS // 2 - 1, 1, more=False)

        @block.vector
        def _(dve):
            def u_low(r, b):
                dve.wait_ge(s.u_high, r * 2 + b + 1)
                nc.vector.tensor_tensor(lo[2 * b], u_slot[b], hi[2 * b], ALU.subtract).then_inc(s.u_low, 1)

            def group(r, b, more=True):
                i = r * 2 + b
                if more:
                    u_low(r if b == 0 else r + 1, 1 - b)
                dve.wait_ge(s.v_high, i + 1)
                nc.vector.tensor_tensor(lo[2 * b + 1], v_slot[b], hi[2 * b + 1], ALU.subtract).then_inc(s.v_low, 1)
                dve.wait_ge(s.activated, i + 1)
                nc.vector.tensor_tensor(product[b], act_buf[b], tile_of(table, i), ALU.mult).then_inc(s.product, 1)
                dve.wait_ge(s.product, i + 1)
                at_least(dve, s.mixed, (r - 1) * 2 + (b + 1))
                nc.vector.tensor_copy(gated[b][0], product[b]).then_inc(s.gated_high, 1)
                dve.wait_ge(s.gated_high, i + 1)
                nc.vector.tensor_tensor(gated[b][1], product[b], gated[b][0], ALU.subtract).then_inc(s.gated, 1)

            u_low(0, 0)
            repeat(dve, KEYS // 2 - 1, lambda r: [group(r, b) for b in range(2)])
            group(KEYS // 2 - 1, 0)
            group(KEYS // 2 - 1, 1, more=False)
            dve.wait_ge(s.mixed, KEYS)
            for dt in range(DT):
                x = k.x[:, dt, first:first + L]
                nc.vector.scalar_tensor_tensor(x, k.bank[dt // 2][:, (dt % 2) * L:(dt % 2 + 1) * L],
                                               k.mod_at(layer, 5, dt, half), x, ALU.mult, ALU.add)
    k.spent += u_loaded + v_loaded


def routing(k, score, results):
    nc = k.nc
    at = [10240]

    def take(n, dt=F32):
        at[0] += n
        v = k.big[:, at[0] - n:at[0]]
        return v if dt == F32 else v.bitcast(dt)

    top, top_i = take(512), take(512, U32)
    top_f = take(512)
    best, best_i = take(256), take(256, U32)
    hi_i, lo_i = take(256, U32), take(256, U32)
    hi_f, lo_f = take(256), take(256)
    comb = take(2 * 2048)
    hot = take(2048)
    row, col, gate = take(256), take(256), take(256)
    small = take(64)
    three = lambda v, n, m: v.rearrange("p (n m) -> p n m", m=m)
    with stage(k, "routing", "chain", "tops", "exps", "ready", "turned") as (block, s):

        @block.vector
        def _(dve):
            chain = Chain(dve, s.chain)

            def best16(values, out, out_i, jobs):
                for half in range(2):
                    sl = slice(8 * half, 8 * half + 8)
                    for j in jobs:
                        chain.add(nc.vector.max(out=out(j)[:, sl], in_=values(j)))
                    chain.settle()
                    for j in jobs:
                        chain.add(nc.vector.max_index(out=out_i(j)[:, sl], in_max=out(j)[:, sl], in_values=values(j)))
                    if half == 0:
                        chain.settle()
                        for j in jobs:
                            chain.add(nc.vector.match_replace(out=values(j), in_to_replace=out(j)[:, sl],
                                                              in_values=values(j), imm_value=-3e38))
                        chain.settle()

            jobs = [(tt, n) for tt in range(2) for n in range(16)]
            sub = lambda v: lambda j: v[:, 256 * j[0] + 16 * j[1]:256 * j[0] + 16 * j[1] + 16]
            best16(lambda j: score[j[0]][:, j[1], :], sub(top), sub(top_i), jobs)
            chain.settle()
            chain.link(nc.vector.tensor_copy(top_f, top_i))
            heads = [(tt, n) for tt in range(2) for n in range(HEADS)]
            pair = three(comb, 16, 256)
            for tt, n in heads:
                a = top[:, 256 * tt + 32 * n:256 * tt + 32 * n + 16]
                b = top[:, 256 * tt + 32 * n + 16:256 * tt + 32 * n + 32]
                chain.add(nc.vector.tensor_tensor(
                    pair[:, 8 * tt + n, :].rearrange("p (i j) -> p i j", j=16),
                    a.unsqueeze(2).broadcast_to([P, 16, 16]), b.unsqueeze(1).broadcast_to([P, 16, 16]), ALU.add))
            chain.settle()
            sub8 = lambda v: lambda j: v[:, 128 * j[0] + 16 * j[1]:128 * j[0] + 16 * j[1] + 16]
            best16(lambda j: pair[:, 8 * j[0] + j[1], :], sub8(best), sub8(best_i), heads)
            chain.settle()
            b3, g3 = three(best, 16, 16), three(gate, 16, 16)
            nc.vector.tensor_tensor(g3, b3, b3[:, :, 0:1].broadcast_to([P, 16, 16]), ALU.subtract).then_inc(s.tops, 1)
            chain.add(nc.vector.tensor_single_scalar(hi_i, best_i, 4, ALU.logical_shift_right))
            chain.add(nc.vector.tensor_single_scalar(lo_i, best_i, 15, ALU.bitwise_and))
            chain.settle()
            chain.add(nc.vector.tensor_copy(hi_f, hi_i))
            chain.add(nc.vector.tensor_copy(lo_f, lo_i))
            chain.settle()
            iota16 = k.iota[:, 0:16].unsqueeze(1).broadcast_to([P, P, 16])
            h3 = three(hot, 128, 16)
            h4 = hot.rearrange("p (h r j) -> p h r j", r=16, j=16)
            for tt in range(2):
                for rank, first, dst in ((hi_f, 0, row), (lo_f, 16, col)):
                    chain.link(nc.vector.tensor_tensor(
                        h3, rank[:, 128 * tt:128 * tt + 128].unsqueeze(2).broadcast_to([P, P, 16]), iota16, ALU.is_equal))
                    ids = top_f[:, 256 * tt:256 * tt + 256].rearrange("p (h n) -> p h n", n=32)[:, :, first:first + 16]
                    chain.link(nc.vector.tensor_tensor(h4, h4, ids.unsqueeze(2).broadcast_to([P, HEADS, 16, 16]), ALU.mult))
                    chain.link(nc.vector.tensor_reduce(dst[:, 128 * tt:128 * tt + 128], h3, AX.X, ALU.add))
            dve.wait_ge(s.exps, 1)
            chain.link(nc.vector.tensor_reduce(small[:, 0:16], g3, AX.X, ALU.add))
            chain.link(nc.vector.reciprocal(small[:, 16:32], small[:, 0:16]))
            nc.vector.tensor_tensor(g3, g3, small[:, 16:32].unsqueeze(2).broadcast_to([P, 16, 16]),
                                    ALU.mult).then_inc(s.ready, 1)
            dve.wait_ge(s.turned, 1)
            for n, dst in enumerate(results):
                nc.vector.tensor_copy(dst, k.bank[n][:, 0:L])

        @block.scalar
        def _(act):
            act.wait_ge(s.tops, 1)
            nc.scalar.activation(gate, gate, ACT.Exp).then_inc(s.exps, 1)

        @block.tensor
        def _(pe):
            pe.wait_ge(s.ready, 1)
            for n, src in enumerate((row, col, gate)):
                for tt in range(2):
                    last = nc.tensor.transpose(k.bank[n][:, tt * P:(tt + 1) * P], src[:, tt * P:(tt + 1) * P], k.ident)
            last.then_inc(s.turned, 1)


def swiglu(k, layer, which, w_up, w_down, then):
    nc = k.nc
    both = k.big[:, 0:FF_T * L].bitcast(BF16).rearrange("p (n t) -> p n t", t=L)
    ah, al = both[:, 0:FF_T, :], both[:, FF_T:2 * FF_T, :]
    y = k.view(FF_T * L, DT, L)
    gate = [k.aux[:, 1024 + L * b:1024 + L * (b + 1)] for b in range(2)]
    prod = [k.aux[:, 1536 + L * b:1536 + L * (b + 1)] for b in range(2)]
    pre, post = f"ffn{which}_pre", f"ffn{which}_post"
    wide = k.view(SCRATCH, DT, L)
    norm(k, "ffn_norm", lambda i: k.x[:, i, TOK:T2], lambda i: wide[:, i, :], DT, L, D,
         gain=lambda i: [((0, L), k.v(pre, 8 * layer + i, 1))], halves=halves_of_h(k, L), prime=w_up.prime)
    body = 2
    rounds = FF_T // body
    w = w_up
    size = DT * P
    hi, lo = k.parts(SLOT)
    with stage(k, "ffn_up", "high", "low", "chunk_used", "silu", "product", "a_high", "a_low") as (block, s):

        @block.sync
        def _(sp):
            def refill(r):
                for slot in range(RING):
                    sp.wait_ge(s.low, r * RING + (slot + 1))
                    w.load(sp, r * RING + (slot + RING), slot)

            repeat(sp, w.chunks // RING - 1, refill)
            sp.wait_ge(s.low, w.chunks)
            w_down.prime(sp)

        @block.tensor
        def _(pe):
            def unit(r, b):
                at_least(pe, s.product, (r - 1) * body + (b + 1))
                for c in range(2):
                    slot = 2 * b + c
                    pe.wait_ge(s.low, r * RING + (slot + 1))
                    dst = k.bank[b][:, c * L:(c + 1) * L]
                    for kk in range(DT):
                        cols = slice(kk * P, (kk + 1) * P)
                        xh, xl = k.hh[:, kk, 0:L], k.hl[:, kk, 0:L]
                        nc.tensor.matmul(dst, hi[slot][:, cols], xh, start=kk == 0, stop=False)
                        nc.tensor.matmul(dst, hi[slot][:, cols], xl, start=False, stop=False)
                        last = nc.tensor.matmul(dst, lo[slot][:, cols], xh, start=False, stop=kk == DT - 1)
                    last.then_inc(s.chunk_used, 1)

            repeat(pe, rounds, lambda r: [unit(r, b) for b in range(body)])

        @block.scalar
        def _(act):
            def high(r, b):
                for slot in (2 * b, 2 * b + 1):
                    act.wait_ge(w.loaded[slot], r * 16 + 16)
                    at_least(act, s.chunk_used, (r - 1) * RING + (slot + 1))
                    nc.scalar.activation(hi[slot][:, 0:size], k.ring[:, slot, 0:size], ACT.Copy).then_inc(s.high, 1)

            def activate(r, b):
                act.wait_ge(s.chunk_used, r * RING + (2 * b + 2))
                at_least(act, s.product, (r - 1) * body + (b + 1))
                nc.scalar.activation(gate[b], k.bank[b][:, 0:L], ACT.Silu).then_inc(s.silu, 1)

            def pair(r, last=False):
                high(r, 1)
                activate(r, 0)
                if not last:
                    high(r + 1, 0)
                activate(r, 1)

            high(0, 0)
            repeat(act, rounds - 1, pair)
            pair(rounds - 1, last=True)

        @block.vector
        def _(dve):
            def low(r, b):
                for slot in (2 * b, 2 * b + 1):
                    dve.wait_ge(s.high, r * RING + (slot + 1))
                    nc.vector.tensor_tensor(lo[slot][:, 0:size], k.ring[:, slot, 0:size], hi[slot][:, 0:size],
                                            ALU.subtract).then_inc(s.low, 1)

            def multiply(r, b):
                u = r * body + b
                dve.wait_ge(s.silu, u + 1)
                nc.vector.tensor_tensor(prod[b], gate[b], k.bank[b][:, L:T2], ALU.mult).then_inc(s.product, 1)
                dve.wait_ge(s.product, u + 1)
                nc.vector.tensor_copy(tile_of(ah, u), prod[b]).then_inc(s.a_high, 1)
                dve.wait_ge(s.a_high, u + 1)
                nc.vector.tensor_tensor(tile_of(al, u), prod[b], tile_of(ah, u), ALU.subtract).then_inc(s.a_low, 1)

            def pair(r, last=False):
                low(r, 1)
                multiply(r, 0)
                if not last:
                    low(r + 1, 0)
                multiply(r, 1)

            low(0, 0)
            repeat(dve, rounds - 1, pair)
            pair(rounds - 1, last=True)

    w_up.retire()
    y2 = k.big[:, FF_T * L:(FF_T + DT) * L].rearrange("p (u n) -> p u n", n=T2)
    linear3(k, "ffn_down", w_down, FF_T, L, lambda kk: (ah[:, kk, :], al[:, kk, :]),
            lambda u, bank: nc.scalar.activation(tile_of(y2, u), bank[:, 0:T2], ACT.Copy), engine="scalar", then=then)
    norm(k, "ffn_post", lambda i: y[:, i, :], lambda i: k.h[:, i, 0:L], DT, L, D,
         gain=lambda i: [((0, L), k.v(post, 8 * layer + i, 1))],
         residual=(lambda i: k.x[:, i, TOK:T2], 0.5))


def conv_pool_mixer(k, layer, w, then):
    nc = k.nc
    z = k.view(0, 48, L)
    z2 = k.big[:, 0:48 * L].rearrange("p (u n) -> p u n", n=T2)
    base = 48 * L
    ya, pool, m1, m2 = (k.view(base + 8 * L * i, DT, L) for i in range(4))
    spare = k.view(base + 32 * L, DT, L)
    counts = k.view(base + 40 * L, 4, L)
    wide = k.view(SCRATCH, DT, L)
    xs = lambda kk: (k.hh[:, kk, 0:L], k.hl[:, kk, 0:L])
    norm(k, "mix_norm", lambda i: k.x[:, i, TOK:T2], lambda i: wide[:, i, :], DT, L, D,
         gain=lambda i: [((0, L), k.v("mix_pre", 8 * layer + i, 1))], halves=halves_of_h(k, L), prime=w.w_in.prime)
    linear3(k, "mix_in", w.w_in, DT, L, xs,
           lambda u, bank: nc.scalar.activation(tile_of(z2, u), bank[:, 0:T2], ACT.Copy), engine="scalar",
           then=lambda sp: w.w_pg.prime(sp))
    taps = k.v("conv_w_2", 24 * layer, 24).rearrange("p (t j) -> p t j", j=3)
    with stage(k, "conv_pool", "counts", "chain", "gates") as (block, s):

        @block.sync
        def _(sp):
            sp.dma_start(counts[:, :, :], k.const("inv_count").rearrange("p (n t) -> p n t", t=L)).then_inc(s.counts, 16)

        @block.scalar
        def _(act):
            for i in range(16):
                nc.scalar.activation(z[:, 32 + i, :], z[:, 32 + i, :], ACT.Sigmoid,
                                     bias=k.v("b_gate", 16 * layer + i, 1)).then_inc(s.gates, 1)

        @block.vector
        def _(dve):
            chain = Chain(dve, s.chain)
            u = m1
            chain.link(nc.vector.tensor_tensor(u[:, :, :], z[:, 8:16, :], z[:, 16:24, :], ALU.mult))
            for i in range(DT):
                chain.add(nc.vector.tensor_scalar(ya[:, i, :], u[:, i, :], taps[:, i, 2:3], None, ALU.mult))
            chain.settle()
            for j in (1, 0):
                o = 2 - j
                for i in range(DT):
                    chain.add(nc.vector.scalar_tensor_tensor(ya[:, i, o:L], u[:, i, 0:L - o], taps[:, i, j:j + 1],
                                                             ya[:, i, o:L], ALU.mult, ALU.add))
                chain.settle()
            chain.add(nc.vector.tensor_tensor(ya[:, :, :], ya[:, :, :], z[:, 0:8, :], ALU.mult))
            src = z[:, 24:32, :]
            dst = m2
            for g in range(4):
                lo = 2 * g
                o = 1 << g
                chain.add(nc.vector.tensor_tensor(dst[:, lo:8, o:L], src[:, lo:8, o:L], src[:, lo:8, 0:L - o], ALU.add))
                chain.link(nc.vector.tensor_copy(dst[:, lo:8, 0:o], src[:, lo:8, 0:o]))
                if g == 0:
                    dve.wait_ge(s.counts, 16)
                part = pool[:, lo:lo + 2, :]
                chain.link(nc.vector.tensor_tensor(part, dst[:, lo:lo + 2, :],
                                                   counts[:, g:g + 1, :].broadcast_to([P, 2, L]), ALU.mult))
                chain.link(nc.vector.tensor_tensor(part, part, z[:, 24 + lo:26 + lo, :], ALU.subtract))
                src, dst = dst, (spare if dst is m2 else m2)

    pooled = m1
    def pool_bias(u, bank):
        for j in range(2):
            n = 2 * u + j
            ins = nc.vector.tensor_scalar(pooled[:, n, :], bank[:, j * L:(j + 1) * L],
                                          k.v("b_pool", 8 * layer + n, 1), k.v("pool_scale", 8 * layer + n, 1),
                                          ALU.add, ALU.mult)
        return ins

    with stage(k, "pool_group", "made", "stored") as (block, s):

        @block.tensor
        def _(pe):
            for g in range(4):
                for j in range(2):
                    for kk in range(2):
                        if kk == 0 and j == 0:
                            pe.wait_ge(w.w_pg.loaded[g], 16)
                        last = nc.tensor.matmul(k.bank[g][:, j * L:(j + 1) * L],
                                                k.ring[:, g, (2 * j + kk) * P:(2 * j + kk + 1) * P],
                                                pool[:, 2 * g + kk, :], start=kk == 0, stop=kk == 1)
                last.then_inc(s.made, 1)

        @block.vector
        def _(dve):
            for g in range(4):
                dve.wait_ge(s.made, g + 1)
                pool_bias(g, k.bank[g])

        @block.sync
        def _(sp):
            sp.wait_ge(s.made, 4)
            w.w_conv_out.prime(sp)

    w.w_pg.retire()

    def branch(dst, gate):
        def run(u, bank):
            for j in range(2):
                ins = nc.vector.tensor_tensor(tile_of(dst, u * 2 + j), bank[:, j * L:(j + 1) * L],
                                              tile_of(z, u * 2 + j + gate), ALU.mult)
            return ins
        return run

    split(k, "ya_halves", ya, DT, L)
    linear3(k, "conv_out", w.w_conv_out, DT, L, xs, branch(m2, 32), then=lambda sp: w.w_pool_out.prime(sp))
    split(k, "pool_halves", pooled, DT, L)
    linear3(k, "pool_out", w.w_pool_out, DT, L, xs, branch(spare, 40), then=lambda sp: w.w_o.prime(sp))
    with stage(k, "mix_add") as (block, s):

        @block.vector
        def _(dve):
            nc.vector.tensor_tensor(m2[:, :, :], m2[:, :, :], spare[:, :, :], ALU.add)

    y2 = k.big[:, base:base + 8 * L].rearrange("p (u n) -> p u n", n=T2)
    split(k, "mix_halves", m2, DT, L)
    linear3(k, "mix_o", w.w_o, DT, L, xs,
           lambda u, bank: nc.scalar.activation(tile_of(y2, u), bank[:, 0:T2], ACT.Copy), engine="scalar", then=then)
    norm(k, "mix_post", lambda i: ya[:, i, :], lambda i: k.h[:, i, 0:L], DT, L, D,
         gain=lambda i: [((0, L), k.v("mix_post", 8 * layer + i, 1))],
         residual=(lambda i: k.x[:, i, TOK:T2], 1.0))


def build_program(nc, io, out, stop=None):
    k = Core()
    k.nc, k.io, k.stage_no, k.spent = nc, io, 0, []
    k.big = nc.alloc_sbuf_tensor("big", [P, BIG], F32)
    k.x = nc.alloc_sbuf_tensor("x_all", [P, DT, T2], F32)
    k.h = nc.alloc_sbuf_tensor("h_all", [P, DT, T2], F32)
    k.ring = nc.alloc_sbuf_tensor("weight_ring", [P, RING, SLOT], F32)
    whole = k.h[:, :, :].rearrange("p n t -> p (n t)")
    half = DT * T2 // 2
    k.hh, k.hl = (whole[:, half * i:half * (i + 1)].bitcast(BF16).rearrange("p (n t) -> p n t", t=T2)
                  for i in range(2))
    k.mod = nc.alloc_sbuf_tensor("modulation", [P, 96, 2], F32)
    vec = nc.alloc_sbuf_tensor("vectors", [P, N_VEC], F32)
    res = nc.alloc_sbuf_tensor("resident_consts", [P, N_RESIDENT], F32)
    k.aux = nc.alloc_sbuf_tensor("aux", [P, AUX], F32)
    k.bank = [nc.alloc_psum_tensor(f"bank{i}", [P, 512], F32) for i in range(8)]

    def resident(name):
        a, n = CONST_AT[name]
        return res[:, a:a + n]

    k.ident, k.ones, k.iota, k.eps = (resident(n) for n in ("ident", "ones", "iota", "eps"))
    k.v = lambda name, off=0, n=None: vec[:, VEC_AT[name] + off:VEC_AT[name] + off + (n or dict(VECTORS)[name])]
    k.const = lambda name: io["consts"][:, CONST_AT[name][0]:CONST_AT[name][0] + CONST_AT[name][1]]
    k.view = lambda at, tiles, t: k.big[:, at:at + tiles * t].rearrange("p (n t) -> p n t", t=t)

    def parts(size, at=PARTS, buf=None):
        buf = k.big if buf is None else buf
        both = [buf[:, at + size * i:at + size * (i + 1)].bitcast(BF16) for i in range(RING)]
        return [b[:, 0:size] for b in both], [b[:, size:2 * size] for b in both]

    k.parts = parts

    def mod_at(layer, part, tile, half):
        n = tile + (48 * layer + 8 * part)
        if isinstance(n, int):
            return k.mod[:, n, half:half + 1]
        return k.mod[:, bass.ds(n, 1), half:half + 1].rearrange("p o t -> p (o t)")

    k.mod_at = mod_at

    def weights(name, kc, chunks, first=0):
        w = Weights(k, name, kc, chunks)
        prime = w.prime
        w.prime = lambda sp: prime(sp, first)
        return w

    w_ada = weights("w_ada", 8, 96)
    w_even_in = weights("w_even_in", 8, 29)
    w_even_out = weights("w_even_out", 8, 8)
    load(k, "inputs", [(k.x[:, :, CTX:L], io["ctx"]), (k.x[:, :, TOK:T2], io["x"]), (vec[:, :], io["vectors"]),
                       (res[:, :], io["consts"][:, 0:N_RESIDENT])], more=w_ada.prime)
    condition(k, w_ada)

    def finish(src):
        with stage(k, "store", "stored") as (block, s):
            @block.sync
            def _(sp):
                sp.dma_start(out, src).then_inc(s.stored, 16)
                sp.wait_ge(s.stored, 16)

    mod_norm(k, 0, False, (0, T2), prime=w_even_in.prime, whole=True)
    if stop == "norm1":
        return finish(k.h[:, :, :])
    even_mixer(k, w_even_in, w_even_out, None)
    if stop == "even":
        return finish(k.x[:, :, :])
    for first in (CTX, TOK):
        experts(k, 0, first, weights("w_peer_q", 8, 16, 0), None)
    if stop == "peer0":
        return finish(k.x[:, :, :])
    mod_norm(k, 1, False, (0, T2), whole=True)
    odd_mixer(k, weights("w_mla_in", 8, 6), weights("w_mla_uq", 3, 12), weights("w_mla_ukv", 2, 16),
              weights("w_mla_out", 8, 8), None)
    if stop == "mla":
        return finish(k.x[:, :, :])
    experts(k, 1, TOK, weights("w_peer_q", 8, 16, 16), None)
    norm(k, "final", lambda i: k.x[:, i, TOK:T2], lambda i: k.x[:, i, TOK:T2], DT, L, D,
         gain=lambda i: [((0, L), k.v("final_g", i, 1))], squares=lambda i: k.h[:, i, 0:L])
    if stop == "first":
        return finish(k.x[:, :, :])
    for layer in range(2):
        swiglu(k, layer, 1, weights("w_up1", 8, 44, 44 * layer), weights("w_down1", 11, 16, 16 * layer), None)
        if stop == "ffn1" and layer == 0:
            return finish(k.x[:, :, :])
        conv_pool_mixer(k, layer, MixerWeights(
            w_in=weights("w_in2", 8, 48, 48 * layer), w_pg=weights("w_pg", 4, 4, 4 * layer),
            w_conv_out=weights("w_conv_out", 8, 8, 8 * layer), w_pool_out=weights("w_pool_out", 8, 8, 8 * layer),
            w_o=weights("w_o", 8, 8, 8 * layer)), None)
        if stop == "mix" and layer == 0:
            return finish(k.x[:, :, :])
        swiglu(k, layer, 2, weights("w_up2", 8, 44, 44 * layer), weights("w_down2", 11, 16, 16 * layer), None)
    finish(k.x[:, :, TOK:T2])


def tiled(w, kc):
    kdim, n = w.shape
    if n % P:
        w = np.concatenate([w, np.zeros((kdim, P - n % P), w.dtype)], 1)
    kt, nt = kdim // P, w.shape[1] // P
    return np.ascontiguousarray(w.reshape(kt // kc, kc, P, nt, P).transpose(3, 0, 2, 1, 4)).reshape(
        nt * (kt // kc), P, kc * P)


def columns(v):
    return np.ascontiguousarray(v.reshape(-1, P).T)


def lay_out(a):
    a = {n: np.asarray(v) for n, v in a.items()}
    io = {}
    feature_major = lambda t: np.ascontiguousarray(t.reshape(L, DT, P).transpose(2, 1, 0))
    io["x"], io["ctx"] = feature_major(a["x"][0]), feature_major(a["ctx"][0])
    per_partition = lambda v: np.broadcast_to(v.reshape(1, -1), (P, v.size))
    taps = lambda w: np.ascontiguousarray(w.reshape(w.shape[0], -1, P).transpose(2, 1, 0)).reshape(P, -1)
    vectors = {
        "c": columns(a["c"]), "c_ctx": columns(a["c_ctx"]), "ada_b": columns(a["ada_b"]),
        "norm1_g": columns(a["norm1_g"]), "norm2_g": columns(a["norm2_g"]), "final_g": columns(a["final_g"]),
        "conv_w": taps(a["even_conv_w"][0]), "gdn_norm_g": columns(a["gdn_norm_g"]),
        "a_log": per_partition(a["gdn_a_log"]), "dt_bias": per_partition(a["gdn_dt_bias"]),
        "mla_q_g": columns(a["mla_q_g"]), "mla_kv_g": columns(a["mla_kv_g"]),
        "ffn1_pre": columns(a["ffn1_pre_2"]), "ffn1_post": columns(a["ffn1_post_2"]),
        "mix_pre": columns(a["mix_pre_2"]), "mix_post": columns(a["mix_post_2"]),
        "ffn2_pre": columns(a["ffn2_pre_2"]), "ffn2_post": columns(a["ffn2_post_2"]),
        "b_gate": columns(a["b_gate_2"]),
        "conv_w_2": np.concatenate([taps(a["conv_w_2"][i]) for i in range(2)], 1),
        "b_pool": columns(a["b_pool_group_2"]), "pool_scale": columns(a["pool_scale_2"]),
    }
    io["vectors"] = np.ascontiguousarray(np.concatenate([vectors[n] for n, _ in VECTORS], 1))
    io["consts"] = CONSTS
    w = a["ada_w"].reshape(2, 4, 2, P, 12, 512)
    io["w_ada"] = np.ascontiguousarray(w.transpose(0, 4, 1, 3, 2, 5)).reshape(96, P, 1024)
    io["w_even_in"] = tiled(a["even_w_in"][0], 8)
    io["w_even_out"] = tiled(a["even_w_out"][0], 8)
    rpb = a["na_rpb"][0]
    wide = np.pad(rpb, ((0, 0), (0, 0), (GRID_W - 16, GRID_W - 16)))
    by_col = np.stack([wide[:, :, GRID_W - 1 - c:2 * GRID_W - 1 - c] for c in range(GRID_W)], 2)
    rows = L // GRID_W
    bias = np.stack([by_col[:, 7 - r:7 - r + rows] for r in range(rows)], 1)
    io["na_bias"] = np.ascontiguousarray(bias.transpose(0, 1, 3, 2, 4)).reshape(HEADS, 2, P, L)
    w = a["mla_w_in"][0]
    io["w_mla_in"] = tiled(np.concatenate([w, w[:, 640:704]], 1), 8)
    w = a["mla_w_uq"][0].reshape(384, HEADS, 192)
    io["w_mla_uq"] = tiled(np.concatenate([w[:, :, :128].reshape(384, -1), w[:, :, 128:].reshape(384, -1)], 1), 3)
    w = a["mla_w_ukv"][0].reshape(256, HEADS, 256)
    io["w_mla_ukv"] = tiled(np.concatenate([w[:, :, :128].reshape(256, -1), w[:, :, 128:].reshape(256, -1)], 1), 2)
    io["w_mla_out"] = tiled(a["mla_w_out"][0], 8)
    both = lambda name, kc: np.concatenate([tiled(a[name][i], kc) for i in range(2)])
    io["w_peer_q"] = both("peer_w_q", 8)
    io["sub_keys"] = np.ascontiguousarray(a["peer_sub_keys"].reshape(2, 16, KEYS, P).transpose(0, 3, 1, 2)).reshape(2, P, -1)
    io["experts_u"] = np.ascontiguousarray(
        a["peer_u"].reshape(2, KEYS, KEYS, DT, P).transpose(0, 1, 4, 3, 2)).reshape(2 * KEYS, P, D)
    io["experts_v"] = np.ascontiguousarray(a["peer_v"].reshape(2 * KEYS, KEYS, D))
    for which in (1, 2):
        w = a[f"ffn{which}_w_gate_up_2"].reshape(2, D, 2, FF_T, P).transpose(0, 1, 3, 2, 4).reshape(2, D, 2 * D_FF)
        io[f"w_up{which}"] = np.concatenate([tiled(w[i], 8) for i in range(2)])
        io[f"w_down{which}"] = both(f"ffn{which}_w_down_2", 11)
    io["w_in2"] = both("w_in_2", 8)
    w = a["w_pool_group_2"].reshape(2, 4, 2, P, 2, P)
    io["w_pg"] = np.ascontiguousarray(w.transpose(0, 1, 3, 4, 2, 5)).reshape(8, P, 4 * P)
    io["w_conv_out"], io["w_pool_out"], io["w_o"] = both("w_conv_out_2", 8), both("w_pool_out_2", 8), both("w_o_2", 8)
    return io


def kernel(**inputs):
    import concourse.bacc as bacc
    from concourse.bass_utils import run_bass_kernel_spmd

    io = lay_out(inputs)
    nc = bacc.Bacc("TRN2", target_bir_lowering=False, num_devices=1)
    arrays = {f"in_{n}": v for n, v in io.items()}
    aps = {n: nc.dram_tensor(f"in_{n}", v.shape, mybir.dt.from_np(v.dtype), kind="ExternalInput").ap()
           for n, v in io.items()}
    out = nc.dram_tensor("out_features", (P, DT, L), F32, kind="ExternalOutput").ap()
    build_program(nc, aps, out)
    r = run_bass_kernel_spmd(nc, [arrays], core_ids=[0])
    y = np.asarray(r.results[0]["out_features"])
    return np.ascontiguousarray(y.transpose(2, 1, 0)).reshape(1, L, D)
```

```python
from collections import namedtuple
from contextlib import contextmanager

import numpy as np

import concourse.bass as bass
from concourse import mybir

F32 = mybir.dt.float32
BF16 = mybir.dt.bfloat16
U32 = mybir.dt.uint32
ACT = mybir.ActivationFunctionType
ALU = mybir.AluOpType
AX = mybir.AxisListType

P = 128
L = 256
T2 = 2 * L
D = 1024
DT = D // P
EPS = 1e-6
GRID_W = 64
HEADS = 8
NA_DH = 64
GDN_H = 4
CHUNK = 128
NCHUNK = T2 // CHUNK
LEVELS = 7
KEYS = 128
TOPK = 16
PAIRS = 4 * TOPK + 12 * 4
D_FF = 2816
FF_T = D_FF // P
POOL_WINDOWS = (2, 4, 8, 16)
RING = 4
SLOT = 11 * P
BIG = 32768
AUX = 5120
CTX, TOK = 0, L
PARTS = 24576
SCRATCH = 28672

VECTORS = [
    ("c", 8), ("c_ctx", 8), ("ada_b", 96), ("norm1_g", 16), ("norm2_g", 16), ("final_g", 8),
    ("conv_w", 60), ("gdn_norm_g", 1), ("a_log", 8), ("dt_bias", 8), ("mla_q_g", 3), ("mla_kv_g", 2),
    ("ffn1_pre", 16), ("ffn1_post", 16), ("mix_pre", 16), ("mix_post", 16), ("ffn2_pre", 16),
    ("ffn2_post", 16), ("b_gate", 32), ("conv_w_2", 48), ("b_pool", 16), ("pool_scale", 16),
]
VEC_AT = {}
_n = 0
for _name, _w in VECTORS:
    VEC_AT[_name] = _n
    _n += _w
N_VEC = _n

def constants():
    i = np.arange(P)
    parts = {}
    parts["ident"] = np.eye(P)
    parts["ones"] = np.ones((P, P))
    parts["iota"] = np.broadcast_to(i, (P, P))
    parts["eps"] = np.broadcast_to(np.array([EPS, 4 * EPS, P * EPS, 1.0]), (P, 4))
    parts["pair"] = i[:, None] % 2 == np.arange(2)[None, :]
    resident = sum(v.shape[1] for v in parts.values())
    parts["tri"] = np.concatenate([i[:, None] <= i[None, :], i[:, None] >= i[None, :]], 1)
    masks = []
    for d in range(2):
        for lev in range(LEVELS):
            b = 1 << lev
            m = (i[:, None] // (2 * b) == i[None, :] // (2 * b)) & (i[:, None] % (2 * b) >= b) & (i[None, :] % (2 * b) < b)
            masks.append(m if d == 0 else m.T)
    parts["levels"] = np.concatenate(masks, 1)
    start = np.clip(i % GRID_W - 8, 0, GRID_W - 16)[:, None]
    col = (np.arange(L) % GRID_W)[None, :]
    parts["window"] = np.where((col >= start) & (col < start + 16), 0.0, -1e30)
    inv = (10000.0 ** (-np.arange(0, 32, 2, dtype=np.float32) / 32)).astype(np.float32)
    t = np.arange(L)
    ar = (t // GRID_W).astype(np.float32)[:, None] * inv
    ac = (t % GRID_W).astype(np.float32)[:, None] * inv
    ang = np.concatenate([ar, ar, ac, ac], -1).T
    parts["cos"] = np.concatenate([np.cos(ang)] * 2, 0)
    parts["sin"] = np.concatenate([np.sin(ang)] * 2, 0)
    rot = np.zeros((P, P))
    for base in (0, 64):
        for blk in (0, 32):
            for j in range(16):
                rot[base + blk + 16 + j, base + blk + j] = -1.0
                rot[base + blk + j, base + blk + 16 + j] = 1.0
    parts["rot"] = rot
    parts["inv_count"] = np.concatenate(
        [np.broadcast_to(1.0 / np.minimum(t + 1, w), (P, L)) for w in POOL_WINDOWS], 1)
    at, n = {}, 0
    for name, v in parts.items():
        at[name] = (n, v.shape[1])
        n += v.shape[1]
    return np.ascontiguousarray(np.concatenate(list(parts.values()), 1).astype(np.float32)), at, resident


CONSTS, CONST_AT, N_RESIDENT = constants()


Unit = namedtuple("Unit", "q k keys v bias base dv out")
MixerWeights = namedtuple("MixerWeights", "w_in w_pg w_conv_out w_pool_out w_o")


class Core:
    pass


def at_least(eng, sem, value):
    if isinstance(value, int) and value <= 0:
        return
    eng.wait_ge(sem, value)


class Chain:

    def __init__(self, eng, sem):
        self.eng, self.sem, self.n = eng, sem, 0

    def add(self, ins):
        ins.then_inc(self.sem, 1)
        self.n += 1

    def settle(self):
        at_least(self.eng, self.sem, self.n)

    def link(self, ins):
        self.add(ins)
        self.settle()


@contextmanager
def stage(k, name, *signals):
    nc = k.nc
    k.stage_no += 1
    s = namedtuple("Signals", signals)(*(nc.alloc_semaphore(f"{name}_{k.stage_no}_{n}") for n in signals))
    with nc.Block() as block:
        yield block, s
    k.spent += list(s)
    if len(k.spent) > 130:
        nc.clear_and_free_semaphores(k.spent)
        nc.all_engine_barrier()
        k.spent = []


class Weights:

    def __init__(self, k, name, kc, chunks):
        self.k, self.dram, self.kc, self.chunks, self.name = k, k.io[name], kc, chunks, name
        self.loaded = None

    def load(self, sp, q, s):
        dst = self.k.ring[:, s, 0:self.kc * P]
        if isinstance(q, int):
            src = self.dram[self.first + q]
        else:
            src = self.dram[bass.ds(q + self.first, 1)].rearrange("o p n -> (o p) n")
        sp.dma_start(dst, src).then_inc(self.loaded[s], 16)

    def retire(self):
        self.k.spent += self.loaded

    def prime(self, sp, first=0):
        k = self.k
        self.first = first
        self.loaded = [k.nc.alloc_semaphore(f"{self.name}_loaded{s}_{k.stage_no}") for s in range(RING)]
        for q in range(min(RING, self.chunks)):
            self.load(sp, q, q)


def repeat(eng, rounds, body):
    if rounds > 0:
        body(0)
    if rounds > 1:
        with eng.Fori(1, rounds) as r:
            body(r)


def linear(k, name, w, kt, t, rhs, epilogue, engine="vector", then=None, body=None, lag=1):
    nc = k.nc
    per_tile = kt // w.kc
    c_unit = per_tile * (512 // t)
    units = w.chunks // c_unit
    body = body or min(4, max(2, units))
    rounds, tail = divmod(units, body)
    size = w.kc * P
    assert units * c_unit == w.chunks and (body * c_unit) % RING == 0
    hi, lo = k.parts(SLOT)
    with stage(k, name, "high", "low", "chunk_used", "bank_free") as (block, s):

        @block.sync
        def _(sp):
            if w.loaded is None:
                w.prime(sp)

            def refill(r):
                for slot in range(RING):
                    sp.wait_ge(s.low, r * RING + (slot + 1))
                    w.load(sp, r * RING + (slot + RING), slot)

            full, rest = divmod(max(w.chunks - RING, 0), RING)
            repeat(sp, full, refill)
            for slot in range(rest):
                sp.wait_ge(s.low, full * RING + slot + 1)
                w.load(sp, full * RING + slot + RING, slot)
            if then is not None:
                sp.wait_ge(s.low, w.chunks)
                then(sp)

        @block.tensor
        def _(pe):
            def unit(r, b):
                at_least(pe, s.bank_free, (r - 1) * body + (b + 1))
                for c in range(c_unit):
                    at = b * c_unit + c
                    slot = at % RING
                    tile, part = divmod(c, per_tile)
                    pe.wait_ge(s.low, r * (body * c_unit) + (at + 1))
                    for j in range(w.kc):
                        kk = part * w.kc + j
                        xh, xl = rhs(kk)
                        dst = k.bank[b][:, tile * t:(tile + 1) * t]
                        cols = slice(j * P, (j + 1) * P)
                        nc.tensor.matmul(dst, hi[slot][:, cols], xh, start=kk == 0, stop=False)
                        nc.tensor.matmul(dst, hi[slot][:, cols], xl, start=False, stop=False)
                        last = nc.tensor.matmul(dst, lo[slot][:, cols], xh, start=False, stop=kk == kt - 1)
                    last.then_inc(s.chunk_used, 1)

            repeat(pe, rounds, lambda r: [unit(r, b) for b in range(body)])
            for b in range(tail):
                unit(rounds, b)

        def split(eng, r, b):
            for c in range(c_unit):
                at = b * c_unit + c
                slot = at % RING
                if eng is nc.scalar:
                    eng.wait_ge(w.loaded[slot], r * (16 * body * c_unit // RING) + 16 * (at // RING + 1))
                    at_least(eng, s.chunk_used, r * (body * c_unit) + (at + 1 - RING))
                    nc.scalar.activation(hi[slot][:, 0:size], k.ring[:, slot, 0:size], ACT.Copy).then_inc(s.high, 1)
                else:
                    eng.wait_ge(s.high, r * (body * c_unit) + (at + 1))
                    nc.vector.tensor_tensor(lo[slot][:, 0:size], k.ring[:, slot, 0:size], hi[slot][:, 0:size],
                                            ALU.subtract).then_inc(s.low, 1)

        def empty(eng, r, b):
            eng.wait_ge(s.chunk_used, r * (body * c_unit) + (b + 1) * c_unit)
            epilogue(r * body + b, k.bank[b]).then_inc(s.bank_free, 1)

        def program(eng, empties):
            def round_(r):
                for b in range(body):
                    split(eng, r, b)
                    if empties and not (isinstance(r, int) and r == 0 and b == 0):
                        empty(eng, r if b else r - 1, b - 1 if b else body - 1)

            repeat(eng, rounds, round_)
            for b in range(tail):
                split(eng, rounds, b)
                if empties:
                    empty(eng, rounds if b else rounds - 1, b - 1 if b else body - 1)
            if empties:
                empty(eng, rounds if tail else rounds - 1, tail - 1 if tail else body - 1)

        @block.vector
        def _(dve):
            program(nc.vector, engine == "vector")

        @block.scalar
        def _(act):
            program(nc.scalar, engine == "scalar")
    w.retire()


def linear_exact(k, name, w, kt, t, rhs, epilogue, engine="vector", then=None):
    nc = k.nc
    per_tile = kt // w.kc
    tiles = 1 if t == 2 else 512 // t
    c_unit = per_tile * tiles
    units = w.chunks // c_unit
    body = max(2, RING // c_unit)
    rounds, tail = divmod(units, body)
    assert units * c_unit == w.chunks and (body * c_unit) % RING == 0
    with stage(k, name, "chunk_used", "bank_free") as (block, s):

        @block.sync
        def _(sp):
            if w.loaded is None:
                w.prime(sp)

            def refill(r):
                for slot in range(RING):
                    sp.wait_ge(s.chunk_used, r * RING + (slot + 1))
                    w.load(sp, r * RING + (slot + RING), slot)

            full, rest = divmod(max(w.chunks - RING, 0), RING)
            repeat(sp, full, refill)
            for slot in range(rest):
                sp.wait_ge(s.chunk_used, full * RING + slot + 1)
                w.load(sp, full * RING + slot + RING, slot)
            if then is not None:
                sp.wait_ge(s.chunk_used, w.chunks)
                then(sp)

        @block.tensor
        def _(pe):
            def unit(r, b):
                at_least(pe, s.bank_free, (r - 1) * body + (b + 1))
                for c in range(c_unit):
                    at = b * c_unit + c
                    slot = at % RING
                    tile, part = divmod(c, per_tile)
                    pe.wait_ge(w.loaded[slot], r * (16 * body * c_unit // RING) + 16 * (at // RING + 1))
                    for j in range(w.kc):
                        kk = part * w.kc + j
                        last = nc.tensor.matmul(k.bank[b][:, tile * t:(tile + 1) * t],
                                                k.ring[:, slot, j * P:(j + 1) * P],
                                                rhs(kk, r * body + b),
                                                start=kk == 0, stop=kk == kt - 1)
                    last.then_inc(s.chunk_used, 1)

            repeat(pe, rounds, lambda r: [unit(r, b) for b in range(body)])
            for b in range(tail):
                unit(rounds, b)

        def empty(eng):
            def unit(r, b):
                eng.wait_ge(s.chunk_used, r * (body * c_unit) + (b + 1) * c_unit)
                epilogue(r * body + b, k.bank[b]).then_inc(s.bank_free, 1)

            repeat(eng, rounds, lambda r: [unit(r, b) for b in range(body)])
            for b in range(tail):
                unit(rounds, b)

        if engine == "vector":
            @block.vector
            def _(dve):
                empty(dve)
        else:
            @block.scalar
            def _(act):
                empty(act)
    w.retire()

def split(k, name, src, tiles, t, hi=None, lo=None, then=None):
    nc = k.nc
    hi = k.hh if hi is None else hi
    lo = k.hl if lo is None else lo
    with stage(k, name, "high") as (block, s):

        @block.scalar
        def _(act):
            for i in range(tiles):
                nc.scalar.activation(hi[:, i, 0:t], src[:, i, :], ACT.Copy).then_inc(s.high, 1)

        @block.vector
        def _(dve):
            for i in range(tiles):
                dve.wait_ge(s.high, i + 1)
                nc.vector.tensor_tensor(lo[:, i, 0:t], src[:, i, :], hi[:, i, 0:t], ALU.subtract)


def tile_of(buf, n, lo=0, hi=None):
    hi = buf.shape[2] if hi is None else hi
    if isinstance(n, int):
        return buf[:, n, lo:hi]
    return buf[:, bass.ds(n, 1), lo:hi].rearrange("p o t -> p (o t)")


def load(k, name, pairs, more=None):
    with stage(k, name, "arrived") as (block, s):

        @block.sync
        def _(sp):
            for dst, src in pairs:
                sp.dma_start(dst, src).then_inc(s.arrived, 16)
            sp.wait_ge(s.arrived, 16 * len(pairs))
            if more is not None:
                more(sp)


def condition(k, w):
    nc = k.nc
    c2 = k.aux[:, 0:16].rearrange("p (t j) -> p t j", j=2)
    c4 = k.aux[:, 16:32].bitcast(BF16).rearrange("p (t j) -> p t j", j=4)
    rows = [k.big[0:4, 512 * i:512 * (i + 1)] for i in range(2)]
    units = 96 * P // 512
    size = 2 * 512
    hi, lo = k.parts(SLOT)
    slots = 2 * RING
    more = [size * (i + 1) for i in range(RING)]
    chunk = [k.ring[:, i, 0:size] for i in range(RING)] + [k.big[:, at:at + size] for at in more]
    with stage(k, "ada", "silu", "c_high", "c_low", "high", "low", "chunk_used", "row_out", "turned", "mod_out",
               "loaded_4", "loaded_5", "loaded_6", "loaded_7") as (block, s):

        loaded = w.loaded + [s.loaded_4, s.loaded_5, s.loaded_6, s.loaded_7]

        @block.sync
        def _(sp):
            for slot in range(RING, slots):
                sp.dma_start(chunk[slot], w.dram[slot]).then_inc(loaded[slot], 16)

            def refill(r):
                for slot in range(slots):
                    sp.wait_ge(s.low, r * slots + (slot + 1))
                    src = w.dram[r * slots + (slot + slots)] if isinstance(r, int) else \
                        w.dram[bass.ds(r * slots + (slot + slots), 1)].rearrange("o p n -> (o p) n")
                    sp.dma_start(chunk[slot], src).then_inc(loaded[slot], 16)

            repeat(sp, w.chunks // slots - 1, refill)

        @block.tensor
        def _(pe):
            pe.wait_ge(s.c_low, 1)

            def round_(r):
                for b in range(2):
                    at_least(pe, s.row_out, (r - 1) * 2 + (b + 1))
                    for c in range(RING):
                        pe.wait_ge(s.low, r * 8 + (4 * b + c + 1))
                        for j in range(2):
                            kk = 2 * c + j
                            cols = slice(512 * j, 512 * (j + 1))
                            nc.tensor.matmul(k.bank[b][0:4, :], c4[:, kk, :], hi[c][:, cols],
                                             start=kk == 0, stop=False)
                            last = nc.tensor.matmul(k.bank[b][0:4, :], c4[:, kk, :], lo[c][:, cols],
                                                    start=False, stop=kk == DT - 1)
                        last.then_inc(s.chunk_used, 1)
                    if not (isinstance(r, int) and r == 0 and b == 0):
                        turn(r if b else r - 1, 1 - b)

            def turn(r, b):
                pe.wait_ge(s.row_out, r * 2 + (b + 1))
                at_least(pe, s.mod_out, (r - 1) * 2 + (b + 1))
                for n in range(4):
                    last = nc.tensor.matmul(k.bank[2 + b][:, 2 * n:2 * n + 2], rows[b][:, n * P:(n + 1) * P],
                                            k.pair[0:4, :], start=True, stop=True)
                last.then_inc(s.turned, 1)

            repeat(pe, units // 2, round_)
            turn(units // 2 - 1, 1)

        @block.scalar
        def _(act):
            nc.scalar.activation(c2[:, :, 0], k.v("c_ctx"), ACT.Silu)
            nc.scalar.activation(c2[:, :, 1], k.v("c"), ACT.Silu).then_inc(s.silu, 1)
            act.wait_ge(s.silu, 1)
            nc.scalar.activation(c4[:, :, 0:2], c2, ACT.Copy).then_inc(s.c_high, 1)

            def round_(r):
                for b in range(2):
                    for c in range(RING):
                        act.wait_ge(loaded[4 * b + c], r * 16 + 16)
                        at_least(act, s.chunk_used, r * 8 + (4 * b + c - 3))
                        nc.scalar.activation(hi[c][:, 0:size], chunk[4 * b + c], ACT.Copy).then_inc(s.high, 1)
                    if not (isinstance(r, int) and r == 0 and b == 0):
                        row_out(r if b else r - 1, 1 - b)

            def row_out(r, b):
                act.wait_ge(s.chunk_used, r * 8 + (4 * b + 4))
                at_least(act, s.turned, (r - 1) * 2 + (b + 1))
                nc.scalar.activation(rows[b], k.bank[b][0:4, :], ACT.Copy).then_inc(s.row_out, 1)

            repeat(act, units // 2, round_)
            row_out(units // 2 - 1, 1)

        @block.vector
        def _(dve):
            dve.wait_ge(s.c_high, 1)
            nc.vector.tensor_tensor(c4[:, :, 2:4], c2, c4[:, :, 0:2], ALU.subtract).then_inc(s.c_low, 1)

            def round_(r):
                for q in range(8):
                    c = q % RING
                    dve.wait_ge(s.high, r * 8 + (q + 1))
                    nc.vector.tensor_tensor(lo[c][:, 0:size], chunk[q], hi[c][:, 0:size],
                                            ALU.subtract).then_inc(s.low, 1)
                    if c == RING - 1 and not (isinstance(r, int) and r == 0):
                        mod_out(r - 1, q // RING)

            def mod_out(r, b):
                dve.wait_ge(s.turned, r * 2 + (b + 1))
                at = bass.ds(r * 8 + 4 * b, 4)
                nc.vector.tensor_tensor(k.mod[:, at, :], k.bank[2 + b][:, 0:8].rearrange("p (n j) -> p n j", j=2),
                                        k.v("ada_b")[:, at].unsqueeze(2).broadcast_to([P, 4, 2]),
                                        ALU.add).then_inc(s.mod_out, 1)

            repeat(dve, units // 2, round_)
            for b in range(2):
                mod_out(units // 2 - 1, b)
    w.retire()
    with stage(k, "ada_gains") as (block, s):

        @block.vector
        def _(dve):
            for layer in range(2):
                for part, gain in ((1, "norm1_g"), (4, "norm2_g")):
                    sc = k.mod[:, 48 * layer + 8 * part:48 * layer + 8 * part + 8, :]
                    g = k.v(gain, 8 * layer, 8).unsqueeze(2).broadcast_to([P, 8, 2])
                    nc.vector.scalar_tensor_tensor(sc, sc, 1.0, g, ALU.add, ALU.mult)


def norm(k, name, src, dst, tiles, t, dim, gain, shift=None, residual=None, prime=None, squares=None,
         halves=None):
    nc = k.nc
    squares = squares or dst
    factor = residual[1] if residual else 1.0
    std, rstd = k.aux[:, 0:t], k.aux[:, 512:512 + t]
    stat = k.bank[7][:, 0:t]
    eps = {1.0: 0, 0.5: 1}[factor]
    with stage(k, name, "sq_a", "sq_v", "summed", "rooted", "scaled", "done", "shifted", "high") as (block, s):

        @block.scalar
        def _(act):
            for i in range(0, tiles, 2):
                nc.scalar.activation(squares(i), src(i), ACT.Square).then_inc(s.sq_a, 1)
            act.wait_ge(s.summed, 1)
            nc.scalar.activation(std, stat, ACT.Sqrt, bias=k.eps[:, eps:eps + 1],
                                 scale=1.0 / (dim * factor * factor)).then_inc(s.rooted, 1)
            if shift is not None:
                for i in range(tiles):
                    act.wait_ge(s.scaled, i + 1)
                    for (lo, hi), sh in shift(i):
                        nc.scalar.activation(dst(i)[:, lo:hi], dst(i)[:, lo:hi], ACT.Identity,
                                             bias=sh).then_inc(s.shifted, 1)
                    if halves is not None:
                        act.wait_ge(s.shifted, (i + 1) * len(shift(0)))
                        nc.scalar.activation(halves(i)[0], dst(i), ACT.Copy).then_inc(s.high, 1)
            elif halves is not None:
                for i in range(tiles):
                    act.wait_ge(s.scaled, i + 1)
                    nc.scalar.activation(halves(i)[0], dst(i), ACT.Copy).then_inc(s.high, 1)

        @block.vector
        def _(dve):
            for i in range(1, tiles, 2):
                nc.vector.tensor_tensor(squares(i), src(i), src(i), ALU.mult).then_inc(s.sq_v, 1)
            dve.wait_ge(s.rooted, 1)
            nc.vector.reciprocal(rstd, std).then_inc(s.done, 1)
            dve.wait_ge(s.done, 1)
            for i in range(tiles):
                parts = gain(i)
                for n, ((lo, hi), g) in enumerate(parts):
                    ins = nc.vector.scalar_tensor_tensor(dst(i)[:, lo:hi], src(i)[:, lo:hi], g,
                                                         rstd[:, lo:hi], ALU.mult, ALU.mult)
                    if n == len(parts) - 1:
                        ins.then_inc(s.scaled, 1)
            if halves is not None:
                for i in range(tiles):
                    dve.wait_ge(s.high, i + 1)
                    nc.vector.tensor_tensor(halves(i)[1], dst(i), halves(i)[0], ALU.subtract)
            if residual is not None:
                for i in range(tiles):
                    dve.wait_ge(s.scaled, i + 1)
                    x = residual[0](i)
                    nc.vector.tensor_tensor(x, x, dst(i), ALU.add)

        @block.tensor
        def _(pe):
            for i in range(tiles):
                pe.wait_ge(s.sq_v if i % 2 else s.sq_a, i // 2 + 1)
                last = nc.tensor.matmul(stat, k.ones, squares(i), start=i == 0, stop=i == tiles - 1)
            last.then_inc(s.summed, 1)

        @block.sync
        def _(sp):
            if prime is not None:
                prime(sp)


def spread_columns(nc, k, columns, rows):
    for g in range(columns.shape[1]):
        last = nc.tensor.matmul(rows[:, g * P:(g + 1) * P], columns[:, g:g + 1].broadcast_to([P, P]), k.ident,
                                start=True, stop=True)
    return last


def halves_of_h(k, t):
    return lambda i: (k.hh[:, i, 0:t], k.hl[:, i, 0:t])


def mod_norm(k, layer, second, halves, prime=None, exact=False):
    part = 3 if second else 0
    lo, hi = halves
    base = 48 * layer + 8 * part

    def scalars(chunk):
        def at(i):
            out = []
            if lo < L:
                out.append(((0, L), k.mod[:, base + 8 * chunk + i, 0:1]))
            if hi > L:
                out.append(((L - lo, hi - lo), k.mod[:, base + 8 * chunk + i, 1:2]))
            return out
        return at

    wide = k.view(SCRATCH, DT, hi - lo)
    norm(k, "mod_norm", lambda i: k.x[:, i, lo:hi], lambda i: k.h[:, i, :] if exact else wide[:, i, :], DT, hi - lo, D,
         gain=scalars(1), shift=scalars(0), prime=prime, halves=None if exact else halves_of_h(k, hi - lo))


def transposes(k, name, jobs):
    nc = k.nc
    with stage(k, name, "turned", "copied") as (block, s):

        @block.tensor
        def _(pe):
            for n, (src, _) in enumerate(jobs):
                at_least(pe, s.copied, n - 3)
                nc.tensor.transpose(k.bank[n % 4][:, 0:P], src, k.ident).then_inc(s.turned, 1)

        @block.vector
        def _(dve):
            for n, (_, dst) in enumerate(jobs):
                dve.wait_ge(s.turned, n + 1)
                nc.vector.tensor_copy(dst, k.bank[n % 4][:, 0:P]).then_inc(s.copied, 1)


def attention(k, name, units, scale, scratch, prime=None):
    nc = k.nc
    at = [scratch]

    def take(n):
        at[0] += n
        return k.big[:, at[0] - n:at[0]]

    score = [take(512) for _ in range(2)]
    prob = [take(512) for _ in range(2)]
    prob_t = [take(512) for _ in range(2)]
    bias = [take(L) for _ in range(2)]
    stat = [take(8) for _ in range(2)]
    n_units = len(units)
    biased = units[0].bias is not None
    exp_scale = 1.0 if biased else scale
    with stage(k, name, "scored", "maxed", "expd", "normed", "turned", "probs_t", "mixed", "stored",
               "chain", "bias_0", "bias_1", "bias_ready") as (block, s):
        bias_loaded = [s.bias_0, s.bias_1]

        @block.sync
        def _(sp):
            if biased:
                for u, un in enumerate(units):
                    at_least(sp, s.maxed, u - 1)
                    sp.dma_start(bias[u % 2], un.bias).then_inc(bias_loaded[u % 2], 16)
            if prime is not None:
                prime(sp)

        @block.gpsimd
        def _(pool):
            if biased:
                for u in range(n_units):
                    pool.wait_ge(bias_loaded[u % 2], 16 * (u // 2 + 1))
                    nc.gpsimd.tensor_tensor(bias[u % 2], bias[u % 2], k.window, ALU.add).then_inc(s.bias_ready, 1)

        @block.tensor
        def _(pe):
            def scores(u):
                un = units[u]
                at_least(pe, s.expd, u - 1)
                for j, (q, key) in enumerate(zip(un.q, un.k)):
                    last = nc.tensor.matmul(k.bank[u % 2][:, 0:un.keys], q, key,
                                            start=j == 0, stop=j == len(un.q) - 1)
                last.then_inc(s.scored, 1)

            def mix(u):
                un = units[u]
                pe.wait_ge(s.probs_t, u + 1)
                at_least(pe, s.stored, u - 1)
                n = un.keys // P
                for j in range(n):
                    last = nc.tensor.matmul(k.bank[4 + u % 2][un.base:un.base + un.dv, 0:P], un.v[j],
                                            prob_t[u % 2][:, j * P:(j + 1) * P], start=j == 0, stop=j == n - 1)
                last.then_inc(s.mixed, 1)

            scores(0)
            scores(1)
            for u in range(n_units):
                pe.wait_ge(s.normed, u + 1)
                at_least(pe, s.probs_t, u - 1)
                for j in range(units[u].keys // P):
                    last = nc.tensor.transpose(k.bank[2 + u % 2][:, j * P:(j + 1) * P],
                                               prob[u % 2][:, j * P:(j + 1) * P], k.ident)
                last.then_inc(s.turned, 1)
                if u >= 1:
                    mix(u - 1)
                if u + 2 < n_units:
                    scores(u + 2)
            mix(n_units - 1)

        @block.scalar
        def _(act):
            def expd(u):
                un = units[u]
                src = score[u % 2] if biased else k.bank[u % 2]
                act.wait_ge(s.maxed, u + 1)
                at_least(act, s.turned, u - 1)
                nc.scalar.activation(prob[u % 2][:, 0:un.keys], src[:, 0:un.keys], ACT.Exp, scale=exp_scale,
                                     bias=stat[u % 2][:, 1:2], accum_out=stat[u % 2][:, 2:3]).then_inc(s.expd, 1)

            def store(u):
                un = units[u]
                act.wait_ge(s.mixed, u + 1)
                nc.scalar.activation(un.out, k.bank[4 + u % 2][un.base:un.base + un.dv, 0:P],
                                     ACT.Copy).then_inc(s.stored, 1)

            expd(0)
            expd(1)
            for u in range(n_units):
                n = units[u].keys
                act.wait_ge(s.turned, u + 1)
                at_least(act, s.mixed, u - 1)
                nc.scalar.activation(prob_t[u % 2][:, 0:n], k.bank[2 + u % 2][:, 0:n],
                                     ACT.Copy).then_inc(s.probs_t, 1)
                if u >= 1:
                    store(u - 1)
                if u + 2 < n_units:
                    expd(u + 2)
            store(n_units - 1)

        @block.vector
        def _(dve):
            chain = Chain(dve, s.chain)

            def maxima(u):
                un = units[u]
                bank, st = k.bank[u % 2], stat[u % 2]
                dve.wait_ge(s.scored, u + 1)
                at_least(dve, s.expd, u - 1)
                src = bank
                if biased:
                    dve.wait_ge(s.bias_ready, u + 1)
                    src = score[u % 2]
                    chain.add(nc.vector.tensor_scalar(src[:, 0:L], bank[:, 0:L], scale, None, ALU.mult))
                    chain.link(nc.vector.scalar_tensor_tensor(src[:, L:T2], bank[:, L:T2], scale, bias[u % 2],
                                                              ALU.mult, ALU.add))
                chain.link(nc.vector.reduce_max(st[:, 0:1], src[:, 0:un.keys], AX.X))
                nc.vector.tensor_scalar(st[:, 1:2], st[:, 0:1], -exp_scale, None, ALU.mult).then_inc(s.maxed, 1)

            for u in range(n_units):
                maxima(u)
                st = stat[u % 2]
                dve.wait_ge(s.expd, u + 1)
                chain.link(nc.vector.reciprocal(st[:, 3:4], st[:, 2:3]))
                n = units[u].keys
                nc.vector.tensor_scalar(prob[u % 2][:, 0:n], prob[u % 2][:, 0:n], st[:, 3:4], None,
                                        ALU.mult).then_inc(s.normed, 1)


EVEN_P = 0
EVEN_Y = 29 * T2
EVEN_WORK = EVEN_Y + 8 * T2


def even_mixer(k, w_in, w_out, then):
    nc = k.nc
    p = k.view(EVEN_P, 29, T2)
    y = k.view(EVEN_Y, 8, T2)

    xs = lambda kk: (k.hh[:, kk, :], k.hl[:, kk, :])
    linear_exact(k, "even_in", w_in, DT, T2, lambda kk, u: k.h[:, kk, :],
           lambda u, bank: nc.scalar.activation(tile_of(p, u), bank[:, 0:T2], ACT.Copy), engine="scalar",
           then=lambda sp: w_out.prime(sp))

    v_tok = k.view(EVEN_WORK, NCHUNK, 512)
    transposes(k, "na_v", [(p[:, 8 + f, c * P:(c + 1) * P], v_tok[:, c, f * P:(f + 1) * P])
                           for c in range(NCHUNK) for f in range(4)])
    load(k, "window", [(k.aux[:, 0:L], k.const("window"))])
    k.window = k.aux[:, 0:L]
    for first in (TOK, CTX):
        units = []
        for head in range(HEADS):
            base, tile = NA_DH * (head % 2), head // 2
            rows = slice(base, base + NA_DH)
            for qt in range(2):
                cols = slice(first + qt * P, first + (qt + 1) * P)
                keys = T2 if first == TOK else L
                units.append(Unit(
                    q=[p[rows, tile, cols]], k=[p[rows, 4 + tile, 0:keys]], keys=keys,
                    v=[v_tok[:, c, head * NA_DH:(head + 1) * NA_DH] for c in range(keys // P)],
                    bias=k.io["na_bias"][head, qt] if first == TOK else None,
                    base=base, dv=NA_DH, out=y[rows, tile, cols]))
        attention(k, "na", units, NA_DH ** -0.5, EVEN_WORK + NCHUNK * 512)

    gated_delta(k, p, y)

    def add_residual(u, bank):
        for half, lo in ((0, CTX), (1, TOK)):
            x = tile_of(k.x, u, lo, lo + L)
            ins = nc.vector.scalar_tensor_tensor(x, bank[:, lo:lo + L], k.mod_at(0, 2, u, half), x,
                                                 ALU.mult, ALU.add)
        return ins

    split(k, "even_halves", y, DT, T2)
    linear(k, "even_out", w_out, DT, T2, xs, add_residual, then=then)


def gated_delta(k, p, y):
    nc = k.nc
    conv_w = k.v("conv_w").rearrange("p (t j) -> p t j", j=5)
    with stage(k, "conv", "chain", "conved") as (block, s):

        @block.vector
        def _(dve):
            chain = Chain(dve, s.chain)
            for quad in range(3):
                for j in (2, 0, 1, 3, 4):
                    for t in range(4 * quad, 4 * quad + 4):
                        src = p[:, 12 + t, :].rearrange("p (h n) -> p h n", h=2)
                        dst = p[:, t, :].rearrange("p (h n) -> p h n", h=2)
                        tap = conv_w[:, t, j:j + 1]
                        if j == 2:
                            ins = nc.vector.tensor_scalar(dst, src, tap, None, ALU.mult)
                        else:
                            o = j - 2
                            a, b = max(0, -o), L - max(0, o)
                            ins = nc.vector.scalar_tensor_tensor(dst[:, :, a:b], src[:, :, a + o:b + o], tap,
                                                                 dst[:, :, a:b], ALU.mult, ALU.add)
                        if j == 4:
                            ins.then_inc(s.conved, 1)
                        else:
                            chain.add(ins)
                    if j != 4:
                        chain.settle()

        @block.scalar
        def _(act):
            for t in range(12):
                act.wait_ge(s.conved, t + 1)
                nc.scalar.activation(p[:, t, :], p[:, t, :], ACT.Silu)

    sq = k.view(EVEN_WORK, 8, T2)
    norms, inverse = k.aux[:, 0:32], k.aux[:, 32:64]
    sums = k.bank[0][:, 0:32]
    with stage(k, "l2norm", "squared", "summed", "rooted", "inverted", "spread") as (block, s):

        @block.vector
        def _(dve):
            for t in range(8):
                nc.vector.tensor_tensor(sq[:, t, :], p[:, t, :], p[:, t, :], ALU.mult).then_inc(s.squared, 1)
            dve.wait_ge(s.rooted, 2)
            nc.vector.reciprocal(inverse, norms).then_inc(s.inverted, 1)
            for t in range(8):
                dve.wait_ge(s.spread, t + 1)
                nc.vector.tensor_tensor(p[:, t, :], p[:, t, :], k.bank[t][:, :], ALU.mult)

        @block.tensor
        def _(pe):
            for t in range(8):
                pe.wait_ge(s.squared, t + 1)
                for c in range(NCHUNK):
                    last = nc.tensor.matmul(sums[:, 4 * t + c:4 * t + c + 1], sq[:, t, c * P:(c + 1) * P],
                                            k.ones[:, 0:1], start=True, stop=True)
            last.then_inc(s.summed, 1)
            pe.wait_ge(s.inverted, 1)
            for t in range(8):
                spread_columns(nc, k, inverse[:, 4 * t:4 * t + 4], k.bank[t][:, :]).then_inc(s.spread, 1)

        @block.scalar
        def _(act):
            act.wait_ge(s.summed, 1)
            for lo, eps, factor in ((0, 2, float(P)), (16, 0, 1.0)):
                nc.scalar.activation(norms[:, lo:lo + 16], sums[:, lo:lo + 16], ACT.Sqrt, bias=k.eps[:, eps:eps + 1],
                                     scale=factor).then_inc(s.rooted, 1)

    k_tok = k.view(12 * T2, NCHUNK, 512)
    v_tok = k.view(16 * T2, NCHUNK, 512)
    out = k.view(20 * T2, GDN_H, T2)
    gate_t = k.view(EVEN_WORK, NCHUNK, P)
    transposes(k, "gdn_turn",
               [(p[:, 28, c * P:(c + 1) * P], gate_t[:, c, :]) for c in range(NCHUNK)]
               + [(p[:, 4 + h, c * P:(c + 1) * P], k_tok[:, c, h * P:(h + 1) * P])
                  for c in range(NCHUNK) for h in range(GDN_H)]
               + [(p[:, 8 + h, c * P:(c + 1) * P], v_tok[:, c, h * P:(h + 1) * P])
                  for c in range(NCHUNK) for h in range(GDN_H)])

    names = ["a", "beta", "abs", "e", "g", "gc", "eg", "total", "k_end", "s_end", "nbeg"]
    tok = {n: k.aux[:, 32 * i:32 * (i + 1)].rearrange("p (c d) -> p c d", d=8) for i, n in enumerate(names)}
    levels = k.aux[:, 512:512 + 2 * LEVELS * P].rearrange("p (l n) -> p l n", n=P)
    tri = k.aux[:, 2304:2304 + 2 * P]
    state = [k.aux[:, 2560 + 512 * d:3072 + 512 * d].rearrange("p (h n) -> p h n", h=GDN_H) for d in range(2)]
    with stage(k, "gates", "tables", "a_ready", "act", "chain", "cumsum") as (block, s):

        @block.sync
        def _(sp):
            sp.dma_start(tri, k.const("tri")).then_inc(s.tables, 16)
            sp.dma_start(levels[:, :, :], k.const("levels").rearrange("p (l n) -> p l n", n=P)).then_inc(s.tables, 16)
            sp.wait_ge(s.tables, 32)

        @block.vector
        def _(dve):
            chain = Chain(dve, s.chain)
            for d in range(2):
                chain.add(nc.vector.tensor_copy(tok["a"][:, :, 4 * d:4 * d + 4], gate_t[:, :, 8 * d:8 * d + 4]))
            chain.settle()
            dt = k.v("dt_bias").unsqueeze(1).broadcast_to([P, NCHUNK, 8])
            nc.vector.tensor_tensor(tok["a"], tok["a"], dt, ALU.add).then_inc(s.a_ready, 1)
            dve.wait_ge(s.act, 6)
            dve.wait_ge(s.a_ready, 1)
            chain.link(nc.vector.scalar_tensor_tensor(tok["e"], tok["a"], 0.0, tok["e"], ALU.max, ALU.add))
            ea = k.aux[:, 384:392].unsqueeze(1).broadcast_to([P, NCHUNK, 8])
            chain.link(nc.vector.scalar_tensor_tensor(tok["g"], tok["e"], -1.0, ea, ALU.mult, ALU.mult))
            dve.wait_ge(s.cumsum, 1)
            sums = k.bank[0][:, 0:64]
            for d in range(2):
                src = sums[:, 16 * d:16 * d + 16].rearrange("p (c h) -> p c h", h=4)
                chain.add(nc.vector.tensor_copy(tok["gc"][:, :, 4 * d:4 * d + 4], src))
            chain.link(nc.vector.tensor_copy(tok["total"], sums[:, 32:64].rearrange("p (c d) -> p c d", d=8)))
            chain.link(nc.vector.tensor_tensor(tok["k_end"], tok["total"], tok["gc"], ALU.subtract))
            dve.wait_ge(s.act, 9)
            nc.vector.scalar_tensor_tensor(tok["nbeg"], tok["beta"], -1.0, tok["eg"], ALU.mult, ALU.mult)
            for d in range(2):
                nc.vector.memset(state[d], 0.0)
            nc.vector.memset(out[:, :, :], 0.0)

        @block.scalar
        def _(act):
            for d in range(2):
                nc.scalar.activation(tok["beta"][:, :, 4 * d:4 * d + 4], gate_t[:, :, 8 * d + 4:8 * d + 8],
                                     ACT.Sigmoid).then_inc(s.act, 1)
            act.wait_ge(s.a_ready, 1)
            nc.scalar.activation(tok["abs"], tok["a"], ACT.Abs).then_inc(s.act, 1)
            act.wait_ge(s.act, 3)
            nc.scalar.activation(tok["e"], tok["abs"], ACT.Exp, scale=-1.0).then_inc(s.act, 1)
            nc.scalar.activation(k.aux[:, 384:392], k.v("a_log"), ACT.Exp).then_inc(s.act, 1)
            act.wait_ge(s.act, 4)
            nc.scalar.activation(tok["e"], tok["e"], ACT.Ln, bias=k.eps[:, 3:4]).then_inc(s.act, 1)
            act.wait_ge(s.chain, 8)
            nc.scalar.activation(tok["eg"], tok["gc"], ACT.Exp).then_inc(s.act, 1)
            nc.scalar.activation(tok["s_end"], tok["total"], ACT.Exp).then_inc(s.act, 1)
            nc.scalar.activation(tok["k_end"], tok["k_end"], ACT.Exp).then_inc(s.act, 1)

        @block.tensor
        def _(pe):
            pe.wait_ge(s.tables, 32)
            pe.wait_ge(s.chain, 4)
            for d in range(2):
                nc.tensor.matmul(k.bank[0][:, 16 * d:16 * d + 16], tri[:, d * P:(d + 1) * P],
                                 tok["g"][:, :, 4 * d:4 * d + 4], start=True, stop=True)
            nc.tensor.matmul(k.bank[0][:, 32:64], k.ones, tok["g"], start=True, stop=True).then_inc(s.cumsum, 1)

    delta_rule(k, p, k_tok, v_tok, out, tok, levels, tri, state)

    z = p[:, 24:28, :]
    sq = k.view(EVEN_WORK, GDN_H, T2)
    norms, inverse = k.aux[:, 0:16], k.aux[:, 16:32]
    sums = k.bank[4][:, 0:16]
    with stage(k, "gdn_out", "squared", "summed", "gated", "rooted", "inverted", "spread", "scaled") as (block, s):

        @block.vector
        def _(dve):
            for h in range(GDN_H):
                nc.vector.tensor_tensor(sq[:, h, :], out[:, h, :], out[:, h, :], ALU.mult).then_inc(s.squared, 1)
            dve.wait_ge(s.rooted, 1)
            nc.vector.reciprocal(inverse, norms).then_inc(s.inverted, 1)
            for h in range(GDN_H):
                dve.wait_ge(s.spread, h + 1)
                nc.vector.scalar_tensor_tensor(out[:, h, :], out[:, h, :], k.v("gdn_norm_g"), k.bank[h][:, :],
                                               ALU.mult, ALU.mult).then_inc(s.scaled, 1)
            dve.wait_ge(s.gated, 1)
            for h in range(GDN_H):
                dve.wait_ge(s.scaled, h + 1)
                nc.vector.tensor_tensor(y[:, 4 + h, :], out[:, h, :], z[:, h, :], ALU.mult)

        @block.tensor
        def _(pe):
            for h in range(GDN_H):
                pe.wait_ge(s.squared, h + 1)
                for c in range(NCHUNK):
                    last = nc.tensor.matmul(sums[:, 4 * h + c:4 * h + c + 1], sq[:, h, c * P:(c + 1) * P],
                                            k.ones[:, 0:1], start=True, stop=True)
            last.then_inc(s.summed, 1)
            pe.wait_ge(s.inverted, 1)
            for h in range(GDN_H):
                spread_columns(nc, k, inverse[:, 4 * h:4 * h + 4], k.bank[h][:, :]).then_inc(s.spread, 1)

        @block.scalar
        def _(act):
            nc.scalar.activation(z, z, ACT.Silu).then_inc(s.gated, 1)
            act.wait_ge(s.summed, 1)
            nc.scalar.activation(norms, sums, ACT.Sqrt, bias=k.eps[:, 0:1], scale=1.0 / P).then_inc(s.rooted, 1)


def delta_rule(k, p, k_tok, v_tok, out, tok, levels, tri, state):
    nc = k.nc
    H4 = range(GDN_H)
    bufs = ["x", "xt", "z", "am", "a", "pt", "exp_r", "dec_t", "kend", "bv", "qdec", "r", "u"]
    w = [{n: k.big[:, EVEN_WORK + 512 * (13 * d + i):EVEN_WORK + 512 * (13 * d + i + 1)]
          .rearrange("p (h n) -> p h n", h=GDN_H) for i, n in enumerate(bufs)} for d in range(2)]
    bank = [[k.bank[4 * d + n][:, :].rearrange("p (h n) -> p h n", h=GDN_H) for n in range(4)] for d in range(2)]
    am = [[w[d]["am"], k.h[:, d, :].rearrange("p (h n) -> p h n", h=GDN_H)] for d in range(2)]

    def part(v, lev, second):
        pairs = v.rearrange("p h n -> p (h n)").rearrange("p (m s b) -> p m s b", s=2, b=1 << lev)
        return pairs[:, :, second, :]

    order = [[0, 1, 2, 3], [1, 0, 3, 2]]
    steps = [(i, d, order[d][i]) for i in range(NCHUNK) for d in range(2)]
    with stage(k, "delta", "mats", "exp_r", "clamped", "decays", "qk_ready", "pool", "masked", "z_made", "z_copied",
               "deltas", "grown", "ks", "rhs", "u_made", "u_copied", "out_made", "s_made", "out_added",
               "s_done", "chain") as (block, s):

        def cols(c):
            return slice(c * P, (c + 1) * P)

        @block.tensor
        def _(pe):
            for i in range(NCHUNK):
                for d in range(2):
                    n, c, b = 2 * i + d, order[d][i], bank[d]
                    at_least(pe, s.out_added, n - 1)
                    for h in H4:
                        nc.tensor.matmul(b[0][:, h, :], tok["g"][:, c, 4 * d + h:4 * d + h + 1].broadcast_to([P, P]),
                                         tri[:, d * P:(d + 1) * P], start=True, stop=True)
                    for h in H4:
                        nc.tensor.matmul(b[1][:, h, :], p[:, 4 + h, cols(c)], p[:, 4 + h, cols(c)],
                                         start=True, stop=True)
                    for h in H4:
                        last = nc.tensor.matmul(b[2][:, h, :], p[:, 4 + h, cols(c)], p[:, h, cols(c)],
                                                start=True, stop=True)
                    last.then_inc(s.mats, 1)
                for d in range(2):
                    pe.wait_ge(s.masked, (i * LEVELS) * 2 + d + 1)
                    for h in H4:
                        last = nc.tensor.matmul(bank[d][1][:, h, :], am[d][0][:, h, :], k.ident,
                                                start=True, stop=True)
                    last.then_inc(s.deltas, 1)
                for lev in range(1, LEVELS):
                    for d in range(2):
                        pe.wait_ge(s.masked, (i * LEVELS + lev) * 2 + d + 1)
                        pe.wait_ge(s.grown, (i * LEVELS + lev - 1) * 2 + d + 1)
                        for h in H4:
                            last = nc.tensor.matmul(bank[d][0][:, h, :], am[d][lev % 2][:, h, :],
                                                    w[d]["xt"][:, h, :], start=True, stop=True)
                        last.then_inc(s.z_made, 1)
                    for d in range(2):
                        z = w[d]["z"]
                        pe.wait_ge(s.z_copied, (i * (LEVELS - 1) + lev - 1) * 2 + d + 1)
                        for h in H4:
                            last = nc.tensor.matmul(bank[d][1][:, h, :], w[d]["x"][:, h, :],
                                                    z[:, h, :], start=True, stop=True)
                        if lev < LEVELS - 1:
                            for h in H4:
                                last = nc.tensor.matmul(bank[d][2][:, h, :], z[:, h, :],
                                                        w[d]["x"][:, h, :], start=True, stop=True)
                        last.then_inc(s.deltas, 1)
                for d in range(2):
                    n, c = 2 * i + d, order[d][i]
                    at_least(pe, s.s_done, n - 1)
                    for h in H4:
                        last = nc.tensor.matmul(bank[d][0][:, h, :], p[:, 4 + h, cols(c)], state[d][:, h, :],
                                                start=True, stop=True)
                    last.then_inc(s.ks, 1)
                for d in range(2):
                    n, c = 2 * i + d, order[d][i]
                    pe.wait_ge(s.rhs, n + 1)
                    pe.wait_ge(s.grown, (i * LEVELS + LEVELS - 1) * 2 + d + 1)
                    for h in H4:
                        last = nc.tensor.matmul(bank[d][1][:, h, :], w[d]["xt"][:, h, :], w[d]["r"][:, h, :],
                                                start=True, stop=True)
                    last.then_inc(s.u_made, 1)
                for d in range(2):
                    n, c = 2 * i + d, order[d][i]
                    pe.wait_ge(s.u_copied, n + 1)
                    pe.wait_ge(s.pool, n + 1)
                    pe.wait_ge(s.qk_ready, n + 1)
                    for h in H4:
                        nc.tensor.matmul(bank[d][2][:, h, :], state[d][:, h, :], w[d]["qdec"][:, h, :],
                                         start=True, stop=False)
                        last = nc.tensor.matmul(bank[d][2][:, h, :], w[d]["u"][:, h, :], w[d]["pt"][:, h, :],
                                                start=False, stop=True)
                    last.then_inc(s.out_made, 1)
                    for h in H4:
                        last = nc.tensor.matmul(bank[d][3][:, h, :], w[d]["kend"][:, h, :], w[d]["u"][:, h, :],
                                                start=True, stop=True)
                    last.then_inc(s.s_made, 1)

        @block.scalar
        def _(act):
            for i in range(NCHUNK):
                for d in range(2):
                    n = 2 * i + d
                    act.wait_ge(s.clamped, n + 1)
                    at_least(act, s.pool, n - 1)
                    nc.scalar.activation(w[d]["exp_r"], bank[d][0], ACT.Exp).then_inc(s.exp_r, 1)
                for d in range(2):
                    nc.scalar.activation(w[d]["a"], w[d]["a"], ACT.Exp, scale=-1.0)
                    nc.scalar.activation(w[d]["dec_t"], w[d]["dec_t"], ACT.Exp).then_inc(s.decays, 1)
                for lev in range(1, LEVELS):
                    for d in range(2):
                        m = (i * (LEVELS - 1) + lev - 1) * 2 + d
                        act.wait_ge(s.z_made, m + 1)
                        at_least(act, s.deltas, (i * LEVELS + lev - 1) * 2 + d + 1 if lev > 1 else
                                 (i * LEVELS - 1) * 2 + d + 1)
                        nc.scalar.activation(w[d]["z"], bank[d][0], ACT.Copy).then_inc(s.z_copied, 1)
                for d in range(2):
                    n = 2 * i + d
                    act.wait_ge(s.u_made, n + 1)
                    at_least(act, s.s_made, n - 1)
                    nc.scalar.activation(w[d]["u"], bank[d][1], ACT.Copy).then_inc(s.u_copied, 1)

        @block.gpsimd
        def _(pool):
            for i, d, c in steps:
                n = 2 * i + d
                at_least(pool, s.s_made, n - 1)
                at_least(pool, s.rhs, n - 1)
                for h in H4:
                    nc.gpsimd.tensor_scalar(w[d]["kend"][:, h, :], k_tok[:, c, h * P:(h + 1) * P],
                                            tok["k_end"][:, c, 4 * d + h:4 * d + h + 1], None, ALU.mult)
                    nc.gpsimd.tensor_scalar(w[d]["bv"][:, h, :], v_tok[:, c, h * P:(h + 1) * P],
                                            tok["beta"][:, c, 4 * d + h:4 * d + h + 1], None, ALU.mult)
                pool.wait_ge(s.exp_r, n + 1)
                nc.gpsimd.tensor_tensor(w[d]["qdec"], p[:, 0:GDN_H, cols(c)], w[d]["exp_r"],
                                        ALU.mult).then_inc(s.pool, 1)

        @block.vector
        def _(dve):
            chain = Chain(dve, s.chain)

            def masked(i, lev):
                for d in range(2):
                    if lev == 2:
                        dve.wait_ge(s.deltas, (i * LEVELS) * 2 + d + 1)
                        dve.wait_ge(s.grown, (i * LEVELS) * 2 + d + 1)
                    else:
                        back = lev - 3 if lev > 2 else -1 - lev
                        at_least(dve, s.z_made, (i * (LEVELS - 1) + back) * 2 + d + 1)
                    mask = levels[:, d * LEVELS + lev, :].unsqueeze(1).broadcast_to([P, GDN_H, P])
                    nc.vector.tensor_tensor(am[d][lev % 2], w[d]["a"], mask, ALU.mult).then_inc(s.masked, 1)

            for i in range(NCHUNK):
                for d in range(2):
                    n, c, b, q = 2 * i + d, order[d][i], bank[d], w[d]
                    dve.wait_ge(s.mats, n + 1)
                    at_least(dve, s.out_made, n - 1)
                    for h in H4:
                        gc = tok["gc"][:, c, 4 * d + h:4 * d + h + 1]
                        nc.vector.tensor_scalar(q["a"][:, h, :], b[0][:, h, :], gc, 0.0, ALU.subtract, ALU.max)
                        ins = nc.vector.tensor_scalar(q["dec_t"][:, h, :], b[0][:, h, :], gc, 0.0,
                                                      ALU.subtract, ALU.min)
                    ins.then_inc(s.clamped, 1)
                for d in range(2):
                    n, c, b, q = 2 * i + d, order[d][i], bank[d], w[d]
                    dve.wait_ge(s.decays, n + 1)
                    for h in H4:
                        chain.add(nc.vector.scalar_tensor_tensor(
                            q["a"][:, h, :], b[1][:, h, :], tok["beta"][:, c, 4 * d + h:4 * d + h + 1],
                            q["a"][:, h, :], ALU.mult, ALU.mult))
                    chain.link(nc.vector.tensor_tensor(q["pt"], b[2], q["dec_t"], ALU.mult))
                    nc.vector.tensor_tensor(q["pt"], q["pt"],
                                            tri[:, d * P:(d + 1) * P].unsqueeze(1).broadcast_to([P, GDN_H, P]),
                                            ALU.mult).then_inc(s.qk_ready, 1)
                masked(i, 0)
                for lev in range(LEVELS):
                    if lev < LEVELS - 1:
                        masked(i, lev + 1)
                    for d in range(2):
                        m, q = (i * LEVELS + lev) * 2 + d, w[d]
                        dve.wait_ge(s.deltas, m + 1)
                        if lev == 0:
                            dve.wait_ge(s.masked, m + 1)
                            eye = k.ident.unsqueeze(1).broadcast_to([P, GDN_H, P])
                            nc.vector.tensor_tensor(q["x"], eye, am[d][0], ALU.subtract)
                            nc.vector.tensor_tensor(q["xt"], eye, bank[d][1], ALU.subtract).then_inc(s.grown, 1)
                            continue
                        dve.wait_ge(s.grown, (i * LEVELS + lev - 1) * 2 + d + 1)
                        if lev < LEVELS - 1:
                            delta = part(bank[d][2], lev, d)
                            nc.vector.tensor_tensor(part(q["x"], lev, d), part(q["x"], lev, d), delta, ALU.subtract)
                        xt = part(q["xt"], lev, 1 - d)
                        nc.vector.tensor_tensor(xt, xt, part(bank[d][1], lev, 1 - d), ALU.subtract).then_inc(s.grown, 1)
                for d in range(2):
                    n, c, q = 2 * i + d, order[d][i], w[d]
                    dve.wait_ge(s.ks, n + 1)
                    dve.wait_ge(s.pool, n + 1)
                    for h in H4:
                        ins = nc.vector.scalar_tensor_tensor(
                            q["r"][:, h, :], bank[d][0][:, h, :], tok["nbeg"][:, c, 4 * d + h:4 * d + h + 1],
                            q["bv"][:, h, :], ALU.mult, ALU.add)
                    ins.then_inc(s.rhs, 1)
                for d in range(2):
                    n, c = 2 * i + d, order[d][i]
                    dve.wait_ge(s.out_made, n + 1)
                    dve.wait_ge(s.out_added, n) if n else None
                    o = out[:, :, cols(c)]
                    nc.vector.tensor_tensor(o, o, bank[d][2], ALU.add).then_inc(s.out_added, 1)
                    dve.wait_ge(s.s_made, n + 1)
                    at_least(dve, s.s_done, n - 1)
                    for h in H4:
                        ins = nc.vector.scalar_tensor_tensor(
                            state[d][:, h, :], state[d][:, h, :], tok["s_end"][:, c, 4 * d + h:4 * d + h + 1],
                            bank[d][3][:, h, :], ALU.mult, ALU.add)
                    ins.then_inc(s.s_done, 1)


def odd_mixer(k, w_in, w_uq, w_ukv, w_out, then):
    nc = k.nc
    at = [0]

    def take(tiles, t):
        v = k.view(at[0], tiles, t)
        at[0] += tiles * t
        return v

    p, cq, ckv = take(6, T2), take(3, L), take(2, T2)
    q, kv, v_tok, y = take(12, L), take(16, T2), take(NCHUNK, 1024), take(8, L)
    linear(k, "mla_in", w_in, DT, T2, lambda kk: (k.hh[:, kk, :], k.hl[:, kk, :]),
           lambda u, bank: nc.scalar.activation(tile_of(p, u), bank[:, 0:T2], ACT.Copy), engine="scalar",
           then=lambda sp: w_uq.prime(sp))
    norm(k, "q_norm", lambda i: p[:, i, TOK:T2], lambda i: cq[:, i, :], 3, L, 384,
         gain=lambda i: [((0, L), k.v("mla_q_g", i, 1))], halves=halves_of_h(k, L))
    norm(k, "kv_norm", lambda i: p[:, 3 + i, :], lambda i: ckv[:, i, :], 2, T2, 256,
         gain=lambda i: [((0, T2), k.v("mla_kv_g", i, 1))], halves=lambda i: (k.hh[:, 3 + i, :], k.hl[:, 3 + i, :]))
    q2 = q.rearrange("p (u s) t -> p u (s t)", s=2)
    linear(k, "mla_q", w_uq, 3, L, lambda kk: (k.hh[:, kk, 0:L], k.hl[:, kk, 0:L]),
           lambda u, bank: nc.scalar.activation(tile_of(q2, u), bank[:, 0:T2], ACT.Copy), engine="scalar",
           then=lambda sp: w_ukv.prime(sp))
    linear(k, "mla_kv", w_ukv, 2, T2, lambda kk: (k.hh[:, 3 + kk, :], k.hl[:, 3 + kk, :]),
           lambda u, bank: nc.scalar.activation(tile_of(kv, u), bank[:, 0:T2], ACT.Copy), engine="scalar",
           then=lambda sp: w_out.prime(sp))

    rot, cos, sin = k.aux[:, 0:P], k.aux[:, 512:512 + L], k.aux[:, 768:768 + L]
    tmp = k.aux[:, 1024:1024 + 5 * L].rearrange("p (n t) -> p n t", t=L)
    roped = [q[:, 8 + j, :] for j in range(4)] + [p[:, 5, TOK:T2]]
    with stage(k, "rope", "tables", "turned", "chain") as (block, s):

        @block.sync
        def _(sp):
            for dst, name in ((rot, "rot"), (cos, "cos"), (sin, "sin")):
                sp.dma_start(dst, k.const(name)).then_inc(s.tables, 16)

        @block.tensor
        def _(pe):
            pe.wait_ge(s.tables, 48)
            for j, x in enumerate(roped):
                nc.tensor.matmul(k.bank[j][:, 0:L], rot, x, start=True, stop=True).then_inc(s.turned, 1)

        @block.vector
        def _(dve):
            chain = Chain(dve, s.chain)
            dve.wait_ge(s.tables, 48)
            for j, x in enumerate(roped):
                dve.wait_ge(s.turned, j + 1)
                chain.add(nc.vector.tensor_tensor(tmp[:, j, :], k.bank[j][:, 0:L], sin, ALU.mult))
                chain.link(nc.vector.tensor_tensor(x, x, cos, ALU.mult))
                nc.vector.tensor_tensor(x, x, tmp[:, j, :], ALU.add)

    transposes(k, "mla_v", [(kv[:, 8 + h, c * P:(c + 1) * P], v_tok[:, c, h * P:(h + 1) * P])
                            for c in range(NCHUNK) for h in range(HEADS)])
    units = []
    for h in range(HEADS):
        rows = slice(64 * (h % 2), 64 * (h % 2) + 64)
        for qt in range(2):
            cols = slice(qt * P, (qt + 1) * P)
            units.append(Unit(
                q=[q[:, h, cols], q[rows, 8 + h // 2, cols]], k=[kv[:, h, :], p[rows, 5, :]], keys=T2,
                v=[v_tok[:, c, h * P:(h + 1) * P] for c in range(NCHUNK)], bias=None, base=0, dv=P,
                out=y[:, h, cols]))
    attention(k, "mla", units, (128 + 64) ** -0.5, at[0])
    split(k, "mla_halves", y, DT, L)

    def add(u, bank):
        for j in range(2):
            x = tile_of(k.x, u * 2 + j, TOK, T2)
            ins = nc.vector.scalar_tensor_tensor(x, bank[:, j * L:(j + 1) * L], k.mod_at(1, 2, u * 2 + j, 1), x,
                                                 ALU.mult, ALU.add)
        return ins

    linear(k, "mla_out", w_out, DT, L, lambda kk: (k.hh[:, kk, 0:L], k.hl[:, kk, 0:L]), add, then=then)


def choices(k):
    now = [k.aux[:, L * j:L * (j + 1)] for j in range(3)]
    ids = k.ring[:, 2, D:D + L].bitcast(BF16)
    return now, [ids[:, 0:L], ids[:, L:T2], k.ring[:, 3, D:D + L]]


def choose(k, layer, halves, w_q):
    nc = k.nc
    lo, hi = halves
    t = hi - lo
    n_tok = t // P
    mod_norm(k, layer, True, halves, prime=w_q.prime)
    qy = k.view(0, 16, t)
    at = 16 * t
    keys = k.view(at, 16, KEYS)
    score = [k.view(at + 2048 * (i + 1), 16, KEYS) for i in range(n_tok)]
    q2 = k.big[:, 0:at].rearrange("p (u n) -> p u n", n=512)
    linear(k, "peer_q", w_q, DT, t, lambda kk: (k.hh[:, kk, 0:t], k.hl[:, kk, 0:t]),
           lambda u, bank: nc.scalar.activation(tile_of(q2, u), bank[:, 0:T2], ACT.Copy), engine="scalar")

    with stage(k, "peer_scores", "keys", "scored", "copied") as (block, s):

        @block.sync
        def _(sp):
            sp.dma_start(keys[:, :, :], k.io["sub_keys"][layer].rearrange("p (n m) -> p n m", n=16)).then_inc(s.keys, 16)

        @block.tensor
        def _(pe):
            pe.wait_ge(s.keys, 16)
            for tt in range(n_tok):
                for g in range(4):
                    at_least(pe, s.copied, 4 * tt + g - 7)
                    for j in range(4):
                        last = nc.tensor.matmul(k.bank[(4 * tt + g) % 8][:, j * P:(j + 1) * P],
                                                qy[:, 4 * g + j, tt * P:(tt + 1) * P], keys[:, 4 * g + j, :],
                                                start=True, stop=True)
                    last.then_inc(s.scored, 1)

        @block.scalar
        def _(act):
            for tt in range(n_tok):
                for g in range(4):
                    act.wait_ge(s.scored, 4 * tt + g + 1)
                    nc.scalar.activation(score[tt][:, 4 * g:4 * g + 4, :],
                                         k.bank[(4 * tt + g) % 8][:, :].rearrange("p (n m) -> p n m", n=4),
                                         ACT.Copy).then_inc(s.copied, 1)

    for half, results in zip(range(t // L), choices(k)):
        routing(k, score[2 * half:2 * half + 2], results, at + 2048 * (n_tok + 1))


def experts(k, layer, first, column, then):
    nc = k.nc
    half = first // L
    xs = lambda kk: (k.hh[:, kk, column:column + L], k.hl[:, kk, column:column + L])
    now, later = choices(k)
    i1_t, i2_t, gate_t = now
    if column:
        with stage(k, "recall") as (block, s):

            @block.vector
            def _(dve):
                for dst, src in zip(now, later):
                    nc.vector.tensor_copy(dst, src)

    table = k.big[:, :].rearrange("p (i t) -> p i t", t=L)
    row_hot = [k.aux[:, 768 + 1024 * b:1280 + 1024 * b].rearrange("p (q n) -> p q n", n=KEYS) for b in range(4)]
    col_hot = [k.aux[:, 1280 + 1024 * b:1792 + 1024 * b].rearrange("p (q n) -> p q n", n=KEYS) for b in range(4)]
    u_loaded = [nc.alloc_semaphore(f"u_loaded{b}_{k.stage_no}") for b in range(2)]
    v_loaded = [nc.alloc_semaphore(f"v_loaded{b}_{k.stage_no}") for b in range(2)]
    u_dram, v_dram = k.io["experts_u"], k.io["experts_v"]
    e0 = layer * KEYS

    def expert_row(dram, i):
        if isinstance(i, int):
            return dram[e0 + i]
        return dram[bass.ds(i + e0, 1)].rearrange("o p n -> (o p) n")

    def load_u(sp, i, b):
        sp.dma_start(k.ring[:, 2 * b, 0:D], expert_row(u_dram, i)).then_inc(u_loaded[b], 16)

    def load_v(sp, i, b):
        sp.dma_start(k.ring[:, 2 * b + 1, 0:D], expert_row(v_dram, i)).then_inc(v_loaded[b], 16)

    with stage(k, "table", "rows", "columns", "gates", "spread", "stored") as (block, s):

        @block.sync
        def _(sp):
            for b in range(2):
                load_u(sp, b, b)
                load_v(sp, b, b)

        @block.vector
        def _(dve):
            iota = k.iota.unsqueeze(1).broadcast_to([P, 4, KEYS])

            def group(r, b):
                g = r * 4 + b
                at_least(dve, s.spread, (r - 1) * 4 + (b + 1))
                tok = bass.ds(g * 4, 4)

                def spread(t):
                    return t[:, tok].unsqueeze(2).broadcast_to([P, 4, KEYS])

                nc.vector.tensor_tensor(col_hot[b], iota, spread(i2_t), ALU.is_equal).then_inc(s.columns, 1)
                nc.vector.tensor_tensor(row_hot[b], iota, spread(i1_t), ALU.is_equal).then_inc(s.rows, 1)

            repeat(dve, L // 16, lambda r: [group(r, b) for b in range(4)])

        @block.gpsimd
        def _(pool):
            def group(r, b):
                g = r * 4 + b
                pool.wait_ge(s.columns, g + 1)
                gate = gate_t[:, bass.ds(g * 4, 4)].unsqueeze(2).broadcast_to([P, 4, KEYS])
                nc.gpsimd.tensor_tensor(col_hot[b], col_hot[b], gate, ALU.mult).then_inc(s.gates, 1)

            repeat(pool, L // 16, lambda r: [group(r, b) for b in range(4)])

        @block.tensor
        def _(pe):
            def group(r, b):
                g = r * 4 + b
                pe.wait_ge(s.gates, g + 1)
                pe.wait_ge(s.rows, g + 1)
                at_least(pe, s.stored, (r - 1) * 4 + (b + 1))
                for j in range(4):
                    last = nc.tensor.matmul(k.bank[b][:, j * P:(j + 1) * P], col_hot[b][:, j, :],
                                            row_hot[b][:, j, :], start=True, stop=True)
                last.then_inc(s.spread, 1)

            repeat(pe, L // 16, lambda r: [group(r, b) for b in range(4)])

        @block.scalar
        def _(act):
            def group(r, b):
                g = r * 4 + b
                act.wait_ge(s.spread, g + 1)
                nc.scalar.activation(table[:, :, bass.ds(g * 4, 4)],
                                     k.bank[b][:, :].rearrange("p (q n) -> p n q", n=KEYS),
                                     ACT.Copy).then_inc(s.stored, 1)

            repeat(act, L // 16, lambda r: [group(r, b) for b in range(4)])

    hi, lo = k.parts(D, at=0, buf=k.aux)
    act_buf = [k.aux[:, 4096 + L * b:4096 + L * (b + 1)] for b in range(2)]
    product = [k.aux[:, 4608 + L * b:4608 + L * (b + 1)] for b in range(2)]
    ends = [k.ring[:, b, D:D + L].bitcast(BF16) for b in range(2)]
    gated = [(ends[b][:, 0:L], ends[b][:, L:2 * L]) for b in range(2)]
    with stage(k, "experts", "u_high", "v_high", "u_low", "v_low", "hidden", "activated", "product", "gated_high",
               "gated", "mixed") as (block, s):
        u_slot = [k.ring[:, 2 * b, 0:D] for b in range(2)]
        v_slot = [k.ring[:, 2 * b + 1, 0:D] for b in range(2)]

        @block.sync
        def _(sp):
            def refill(r):
                for b in range(2):
                    i = r * 2 + b
                    sp.wait_ge(s.u_low, i + 1)
                    load_u(sp, i + 2, b)
                    sp.wait_ge(s.v_low, i + 1)
                    load_v(sp, i + 2, b)

            repeat(sp, KEYS // 2 - 1, refill)
            if then is not None:
                then(sp)

        @block.tensor
        def _(pe):
            def hidden(r, b):
                pe.wait_ge(s.u_low, r * 2 + b + 1)
                at_least(pe, s.activated, (r - 1) * 2 + (b + 1))
                dst = k.bank[4 + b][:, 0:L]
                for kk in range(DT):
                    cols = slice(kk * P, (kk + 1) * P)
                    xh, xl = xs(kk)
                    nc.tensor.matmul(dst, hi[2 * b][:, cols], xh, start=kk == 0, stop=False)
                    nc.tensor.matmul(dst, hi[2 * b][:, cols], xl, start=False, stop=False)
                    last = nc.tensor.matmul(dst, lo[2 * b][:, cols], xh, start=False, stop=kk == DT - 1)
                last.then_inc(s.hidden, 1)

            def mix(r, b, first=False, last_group=False):
                pe.wait_ge(s.v_low, r * 2 + b + 1)
                pe.wait_ge(s.gated, r * 2 + b + 1)
                gh, gl = gated[b]
                for dt in range(DT):
                    cols = slice(dt * P, (dt + 1) * P)
                    dst = k.bank[dt // 2][:, (dt % 2) * L:(dt % 2 + 1) * L]
                    nc.tensor.matmul(dst, hi[2 * b + 1][:, cols], gh, start=first and dt % 2 == 0, stop=False,
                                     skip_group_check=True)
                    nc.tensor.matmul(dst, hi[2 * b + 1][:, cols], gl, start=False, stop=False, skip_group_check=True)
                    ins = nc.tensor.matmul(dst, lo[2 * b + 1][:, cols], gh, start=False, stop=last_group,
                                           skip_group_check=True)
                ins.then_inc(s.mixed, 1)

            hidden(0, 0)
            hidden(0, 1)
            mix(0, 0, first=True)
            hidden(1, 0)
            mix(0, 1)

            with pe.Fori(1, KEYS // 2 - 1) as r:
                hidden(r, 1)
                mix(r, 0)
                hidden(r + 1, 0)
                mix(r, 1)
            end = KEYS // 2 - 1
            hidden(end, 1)
            mix(end, 0)
            mix(end, 1, last_group=True)

        @block.scalar
        def _(act):
            def u_high(r, b):
                act.wait_ge(u_loaded[b], r * 16 + 16)
                at_least(act, s.hidden, (r - 1) * 2 + (b + 1))
                nc.scalar.activation(hi[2 * b], u_slot[b], ACT.Copy).then_inc(s.u_high, 1)

            def group(r, b, more=True):
                i = r * 2 + b
                if more:
                    u_high(r if b == 0 else r + 1, 1 - b)
                act.wait_ge(v_loaded[b], r * 16 + 16)
                at_least(act, s.mixed, (r - 1) * 2 + (b + 1))
                nc.scalar.activation(hi[2 * b + 1], v_slot[b], ACT.Copy).then_inc(s.v_high, 1)
                act.wait_ge(s.hidden, i + 1)
                at_least(act, s.product, (r - 1) * 2 + (b + 1))
                nc.scalar.activation(act_buf[b], k.bank[4 + b][:, 0:L], ACT.Gelu).then_inc(s.activated, 1)

            u_high(0, 0)
            repeat(act, KEYS // 2 - 1, lambda r: [group(r, b) for b in range(2)])
            group(KEYS // 2 - 1, 0)
            group(KEYS // 2 - 1, 1, more=False)

        @block.vector
        def _(dve):
            def u_low(r, b):
                dve.wait_ge(s.u_high, r * 2 + b + 1)
                nc.vector.tensor_tensor(lo[2 * b], u_slot[b], hi[2 * b], ALU.subtract).then_inc(s.u_low, 1)

            def group(r, b, more=True):
                i = r * 2 + b
                if more:
                    u_low(r if b == 0 else r + 1, 1 - b)
                dve.wait_ge(s.v_high, i + 1)
                nc.vector.tensor_tensor(lo[2 * b + 1], v_slot[b], hi[2 * b + 1], ALU.subtract).then_inc(s.v_low, 1)
                dve.wait_ge(s.activated, i + 1)
                nc.vector.tensor_tensor(product[b], act_buf[b], tile_of(table, i), ALU.mult).then_inc(s.product, 1)
                dve.wait_ge(s.product, i + 1)
                at_least(dve, s.mixed, (r - 1) * 2 + (b + 1))
                nc.vector.tensor_copy(gated[b][0], product[b]).then_inc(s.gated_high, 1)
                dve.wait_ge(s.gated_high, i + 1)
                nc.vector.tensor_tensor(gated[b][1], product[b], gated[b][0], ALU.subtract).then_inc(s.gated, 1)

            u_low(0, 0)
            repeat(dve, KEYS // 2 - 1, lambda r: [group(r, b) for b in range(2)])
            group(KEYS // 2 - 1, 0)
            group(KEYS // 2 - 1, 1, more=False)
            dve.wait_ge(s.mixed, KEYS)
            for dt in range(DT):
                x = k.x[:, dt, first:first + L]
                nc.vector.scalar_tensor_tensor(x, k.bank[dt // 2][:, (dt % 2) * L:(dt % 2 + 1) * L],
                                               k.mod_at(layer, 5, dt, half), x, ALU.mult, ALU.add)
    k.spent += u_loaded + v_loaded


def routing(k, score, results, scratch):
    nc = k.nc
    at = [scratch]

    def take(n, dt=F32):
        at[0] += n
        v = k.big[:, at[0] - n:at[0]]
        return v if dt == F32 else v.bitcast(dt)

    top, top_i = take(512), take(512, U32)
    top_f = take(512)
    best, best_i = take(256), take(256, U32)
    hi_i, lo_i = take(256, U32), take(256, U32)
    hi_f, lo_f = take(256), take(256)
    comb = take(16 * PAIRS)
    hot = take(2048)
    row, col, gate = take(256), take(256), take(256)
    small = take(64)
    late, pos = take(256), take(256)
    three = lambda v, n, m: v.rearrange("p (n m) -> p n m", m=m)
    with stage(k, "routing", "chain", "tops", "exps", "ready", "turned") as (block, s):

        @block.vector
        def _(dve):
            chain = Chain(dve, s.chain)

            def best16(values, out, out_i, jobs):
                for half in range(2):
                    sl = slice(8 * half, 8 * half + 8)
                    for j in jobs:
                        chain.add(nc.vector.max(out=out(j)[:, sl], in_=values(j)))
                    chain.settle()
                    for j in jobs:
                        chain.add(nc.vector.max_index(out=out_i(j)[:, sl], in_max=out(j)[:, sl], in_values=values(j)))
                    if half == 0:
                        chain.settle()
                        for j in jobs:
                            chain.add(nc.vector.match_replace(out=values(j), in_to_replace=out(j)[:, sl],
                                                              in_values=values(j), imm_value=-3e38))
                        chain.settle()

            jobs = [(tt, n) for tt in range(2) for n in range(16)]
            sub = lambda v: lambda j: v[:, 256 * j[0] + 16 * j[1]:256 * j[0] + 16 * j[1] + 16]
            best16(lambda j: score[j[0]][:, j[1], :], sub(top), sub(top_i), jobs)
            chain.settle()
            chain.link(nc.vector.tensor_copy(top_f, top_i))
            heads = [(tt, n) for tt in range(2) for n in range(HEADS)]
            pair = three(comb, 16, PAIRS)
            for tt, n in heads:
                a = top[:, 256 * tt + 32 * n:256 * tt + 32 * n + 16]
                b = top[:, 256 * tt + 32 * n + 16:256 * tt + 32 * n + 32]
                for i0, i1, at0, nj in ((0, 4, 0, 16), (4, 16, 64, 4)):
                    chain.add(nc.vector.tensor_tensor(
                        pair[:, 8 * tt + n, at0:at0 + (i1 - i0) * nj].rearrange("p (i j) -> p i j", j=nj),
                        a[:, i0:i1].unsqueeze(2).broadcast_to([P, i1 - i0, nj]),
                        b[:, 0:nj].unsqueeze(1).broadcast_to([P, i1 - i0, nj]), ALU.add))
            chain.settle()
            sub8 = lambda v: lambda j: v[:, 128 * j[0] + 16 * j[1]:128 * j[0] + 16 * j[1] + 16]
            best16(lambda j: pair[:, 8 * j[0] + j[1], :], sub8(best), sub8(best_i), heads)
            chain.settle()
            b3, g3 = three(best, 16, 16), three(gate, 16, 16)
            nc.vector.tensor_tensor(g3, b3, b3[:, :, 0:1].broadcast_to([P, 16, 16]), ALU.subtract).then_inc(s.tops, 1)
            chain.add(nc.vector.tensor_single_scalar(hi_i, best_i, 4, ALU.logical_shift_right))
            chain.add(nc.vector.tensor_single_scalar(lo_i, best_i, 2, ALU.logical_shift_right))
            chain.add(nc.vector.tensor_copy(pos, best_i))
            chain.settle()
            chain.add(nc.vector.tensor_copy(hi_f, hi_i))
            chain.add(nc.vector.tensor_copy(lo_f, lo_i))
            chain.add(nc.vector.tensor_single_scalar(late, pos, 64.0, ALU.is_ge))
            chain.settle()
            chain.add(nc.vector.scalar_tensor_tensor(lo_f, lo_f, -12.0, hi_f, ALU.add, ALU.subtract))
            chain.settle()
            chain.link(nc.vector.tensor_tensor(lo_f, lo_f, late, ALU.mult))
            chain.link(nc.vector.tensor_tensor(hi_f, hi_f, lo_f, ALU.add))
            chain.add(nc.vector.tensor_scalar(lo_f, hi_f, 12.0, -48.0, ALU.mult, ALU.add))
            chain.link(nc.vector.scalar_tensor_tensor(pos, hi_f, -16.0, pos, ALU.mult, ALU.add))
            chain.link(nc.vector.tensor_tensor(lo_f, lo_f, late, ALU.mult))
            chain.link(nc.vector.tensor_tensor(lo_f, lo_f, pos, ALU.add))
            iota16 = k.iota[:, 0:16].unsqueeze(1).broadcast_to([P, P, 16])
            h3 = three(hot, 128, 16)
            h4 = hot.rearrange("p (h r j) -> p h r j", r=16, j=16)
            for tt in range(2):
                for rank, first, dst in ((hi_f, 0, row), (lo_f, 16, col)):
                    chain.link(nc.vector.tensor_tensor(
                        h3, rank[:, 128 * tt:128 * tt + 128].unsqueeze(2).broadcast_to([P, P, 16]), iota16, ALU.is_equal))
                    ids = top_f[:, 256 * tt:256 * tt + 256].rearrange("p (h n) -> p h n", n=32)[:, :, first:first + 16]
                    chain.link(nc.vector.tensor_tensor(h4, h4, ids.unsqueeze(2).broadcast_to([P, HEADS, 16, 16]), ALU.mult))
                    chain.link(nc.vector.tensor_reduce(dst[:, 128 * tt:128 * tt + 128], h3, AX.X, ALU.add))
            dve.wait_ge(s.exps, 1)
            chain.link(nc.vector.tensor_reduce(small[:, 0:16], g3, AX.X, ALU.add))
            chain.link(nc.vector.reciprocal(small[:, 16:32], small[:, 0:16]))
            nc.vector.tensor_tensor(g3, g3, small[:, 16:32].unsqueeze(2).broadcast_to([P, 16, 16]),
                                    ALU.mult).then_inc(s.ready, 1)
            dve.wait_ge(s.turned, 1)
            for n, dst in enumerate(results):
                nc.vector.tensor_copy(dst, k.bank[n][:, 0:L])

        @block.scalar
        def _(act):
            act.wait_ge(s.tops, 1)
            nc.scalar.activation(gate, gate, ACT.Exp).then_inc(s.exps, 1)

        @block.tensor
        def _(pe):
            pe.wait_ge(s.ready, 1)
            for n, src in enumerate((row, col, gate)):
                for tt in range(2):
                    last = nc.tensor.transpose(k.bank[n][:, tt * P:(tt + 1) * P], src[:, tt * P:(tt + 1) * P], k.ident)
            last.then_inc(s.turned, 1)


def swiglu(k, layer, which, w_up, w_down, then):
    nc = k.nc
    both = k.big[:, 0:FF_T * L].bitcast(BF16).rearrange("p (n t) -> p n t", t=L)
    ah, al = both[:, 0:FF_T, :], both[:, FF_T:2 * FF_T, :]
    y = k.view(FF_T * L, DT, L)
    gate = [k.aux[:, 1024 + L * b:1024 + L * (b + 1)] for b in range(2)]
    prod = [k.aux[:, 1536 + L * b:1536 + L * (b + 1)] for b in range(2)]
    pre, post = f"ffn{which}_pre", f"ffn{which}_post"
    wide = k.view(SCRATCH, DT, L)
    norm(k, "ffn_norm", lambda i: k.x[:, i, TOK:T2], lambda i: wide[:, i, :], DT, L, D,
         gain=lambda i: [((0, L), k.v(pre, 8 * layer + i, 1))], halves=halves_of_h(k, L), prime=w_up.prime)
    body = 2
    rounds = FF_T // body
    w = w_up
    size = DT * P
    hi, lo = k.parts(SLOT)
    with stage(k, "ffn_up", "high", "low", "chunk_used", "silu", "product", "a_high", "a_low") as (block, s):

        @block.sync
        def _(sp):
            def refill(r):
                for slot in range(RING):
                    sp.wait_ge(s.low, r * RING + (slot + 1))
                    w.load(sp, r * RING + (slot + RING), slot)

            repeat(sp, w.chunks // RING - 1, refill)
            sp.wait_ge(s.low, w.chunks)
            w_down.prime(sp)

        @block.tensor
        def _(pe):
            def unit(r, b):
                at_least(pe, s.product, (r - 1) * body + (b + 1))
                for c in range(2):
                    slot = 2 * b + c
                    pe.wait_ge(s.low, r * RING + (slot + 1))
                    dst = k.bank[b][:, c * L:(c + 1) * L]
                    for kk in range(DT):
                        cols = slice(kk * P, (kk + 1) * P)
                        xh, xl = k.hh[:, kk, 0:L], k.hl[:, kk, 0:L]
                        nc.tensor.matmul(dst, hi[slot][:, cols], xh, start=kk == 0, stop=False)
                        nc.tensor.matmul(dst, hi[slot][:, cols], xl, start=False, stop=False)
                        last = nc.tensor.matmul(dst, lo[slot][:, cols], xh, start=False, stop=kk == DT - 1)
                    last.then_inc(s.chunk_used, 1)

            repeat(pe, rounds, lambda r: [unit(r, b) for b in range(body)])

        @block.scalar
        def _(act):
            def high(r, b):
                for slot in (2 * b, 2 * b + 1):
                    act.wait_ge(w.loaded[slot], r * 16 + 16)
                    at_least(act, s.chunk_used, (r - 1) * RING + (slot + 1))
                    nc.scalar.activation(hi[slot][:, 0:size], k.ring[:, slot, 0:size], ACT.Copy).then_inc(s.high, 1)

            def activate(r, b):
                act.wait_ge(s.chunk_used, r * RING + (2 * b + 2))
                at_least(act, s.product, (r - 1) * body + (b + 1))
                nc.scalar.activation(gate[b], k.bank[b][:, 0:L], ACT.Silu).then_inc(s.silu, 1)

            def pair(r, last=False):
                high(r, 1)
                activate(r, 0)
                if not last:
                    high(r + 1, 0)
                activate(r, 1)

            high(0, 0)
            repeat(act, rounds - 1, pair)
            pair(rounds - 1, last=True)

        @block.vector
        def _(dve):
            def low(r, b):
                for slot in (2 * b, 2 * b + 1):
                    dve.wait_ge(s.high, r * RING + (slot + 1))
                    nc.vector.tensor_tensor(lo[slot][:, 0:size], k.ring[:, slot, 0:size], hi[slot][:, 0:size],
                                            ALU.subtract).then_inc(s.low, 1)

            def multiply(r, b):
                u = r * body + b
                dve.wait_ge(s.silu, u + 1)
                nc.vector.tensor_tensor(prod[b], gate[b], k.bank[b][:, L:T2], ALU.mult).then_inc(s.product, 1)
                dve.wait_ge(s.product, u + 1)
                nc.vector.tensor_copy(tile_of(ah, u), prod[b]).then_inc(s.a_high, 1)
                dve.wait_ge(s.a_high, u + 1)
                nc.vector.tensor_tensor(tile_of(al, u), prod[b], tile_of(ah, u), ALU.subtract).then_inc(s.a_low, 1)

            def pair(r, last=False):
                low(r, 1)
                multiply(r, 0)
                if not last:
                    low(r + 1, 0)
                multiply(r, 1)

            low(0, 0)
            repeat(dve, rounds - 1, pair)
            pair(rounds - 1, last=True)

    w_up.retire()
    y2 = k.big[:, FF_T * L:(FF_T + DT) * L].rearrange("p (u n) -> p u n", n=T2)
    linear(k, "ffn_down", w_down, FF_T, L, lambda kk: (ah[:, kk, :], al[:, kk, :]),
            lambda u, bank: nc.scalar.activation(tile_of(y2, u), bank[:, 0:T2], ACT.Copy), engine="scalar", then=then)
    norm(k, "ffn_post", lambda i: y[:, i, :], lambda i: k.h[:, i, 0:L], DT, L, D,
         gain=lambda i: [((0, L), k.v(post, 8 * layer + i, 1))],
         residual=(lambda i: k.x[:, i, TOK:T2], 0.5))


def conv_pool_mixer(k, layer, w, then):
    nc = k.nc
    z = k.view(0, 48, L)
    z2 = k.big[:, 0:48 * L].rearrange("p (u n) -> p u n", n=T2)
    base = 48 * L
    ya, pool, m1, m2 = (k.view(base + 8 * L * i, DT, L) for i in range(4))
    spare = k.view(base + 32 * L, DT, L)
    counts = k.view(base + 40 * L, 4, L)
    wide = k.view(SCRATCH, DT, L)
    xs = lambda kk: (k.hh[:, kk, 0:L], k.hl[:, kk, 0:L])
    norm(k, "mix_norm", lambda i: k.x[:, i, TOK:T2], lambda i: wide[:, i, :], DT, L, D,
         gain=lambda i: [((0, L), k.v("mix_pre", 8 * layer + i, 1))], halves=halves_of_h(k, L), prime=w.w_in.prime)
    linear(k, "mix_in", w.w_in, DT, L, xs,
           lambda u, bank: nc.scalar.activation(tile_of(z2, u), bank[:, 0:T2], ACT.Copy), engine="scalar",
           then=lambda sp: w.w_pg.prime(sp))
    taps = k.v("conv_w_2", 24 * layer, 24).rearrange("p (t j) -> p t j", j=3)
    with stage(k, "conv_pool", "counts", "chain", "gates") as (block, s):

        @block.sync
        def _(sp):
            sp.dma_start(counts[:, :, :], k.const("inv_count").rearrange("p (n t) -> p n t", t=L)).then_inc(s.counts, 16)

        @block.scalar
        def _(act):
            for i in range(16):
                nc.scalar.activation(z[:, 32 + i, :], z[:, 32 + i, :], ACT.Sigmoid,
                                     bias=k.v("b_gate", 16 * layer + i, 1)).then_inc(s.gates, 1)

        @block.vector
        def _(dve):
            chain = Chain(dve, s.chain)
            u = m1
            chain.link(nc.vector.tensor_tensor(u[:, :, :], z[:, 8:16, :], z[:, 16:24, :], ALU.mult))
            for i in range(DT):
                chain.add(nc.vector.tensor_scalar(ya[:, i, :], u[:, i, :], taps[:, i, 2:3], None, ALU.mult))
            chain.settle()
            for j in (1, 0):
                o = 2 - j
                for i in range(DT):
                    chain.add(nc.vector.scalar_tensor_tensor(ya[:, i, o:L], u[:, i, 0:L - o], taps[:, i, j:j + 1],
                                                             ya[:, i, o:L], ALU.mult, ALU.add))
                chain.settle()
            chain.add(nc.vector.tensor_tensor(ya[:, :, :], ya[:, :, :], z[:, 0:8, :], ALU.mult))
            src = z[:, 24:32, :]
            dst = m2
            for g in range(4):
                lo = 2 * g
                o = 1 << g
                chain.add(nc.vector.tensor_tensor(dst[:, lo:8, o:L], src[:, lo:8, o:L], src[:, lo:8, 0:L - o], ALU.add))
                chain.link(nc.vector.tensor_copy(dst[:, lo:8, 0:o], src[:, lo:8, 0:o]))
                if g == 0:
                    dve.wait_ge(s.counts, 16)
                part = pool[:, lo:lo + 2, :]
                chain.link(nc.vector.tensor_tensor(part, dst[:, lo:lo + 2, :],
                                                   counts[:, g:g + 1, :].broadcast_to([P, 2, L]), ALU.mult))
                chain.link(nc.vector.tensor_tensor(part, part, z[:, 24 + lo:26 + lo, :], ALU.subtract))
                src, dst = dst, (spare if dst is m2 else m2)

    pooled = m1
    def pool_bias(u, bank):
        for j in range(2):
            n = 2 * u + j
            ins = nc.vector.tensor_scalar(pooled[:, n, :], bank[:, j * L:(j + 1) * L],
                                          k.v("b_pool", 8 * layer + n, 1), k.v("pool_scale", 8 * layer + n, 1),
                                          ALU.add, ALU.mult)
        return ins

    with stage(k, "pool_group", "made", "stored") as (block, s):

        @block.tensor
        def _(pe):
            for g in range(4):
                for j in range(2):
                    for kk in range(2):
                        if kk == 0 and j == 0:
                            pe.wait_ge(w.w_pg.loaded[g], 16)
                        last = nc.tensor.matmul(k.bank[g][:, j * L:(j + 1) * L],
                                                k.ring[:, g, (2 * j + kk) * P:(2 * j + kk + 1) * P],
                                                pool[:, 2 * g + kk, :], start=kk == 0, stop=kk == 1)
                last.then_inc(s.made, 1)

        @block.vector
        def _(dve):
            for g in range(4):
                dve.wait_ge(s.made, g + 1)
                pool_bias(g, k.bank[g])

        @block.sync
        def _(sp):
            sp.wait_ge(s.made, 4)
            w.w_conv_out.prime(sp)

    w.w_pg.retire()

    def branch(dst, gate):
        def run(u, bank):
            for j in range(2):
                ins = nc.vector.tensor_tensor(tile_of(dst, u * 2 + j), bank[:, j * L:(j + 1) * L],
                                              tile_of(z, u * 2 + j + gate), ALU.mult)
            return ins
        return run

    split(k, "ya_halves", ya, DT, L)
    linear(k, "conv_out", w.w_conv_out, DT, L, xs, branch(m2, 32), then=lambda sp: w.w_pool_out.prime(sp))
    split(k, "pool_halves", pooled, DT, L)
    linear(k, "pool_out", w.w_pool_out, DT, L, xs, branch(spare, 40), then=lambda sp: w.w_o.prime(sp))
    with stage(k, "mix_add") as (block, s):

        @block.vector
        def _(dve):
            nc.vector.tensor_tensor(m2[:, :, :], m2[:, :, :], spare[:, :, :], ALU.add)

    y2 = k.big[:, base:base + 8 * L].rearrange("p (u n) -> p u n", n=T2)
    split(k, "mix_halves", m2, DT, L)
    linear(k, "mix_o", w.w_o, DT, L, xs,
           lambda u, bank: nc.scalar.activation(tile_of(y2, u), bank[:, 0:T2], ACT.Copy), engine="scalar", then=then)
    norm(k, "mix_post", lambda i: ya[:, i, :], lambda i: k.h[:, i, 0:L], DT, L, D,
         gain=lambda i: [((0, L), k.v("mix_post", 8 * layer + i, 1))],
         residual=(lambda i: k.x[:, i, TOK:T2], 1.0))


def build_program(nc, io, out, stop=None):
    k = Core()
    k.nc, k.io, k.stage_no, k.spent = nc, io, 0, []
    k.big = nc.alloc_sbuf_tensor("big", [P, BIG], F32)
    k.x = nc.alloc_sbuf_tensor("x_all", [P, DT, T2], F32)
    k.h = nc.alloc_sbuf_tensor("h_all", [P, DT, T2], F32)
    k.ring = nc.alloc_sbuf_tensor("weight_ring", [P, RING, SLOT], F32)
    whole = k.h[:, :, :].rearrange("p n t -> p (n t)")
    half = DT * T2 // 2
    k.hh, k.hl = (whole[:, half * i:half * (i + 1)].bitcast(BF16).rearrange("p (n t) -> p n t", t=T2)
                  for i in range(2))
    k.mod = nc.alloc_sbuf_tensor("modulation", [P, 96, 2], F32)
    vec = nc.alloc_sbuf_tensor("vectors", [P, N_VEC], F32)
    res = nc.alloc_sbuf_tensor("resident_consts", [P, N_RESIDENT], F32)
    k.aux = nc.alloc_sbuf_tensor("aux", [P, AUX], F32)
    k.bank = [nc.alloc_psum_tensor(f"bank{i}", [P, 512], F32) for i in range(8)]

    def resident(name):
        a, n = CONST_AT[name]
        return res[:, a:a + n]

    k.ident, k.ones, k.iota, k.eps, k.pair = (resident(n) for n in ("ident", "ones", "iota", "eps", "pair"))
    k.v = lambda name, off=0, n=None: vec[:, VEC_AT[name] + off:VEC_AT[name] + off + (n or dict(VECTORS)[name])]
    k.const = lambda name: io["consts"][:, CONST_AT[name][0]:CONST_AT[name][0] + CONST_AT[name][1]]
    k.view = lambda at, tiles, t: k.big[:, at:at + tiles * t].rearrange("p (n t) -> p n t", t=t)

    def parts(size, at=PARTS, buf=None):
        buf = k.big if buf is None else buf
        both = [buf[:, at + size * i:at + size * (i + 1)].bitcast(BF16) for i in range(RING)]
        return [b[:, 0:size] for b in both], [b[:, size:2 * size] for b in both]

    k.parts = parts

    def mod_at(layer, part, tile, half):
        n = tile + (48 * layer + 8 * part)
        if isinstance(n, int):
            return k.mod[:, n, half:half + 1]
        return k.mod[:, bass.ds(n, 1), half:half + 1].rearrange("p o t -> p (o t)")

    k.mod_at = mod_at

    def weights(name, kc, chunks, first=0):
        w = Weights(k, name, kc, chunks)
        prime = w.prime
        w.prime = lambda sp: prime(sp, first)
        return w

    w_ada = weights("w_ada", 8, 96)
    w_even_in = weights("w_even_in", 8, 29)
    w_even_out = weights("w_even_out", 8, 8)
    load(k, "inputs", [(k.x[:, :, CTX:L], io["ctx"]), (k.x[:, :, TOK:T2], io["x"]), (vec[:, :], io["vectors"]),
                       (res[:, :], io["consts"][:, 0:N_RESIDENT])], more=w_ada.prime)
    condition(k, w_ada)

    def finish(src):
        with stage(k, "store", "stored") as (block, s):
            @block.sync
            def _(sp):
                sp.dma_start(out, src).then_inc(s.stored, 16)
                sp.wait_ge(s.stored, 16)

    mod_norm(k, 0, False, (0, T2), prime=w_even_in.prime, exact=True)
    if stop == "norm1":
        return finish(k.h[:, :, :])
    even_mixer(k, w_even_in, w_even_out, None)
    if stop == "even":
        return finish(k.x[:, :, :])
    choose(k, 0, (0, T2), weights("w_peer_q", 8, 16, 0))
    for first in (CTX, TOK):
        experts(k, 0, first, first, None)
    if stop == "peer0":
        return finish(k.x[:, :, :])
    mod_norm(k, 1, False, (0, T2))
    odd_mixer(k, weights("w_mla_in", 8, 6), weights("w_mla_uq", 3, 12), weights("w_mla_ukv", 2, 16),
              weights("w_mla_out", 8, 8), None)
    if stop == "mla":
        return finish(k.x[:, :, :])
    choose(k, 1, (TOK, T2), weights("w_peer_q", 8, 16, 16))
    experts(k, 1, TOK, 0, None)
    norm(k, "final", lambda i: k.x[:, i, TOK:T2], lambda i: k.x[:, i, TOK:T2], DT, L, D,
         gain=lambda i: [((0, L), k.v("final_g", i, 1))], squares=lambda i: k.h[:, i, 0:L])
    if stop == "first":
        return finish(k.x[:, :, :])
    for layer in range(2):
        swiglu(k, layer, 1, weights("w_up1", 8, 44, 44 * layer), weights("w_down1", 11, 16, 16 * layer), None)
        if stop == "ffn1" and layer == 0:
            return finish(k.x[:, :, :])
        conv_pool_mixer(k, layer, MixerWeights(
            w_in=weights("w_in2", 8, 48, 48 * layer), w_pg=weights("w_pg", 4, 4, 4 * layer),
            w_conv_out=weights("w_conv_out", 8, 8, 8 * layer), w_pool_out=weights("w_pool_out", 8, 8, 8 * layer),
            w_o=weights("w_o", 8, 8, 8 * layer)), None)
        if stop == "mix" and layer == 0:
            return finish(k.x[:, :, :])
        swiglu(k, layer, 2, weights("w_up2", 8, 44, 44 * layer), weights("w_down2", 11, 16, 16 * layer), None)
    finish(k.x[:, :, TOK:T2])


def tiled(w, kc):
    kdim, n = w.shape
    if n % P:
        w = np.concatenate([w, np.zeros((kdim, P - n % P), w.dtype)], 1)
    kt, nt = kdim // P, w.shape[1] // P
    return np.ascontiguousarray(w.reshape(kt // kc, kc, P, nt, P).transpose(3, 0, 2, 1, 4)).reshape(
        nt * (kt // kc), P, kc * P)


def columns(v):
    return np.ascontiguousarray(v.reshape(-1, P).T)


def lay_out(a):
    a = {n: np.asarray(v) for n, v in a.items()}
    io = {}
    feature_major = lambda t: np.ascontiguousarray(t.reshape(L, DT, P).transpose(2, 1, 0))
    io["x"], io["ctx"] = feature_major(a["x"][0]), feature_major(a["ctx"][0])
    per_partition = lambda v: np.broadcast_to(v.reshape(1, -1), (P, v.size))
    taps = lambda w: np.ascontiguousarray(w.reshape(w.shape[0], -1, P).transpose(2, 1, 0)).reshape(P, -1)
    vectors = {
        "c": columns(a["c"]), "c_ctx": columns(a["c_ctx"]), "ada_b": columns(a["ada_b"]),
        "norm1_g": columns(a["norm1_g"]), "norm2_g": columns(a["norm2_g"]), "final_g": columns(a["final_g"]),
        "conv_w": taps(a["even_conv_w"][0]), "gdn_norm_g": columns(a["gdn_norm_g"]),
        "a_log": per_partition(a["gdn_a_log"]), "dt_bias": per_partition(a["gdn_dt_bias"]),
        "mla_q_g": columns(a["mla_q_g"]), "mla_kv_g": columns(a["mla_kv_g"]),
        "ffn1_pre": columns(a["ffn1_pre_2"]), "ffn1_post": columns(a["ffn1_post_2"]),
        "mix_pre": columns(a["mix_pre_2"]), "mix_post": columns(a["mix_post_2"]),
        "ffn2_pre": columns(a["ffn2_pre_2"]), "ffn2_post": columns(a["ffn2_post_2"]),
        "b_gate": columns(a["b_gate_2"]),
        "conv_w_2": np.concatenate([taps(a["conv_w_2"][i]) for i in range(2)], 1),
        "b_pool": columns(a["b_pool_group_2"]), "pool_scale": columns(a["pool_scale_2"]),
    }
    io["vectors"] = np.ascontiguousarray(np.concatenate([vectors[n] for n, _ in VECTORS], 1))
    io["consts"] = CONSTS
    w = a["ada_w"].reshape(2, 4, 2, P, 12, 512)
    io["w_ada"] = np.ascontiguousarray(w.transpose(0, 4, 1, 3, 2, 5)).reshape(96, P, 1024)
    io["w_even_in"] = tiled(a["even_w_in"][0], 8)
    io["w_even_out"] = tiled(a["even_w_out"][0], 8)
    rpb = a["na_rpb"][0]
    wide = np.pad(rpb, ((0, 0), (0, 0), (GRID_W - 16, GRID_W - 16)))
    by_col = np.stack([wide[:, :, GRID_W - 1 - c:2 * GRID_W - 1 - c] for c in range(GRID_W)], 2)
    rows = L // GRID_W
    bias = np.stack([by_col[:, 7 - r:7 - r + rows] for r in range(rows)], 1)
    io["na_bias"] = np.ascontiguousarray(bias.transpose(0, 1, 3, 2, 4)).reshape(HEADS, 2, P, L)
    w = a["mla_w_in"][0]
    io["w_mla_in"] = tiled(np.concatenate([w, w[:, 640:704]], 1), 8)
    w = a["mla_w_uq"][0].reshape(384, HEADS, 192)
    io["w_mla_uq"] = tiled(np.concatenate([w[:, :, :128].reshape(384, -1), w[:, :, 128:].reshape(384, -1)], 1), 3)
    w = a["mla_w_ukv"][0].reshape(256, HEADS, 256)
    io["w_mla_ukv"] = tiled(np.concatenate([w[:, :, :128].reshape(256, -1), w[:, :, 128:].reshape(256, -1)], 1), 2)
    io["w_mla_out"] = tiled(a["mla_w_out"][0], 8)
    both = lambda name, kc: np.concatenate([tiled(a[name][i], kc) for i in range(2)])
    io["w_peer_q"] = both("peer_w_q", 8)
    io["sub_keys"] = np.ascontiguousarray(a["peer_sub_keys"].reshape(2, 16, KEYS, P).transpose(0, 3, 1, 2)).reshape(2, P, -1)
    io["experts_u"] = np.ascontiguousarray(
        a["peer_u"].reshape(2, KEYS, KEYS, DT, P).transpose(0, 1, 4, 3, 2)).reshape(2 * KEYS, P, D)
    io["experts_v"] = np.ascontiguousarray(a["peer_v"].reshape(2 * KEYS, KEYS, D))
    for which in (1, 2):
        w = a[f"ffn{which}_w_gate_up_2"].reshape(2, D, 2, FF_T, P).transpose(0, 1, 3, 2, 4).reshape(2, D, 2 * D_FF)
        io[f"w_up{which}"] = np.concatenate([tiled(w[i], 8) for i in range(2)])
        io[f"w_down{which}"] = both(f"ffn{which}_w_down_2", 11)
    io["w_in2"] = both("w_in_2", 8)
    w = a["w_pool_group_2"].reshape(2, 4, 2, P, 2, P)
    io["w_pg"] = np.ascontiguousarray(w.transpose(0, 1, 3, 4, 2, 5)).reshape(8, P, 4 * P)
    io["w_conv_out"], io["w_pool_out"], io["w_o"] = both("w_conv_out_2", 8), both("w_pool_out_2", 8), both("w_o_2", 8)
    return io


def kernel(**inputs):
    import concourse.bacc as bacc
    from concourse.bass_utils import run_bass_kernel_spmd

    io = lay_out(inputs)
    nc = bacc.Bacc("TRN2", target_bir_lowering=False, num_devices=1)
    arrays = {f"in_{n}": v for n, v in io.items()}
    aps = {n: nc.dram_tensor(f"in_{n}", v.shape, mybir.dt.from_np(v.dtype), kind="ExternalInput").ap()
           for n, v in io.items()}
    out = nc.dram_tensor("out_features", (P, DT, L), F32, kind="ExternalOutput").ap()
    build_program(nc, aps, out)
    r = run_bass_kernel_spmd(nc, [arrays], core_ids=[0])
    y = np.asarray(r.results[0]["out_features"])
    return np.ascontiguousarray(y.transpose(2, 1, 0)).reshape(1, L, D)
```
